# Optimizing a Trainium2 kernel written in Bass

```python
import math, functools
import jax, jax.numpy as jnp
from jax import lax
import numpy as np

D_MODEL = 1024
BATCH = 1
SEQ = 256
DEPTH = 2
DEC_BATCH = 8
DEC_SEQ = 8
PAST_LEN = 1024
PAGE_SIZE = 128

HEAD_DIM = 64
ATTN_W = D_MODEL // 2
N_Q_HEADS = ATTN_W // HEAD_DIM
N_KV_HEADS = N_Q_HEADS // 4
Q_GROUP = N_Q_HEADS // N_KV_HEADS
KV_W = N_KV_HEADS * HEAD_DIM
WINDOW = 128
BLOCK = 128
ROT_DIM = HEAD_DIM // 4
ROPE_THETA = 500000.0
SSM_W = D_MODEL - ATTN_W
SSM_GROUP_CH = 16
N_SSM_GROUPS = SSM_W // SSM_GROUP_CH
SSM_STATE = 64
DT_MIN = 1e-3
DT_MAX = 1e-1
MIX_W = ATTN_W + SSM_W
IN_W = ATTN_W + 2 * KV_W + ATTN_W + 2 * SSM_W
SPLIT_IDX = (ATTN_W, ATTN_W + KV_W, ATTN_W + 2 * KV_W, 2 * ATTN_W + 2 * KV_W,
             2 * ATTN_W + 2 * KV_W + SSM_W)
EPS = 1e-6
NEG_INF = -1e30

kernel_name = "hymba_swa_sink_s5_adaln_step"

def rms_norm(x, g):
    xf = x.astype(jnp.float32)
    y = xf * lax.rsqrt(jnp.mean(xf * xf, axis=-1, keepdims=True) + EPS)
    return (y * g.astype(jnp.float32)).astype(x.dtype)

def rope_partial(x, pos):
    half = ROT_DIM // 2
    inv = ROPE_THETA ** (-jnp.arange(half, dtype=jnp.float32) / half)
    ang = pos.astype(jnp.float32)[:, None] * inv[None, :]
    cos = jnp.cos(ang)[:, None, :].astype(x.dtype)
    sin = jnp.sin(ang)[:, None, :].astype(x.dtype)
    x1 = x[..., :half]
    x2 = x[..., half:ROT_DIM]
    return jnp.concatenate([x1 * cos - x2 * sin, x2 * cos + x1 * sin, x[..., ROT_DIM:]], axis=-1)

def sink_attention(q, k, v, mask, sinks):
    s = jnp.einsum('...qhgd,...khd->...hgqk', q, k).astype(jnp.float32) * (HEAD_DIM ** -0.5)
    s = jnp.where(mask, s, NEG_INF)
    sink = sinks.astype(jnp.float32).reshape(N_KV_HEADS, Q_GROUP)[:, :, None, None]
    m = jnp.maximum(jnp.max(s, axis=-1, keepdims=True), sink)
    p = jnp.exp(s - m)
    p = p / (jnp.sum(p, axis=-1, keepdims=True) + jnp.exp(sink - m))
    return jnp.einsum('...hgqk,...khd->...qhgd', p.astype(v.dtype), v)

def attend_prompt(q, k, v, sinks):
    Bn, L = q.shape[0], q.shape[1]
    nb = L // BLOCK
    qb = q.reshape(Bn, nb, BLOCK, N_KV_HEADS, Q_GROUP, HEAD_DIM)
    kb = k.reshape(Bn, nb, BLOCK, N_KV_HEADS, HEAD_DIM)
    vb = v.reshape(Bn, nb, BLOCK, N_KV_HEADS, HEAD_DIM)
    kk = jnp.concatenate([jnp.concatenate([jnp.zeros_like(kb[:, :1]), kb[:, :-1]], axis=1), kb], axis=2)
    vv = jnp.concatenate([jnp.concatenate([jnp.zeros_like(vb[:, :1]), vb[:, :-1]], axis=1), vb], axis=2)
    blk = jnp.arange(nb)[:, None]
    qpos = blk * BLOCK + jnp.arange(BLOCK)[None, :]
    kpos = (blk - 1) * BLOCK + jnp.arange(2 * BLOCK)[None, :]
    diff = qpos[:, :, None] - kpos[:, None, :]
    mask = (diff >= 0) & (diff <= WINDOW) & (kpos[:, None, :] >= 0)
    out = sink_attention(qb, kk, vv, mask[:, None, None], sinks)
    return out.reshape(Bn, L, ATTN_W)

def attend_sample(buf_k, buf_v, q, k, v, sinks):
    Bn, T = q.shape[0], q.shape[1]
    w = buf_k.shape[1]
    kk = jnp.concatenate([buf_k.astype(k.dtype), k], axis=1)
    vv = jnp.concatenate([buf_v.astype(v.dtype), v], axis=1)
    qpos = PAST_LEN + jnp.arange(T)
    kpos = PAST_LEN - w + jnp.arange(w + T)
    diff = qpos[:, None] - kpos[None, :]
    mask = (diff >= 0) & (diff <= WINDOW)
    qg = q.reshape(Bn, T, N_KV_HEADS, Q_GROUP, HEAD_DIM)
    out = sink_attention(qg, kk, vv, mask, sinks)
    return out.reshape(Bn, T, ATTN_W)

def complex_scan_combine(e1, e2):
    a1r, a1i, b1r, b1i = e1
    a2r, a2i, b2r, b2i = e2
    ar = a1r * a2r - a1i * a2i
    ai = a1r * a2i + a1i * a2r
    br = a2r * b1r - a2i * b1i + b2r
    bi = a2r * b1i + a2i * b1r + b2i
    return (ar, ai, br, bi)

def s5_branch(u, h0_re, h0_im, a_re, a_im, log_dt, b_re, b_im, c_re, c_im, d, w_glu, b_glu):
    f32 = jnp.float32
    Bn, L = u.shape[0], u.shape[1]
    uf = u.astype(f32).reshape(Bn, L, N_SSM_GROUPS, SSM_GROUP_CH)
    a_re = a_re.astype(f32)
    a_im = a_im.astype(f32)
    dt = jnp.exp(log_dt.astype(f32))[:, None]
    mag = jnp.exp(a_re * dt)
    abar_re = mag * jnp.cos(a_im * dt)
    abar_im = mag * jnp.sin(a_im * dt)
    den = a_re * a_re + a_im * a_im
    nr = abar_re - 1.0
    coef_re = (nr * a_re + abar_im * a_im) / den
    coef_im = (abar_im * a_re - nr * a_im) / den
    br = b_re.astype(f32)
    bi = b_im.astype(f32)
    bb_re = coef_re[..., None] * br - coef_im[..., None] * bi
    bb_im = coef_re[..., None] * bi + coef_im[..., None] * br
    bu_re = jnp.einsum('gpc,blgc->blgp', bb_re, uf)
    bu_im = jnp.einsum('gpc,blgc->blgp', bb_im, uf)
    a_seq_re = jnp.broadcast_to(abar_re, (1, L, N_SSM_GROUPS, SSM_STATE))
    a_seq_im = jnp.broadcast_to(abar_im, (1, L, N_SSM_GROUPS, SSM_STATE))
    acum_re, acum_im, hz_re, hz_im = lax.associative_scan(
        complex_scan_combine, (a_seq_re, a_seq_im, bu_re, bu_im), axis=1)
    s_re = h0_re.astype(f32)[:, None]
    s_im = h0_im.astype(f32)[:, None]
    h_re = hz_re + acum_re * s_re - acum_im * s_im
    h_im = hz_im + acum_re * s_im + acum_im * s_re
    y = (jnp.einsum('gcp,blgp->blgc', c_re.astype(f32), h_re)
         - jnp.einsum('gcp,blgp->blgc', c_im.astype(f32), h_im)
         + d.astype(f32) * uf)
    y = jax.nn.gelu(y.reshape(Bn, L, SSM_W))
    y = y * jax.nn.sigmoid(y @ w_glu.astype(f32) + b_glu.astype(f32))
    return y.astype(u.dtype), h_re[:, -1].astype(h0_re.dtype), h_im[:, -1].astype(h0_im.dtype)

def decoder_layer(x, c, pos, attend, h0_re, h0_im, norm_g, w_ada, b_ada, w_in, sinks,
                  a_re, a_im, log_dt, b_re, b_im, c_re, c_im, d, w_glu, b_glu, w_out):
    Bn, L = x.shape[0], x.shape[1]
    mod = jax.nn.silu(c) @ w_ada + b_ada
    shift, scale, gate = jnp.split(mod[:, None, :], 3, axis=-1)
    h = rms_norm(x, norm_g) * (1.0 + scale) + shift
    proj = h @ w_in
    q, k, v, za, u, zs = jnp.split(proj, SPLIT_IDX, axis=-1)
    q = rope_partial(q.reshape(Bn, L, N_Q_HEADS, HEAD_DIM), pos)
    k = rope_partial(k.reshape(Bn, L, N_KV_HEADS, HEAD_DIM), pos)
    v = v.reshape(Bn, L, N_KV_HEADS, HEAD_DIM)
    ya = attend(q, k, v, sinks)
    ys, hT_re, hT_im = s5_branch(u, h0_re, h0_im, a_re, a_im, log_dt, b_re, b_im,
                                 c_re, c_im, d, w_glu, b_glu)
    mix = jnp.concatenate([ya * jax.nn.silu(za), ys * jax.nn.silu(zs)], axis=-1)
    x = x + gate * (mix @ w_out)
    return x, k, v, hT_re, hT_im

def setup_inputs(seed: int = 0) -> dict:
    key = jax.random.key(seed)
    ks = jax.random.split(key, 26)
    f32 = jnp.float32
    win_buf = min(WINDOW, PAST_LEN)
    nrm = lambda k, s: jax.random.normal(k, s, f32)
    return {
        "x_prompt": nrm(ks[0], (BATCH, SEQ, D_MODEL)),
        "x_sample": nrm(ks[1], (DEC_BATCH, DEC_SEQ, D_MODEL)),
        "cache_k": nrm(ks[2], (DEPTH, DEC_BATCH, win_buf, N_KV_HEADS, HEAD_DIM)),
        "cache_v": nrm(ks[3], (DEPTH, DEC_BATCH, win_buf, N_KV_HEADS, HEAD_DIM)),
        "state_ssm_re": 0.3 * nrm(ks[4], (DEPTH, DEC_BATCH, N_SSM_GROUPS, SSM_STATE)),
        "state_ssm_im": 0.3 * nrm(ks[5], (DEPTH, DEC_BATCH, N_SSM_GROUPS, SSM_STATE)),
        "c_prompt": nrm(ks[6], (BATCH, D_MODEL)),
        "c_sample": nrm(ks[7], (DEC_BATCH, D_MODEL)),
        "norm_g": 1.0 + 0.05 * nrm(ks[8], (DEPTH, D_MODEL)),
        "w_ada": 0.3 * D_MODEL ** -0.5 * nrm(ks[9], (DEPTH, D_MODEL, 3 * D_MODEL)),
        "b_ada": 0.01 * nrm(ks[10], (DEPTH, 3 * D_MODEL)),
        "w_in": D_MODEL ** -0.5 * nrm(ks[11], (DEPTH, D_MODEL, IN_W)),
        "attn_sinks": 0.5 * nrm(ks[12], (DEPTH, N_Q_HEADS)),
        "ssm_a_re": -0.5 + 0.01 * nrm(ks[13], (DEPTH, N_SSM_GROUPS, SSM_STATE)),
        "ssm_a_im": math.pi * jnp.arange(SSM_STATE, dtype=f32)
                    + 0.01 * nrm(ks[14], (DEPTH, N_SSM_GROUPS, SSM_STATE)),
        "ssm_log_dt": jax.random.uniform(ks[15], (DEPTH, N_SSM_GROUPS), f32,
                                         math.log(DT_MIN), math.log(DT_MAX)),
        "ssm_b_re": (2 * SSM_GROUP_CH) ** -0.5 * nrm(ks[16], (DEPTH, N_SSM_GROUPS, SSM_STATE, SSM_GROUP_CH)),
        "ssm_b_im": (2 * SSM_GROUP_CH) ** -0.5 * nrm(ks[17], (DEPTH, N_SSM_GROUPS, SSM_STATE, SSM_GROUP_CH)),
        "ssm_c_re": SSM_STATE ** -0.5 * nrm(ks[18], (DEPTH, N_SSM_GROUPS, SSM_GROUP_CH, SSM_STATE)),
        "ssm_c_im": SSM_STATE ** -0.5 * nrm(ks[19], (DEPTH, N_SSM_GROUPS, SSM_GROUP_CH, SSM_STATE)),
        "ssm_d": nrm(ks[20], (DEPTH, N_SSM_GROUPS, SSM_GROUP_CH)),
        "w_glu": SSM_W ** -0.5 * nrm(ks[21], (DEPTH, SSM_W, SSM_W)),
        "b_glu": 0.01 * nrm(ks[22], (DEPTH, SSM_W)),
        "w_out": MIX_W ** -0.5 * nrm(ks[23], (DEPTH, MIX_W, D_MODEL)),
        "final_g": 1.0 + 0.05 * nrm(ks[24], (D_MODEL,)),
    }

def reference(x_prompt, x_sample, cache_k, cache_v, state_ssm_re, state_ssm_im, c_prompt, c_sample,
              norm_g, w_ada, b_ada, w_in, attn_sinks, ssm_a_re, ssm_a_im, ssm_log_dt,
              ssm_b_re, ssm_b_im, ssm_c_re, ssm_c_im, ssm_d, w_glu, b_glu, w_out, final_g):
    win_buf = cache_k.shape[2]
    pos_p = jnp.arange(x_prompt.shape[1])
    pos_s = PAST_LEN + jnp.arange(x_sample.shape[1])
    zeros_state = jnp.zeros((x_prompt.shape[0], N_SSM_GROUPS, SSM_STATE), x_prompt.dtype)
    xp, xs = x_prompt, x_sample
    kp_l, vp_l, srp_l, sip_l = [], [], [], []
    ks_l, vs_l, srs_l, sis_l = [], [], [], []
    for l in range(DEPTH):
        params = (norm_g[l], w_ada[l], b_ada[l], w_in[l], attn_sinks[l], ssm_a_re[l], ssm_a_im[l],
                  ssm_log_dt[l], ssm_b_re[l], ssm_b_im[l], ssm_c_re[l], ssm_c_im[l], ssm_d[l],
                  w_glu[l], b_glu[l], w_out[l])
        xp, kp, vp, hr, hi = decoder_layer(xp, c_prompt, pos_p, attend_prompt,
                                           zeros_state, zeros_state, *params)
        kp_l.append(kp[:, -win_buf:])
        vp_l.append(vp[:, -win_buf:])
        srp_l.append(hr)
        sip_l.append(hi)
        att_s = functools.partial(attend_sample, cache_k[l], cache_v[l])
        xs, kn, vn, hr_s, hi_s = decoder_layer(xs, c_sample, pos_s, att_s,
                                               state_ssm_re[l], state_ssm_im[l], *params)
        ks_l.append(jnp.concatenate([cache_k[l].astype(kn.dtype), kn], axis=1)[:, -win_buf:])
        vs_l.append(jnp.concatenate([cache_v[l].astype(vn.dtype), vn], axis=1)[:, -win_buf:])
        srs_l.append(hr_s)
        sis_l.append(hi_s)
    y_prompt = rms_norm(xp, final_g)
    y_sample = rms_norm(xs, final_g)
    new_k_prompt = jnp.stack(kp_l)
    new_v_prompt = jnp.stack(vp_l)
    new_ssm_re_prompt = jnp.stack(srp_l)
    new_ssm_im_prompt = jnp.stack(sip_l)
    new_k_sample = jnp.stack(ks_l)
    new_v_sample = jnp.stack(vs_l)
    new_ssm_re_sample = jnp.stack(srs_l)
    new_ssm_im_sample = jnp.stack(sis_l)
    return (y_prompt, y_sample, new_k_prompt, new_v_prompt, new_ssm_re_prompt, new_ssm_im_prompt,
            new_k_sample, new_v_sample, new_ssm_re_sample, new_ssm_im_sample)


_drawn_inputs = setup_inputs


def setup_inputs(seed=0):
    import zlib

    import numpy as np

    out = dict(_drawn_inputs(seed))
    spreads = {}
    factors = {'attn_sinks': 48.277,
     'ssm_a_re': 17.147,
     'ssm_c_re': 5.014,
     'ssm_c_im': 5.004,
     'w_glu': 4.577,
     'b_glu': 64.0,
     'b_ada': 3.142}
    for name, (base, spread) in spreads.items():
        noise = np.random.default_rng([zlib.crc32(name.encode()), seed]).standard_normal(out[name].shape)
        drawn = base * np.exp(spread * noise) if base else spread * noise
        out[name] = __import__('jax').numpy.asarray(drawn.astype(out[name].dtype))
    for name, factor in factors.items():
        out[name] = (out[name] * factor).astype(out[name].dtype)
    return out
```

```python
from contextlib import ExitStack

import numpy as np

import concourse.bass as bass
from concourse import mybir
from concourse.alu_op_type import AluOpType as ALU

F32 = mybir.dt.float32
F32R = mybir.dt.float32r
ACT = mybir.ActivationFunctionType
AX = mybir.AxisListType

P = 128
D = 1024
KT = D // P
DEPTH = 2
SEQ = 256
NB = 8
T = 8
NS = NB * T
TOK = SEQ + NS
J = TOK // T
JP = SEQ // T
HD = 64
NQ = 4
KV = 2
WIN = 128
IN_W = 2304
COL_K, COL_V, COL_ZA, COL_U, COL_ZS = 512, 640, 768, 1280, 1792
NI = 16
GC = 16
NST = 64
G = 2 * NI
MT = 4
PAST = 1024
EPS = 1e-6
NEG = -1e30
CT = 1 + NB
SCALE = HD ** -0.5
ROT = HD // 4
GELU_A = 0.044715
GELU_B = 1.5957691216057308
TWO_PI = 6.283185307179586
PI_1, PI_2 = 6.28125, 0.0019350051879882812
PI_3 = TWO_PI - PI_1 - PI_2
PI_SAFE = 3.1415925
EXP_SAFE = 80.0
ROUND = 12582912.0

C_ID, C_ROT, C_COS, C_SIN = 0, 128, 256, 576
C_MP, C_MS, C_SEL, C_END = 896, 1152, 1536, 1664

S_G, S_BADA, S_BGLU, S_D, S_SINKP, S_SINKS = 0, 8, 32, 36, 40, 48
S_A8R, S_A8I, S_A16R, S_A16I, S_END = 50, 66, 98, 114, 146
ROWS_L = 40

UNITS = ([f"ss{m}" for m in range(16)] + [f"u{m}" for m in range(4)] + [f"q{m}" for m in range(4)]
         + ["k", "v"] + [f"za{m}" for m in range(4)] + [f"zs{m}" for m in range(4)]
         + [f"gate{m}" for m in range(8)] + ["glu0", "glu1"] + [f"out{m}" for m in range(8)])
RAW = 4
SPLIT = [u for u in UNITS if not u.startswith(("ss", "gate"))]
HL = 2
DMAS = {u: 2 if u[0] == "q" or u[:2] == "za" else 3 if u.startswith("out") else 1 for u in UNITS}

PROJ_JOBS = ([f"u{m}" for m in range(4)] + [f"q{m}" for m in range(4)] + ["k"]
             + [f"za{m}" for m in range(4)] + [f"zs{m}" for m in range(4)]
             + [f"glu{m}" for m in range(4)] + [f"out{m}" for m in range(8)])
FIRST_PROJ_JOBS = ["BT0", "BT1"]
FIRST_JOBS = (["cT", "rowsT", "sinks"] + [f"CT{n}" for n in range(4)]
              + [f"xT{k}" for k in range(KT)])
WORK_JOBS = (["rms"]
             + ["WB0", "WB1", "rope0", "WB2", "WB3", "rope1", "WB4", "WB5", "rope2", "WB6", "WB7",
                "rope3", "v", "rope4", "h0", "kcT0", "kcT1"]
             + [f"S{n}" for n in range(8)] + [f"K{n}" for n in range(4)] + ["ktok"]
             + [f"y{n}" for n in range(4)] + ["state"]
             + ["sc00", "sc01", "sc10", "sc11", "sc12", "sc13", "ss0", "ss1"]
             + [f"PT{n}" for n in range(6)] + ["pv0", "pv1", "PTc", "PTn", "pvs"])
LAST_JOBS = ["rmsF"] + [f"yT{n}" for n in range(6)]


def constants():
    c = np.zeros((P, C_END), np.float32)
    c[:, C_ID:C_ID + P] = np.eye(P, dtype=np.float32)
    half = ROT // 2
    inv = (np.float32(500000.0) ** (-np.arange(half, dtype=np.float32) / np.float32(half))).astype(np.float32)
    pos = np.concatenate([np.arange(SEQ), np.tile(PAST + np.arange(T), NB)]).astype(np.float32)
    ang = pos[None, :] * inv[:, None]
    c[:, C_COS:C_COS + TOK] = 1.0
    for kv in range(KV):
        a = kv * HD
        for d in range(half):
            c[a + d, C_COS:C_COS + TOK] = c[a + d + half, C_COS:C_COS + TOK] = np.cos(ang[d])
            c[a + d, C_SIN:C_SIN + TOK] = -np.sin(ang[d])
            c[a + d + half, C_SIN:C_SIN + TOK] = np.sin(ang[d])
            c[a + d + half, C_ROT + a + d] = c[a + d, C_ROT + a + d + half] = 1.0
    r = np.arange(P)
    diff = P + r[:, None] - np.arange(2 * P)[None, :]
    c[:, C_MP:C_MP + 2 * P] = np.where((diff >= 0) & (diff <= WIN), 0.0, NEG)
    b4, t = r // 32, r % T
    for half_b in range(2):
        m = np.full((P, WIN + NS), NEG, np.float32)
        m[:, :WIN][np.arange(WIN)[None, :] >= t[:, None]] = 0.0
        col = np.arange(NS)
        m[:, WIN:][(col[None, :] // T == (half_b * 4 + b4)[:, None]) & (col[None, :] % T <= t[:, None])] = 0.0
        c[:, C_MS + half_b * (WIN + NS):C_MS + (half_b + 1) * (WIN + NS)] = m
    for i in range(NQ):
        c[i, C_SEL:C_SEL + P] = (r // T % NQ == i)
    return c


class Ring:

    def __init__(self, banks, filled, emptied, first, layer, last):
        self.banks, self.n = banks, len(banks)
        self._filled, self._emptied = filled, emptied
        self.first, self.layer, self.last = first, layer, last

    def _at(self, l, job):
        n = self.n
        of = [sum(1 for q in range(len(x)) if q % n == b) for x in (self.first, self.layer) for b in range(n)]
        if job in self.layer:
            q = self.layer.index(job)
            return q % n, of[q % n] + l * of[n + q % n] + q // n
        if job in self.first:
            q = self.first.index(job)
            return q % n, q // n
        q = self.last.index(job)
        return q % n, of[q % n] + DEPTH * of[n + q % n] + q // n

    def bank(self, job):
        for x in (self.first, self.layer, self.last):
            if job in x:
                return self.banks[x.index(job) % self.n]

    def room(self, l, job):
        b, k = self._at(l, job)
        return self._emptied[b], k

    def ready(self, l, job):
        b, k = self._at(l, job)
        return self._filled[b], k + 1

    def taken(self, l, job):
        b, k = self._at(l, job)
        return self._emptied[b], k + 1

    def filled(self, job):
        return self._filled[self._at(0, job)[0]]

    def emptied(self, job):
        return self._emptied[self._at(0, job)[0]]


class Steps:

    def __init__(self, eng, sem):
        self.eng, self.sem, self.n = eng, sem, 0

    def add(self, ins):
        self.n += 1
        ins.then_inc(self.sem, 1)

    def wait(self):
        self.eng.wait_ge(self.sem, self.n)

    def restart(self):
        if self.n:
            self.wait()
        self.eng.sem_clear(self.sem)
        self.n = 0


def slot_of(unit):
    return UNITS.index(unit) % RAW


def loads_at(l, unit):
    s = slot_of(unit)
    own = [u for u in UNITS if slot_of(u) == s]
    return l * (16 * sum(DMAS[u] for u in own)) + 16 * sum(DMAS[u] for u in own[:own.index(unit) + 1])


def uses_at(l, unit):
    return l * (len(UNITS) // RAW) + UNITS.index(unit) // RAW + 1


def build(nc, a, out):
    ctx = ExitStack()
    with ctx:
        def sb(name, shape, dt=F32):
            return ctx.enter_context(nc.sbuf_tensor(name, shape, dt))

        def sem(name):
            return ctx.enter_context(nc.semaphore(name))

        banks = [ctx.enter_context(nc.psum_tensor(f"bank{b}", [P, 512], F32)) for b in range(8)]

        const = sb("const", [P, C_SEL])
        ident = const[:, C_ID:C_ID + P]
        rot = const[:, C_ROT:C_ROT + P]
        cos, sin = const[:, C_COS:C_COS + TOK], const[:, C_SIN:C_SIN + TOK]
        mean = sb("mean", [P, P])
        raw = sb("raw", [P, RAW, D])
        w_hi = sb("w_hi", [P, HL, D], F32R)
        w_lo = sb("w_lo", [P, HL, D], F32R)
        xT = sb("xT", [P, KT, TOK])
        h_hi = sb("h_hi", [P, KT, TOK], F32R)
        h_lo = sb("h_lo", [P, KT, TOK], F32R)
        hn = sb("hn", [P, 2, TOK])
        hf = sb("hf", [P, 2, TOK])
        ez = sb("ez", [P, 2, TOK])
        sq = ez
        sqsum = sb("sqsum", [P, TOK])
        rstd = sb("rstd", [P, 2, TOK])
        u_sb = sb("u_sb", [P, MT, T, J])
        U = sb("U", [P, G, J])
        HY = sb("HY", [P, 2 * NI * J])
        Hst = HY[:, :].rearrange("p (r i j) -> p r i j", r=2, i=NI)
        Ysb = HY[:, 0:G * J].rearrange("p (g j) -> p g j", g=G)
        R1 = sb("R1", [P, 4096])
        Ssb = R1[:, 0:1280].rearrange("p (r i j) -> p r i j", r=2, i=NI)
        Hblk = R1[:, 1280:1280 + 2560].rearrange("p (r i h j) -> p r i h j", r=2, i=NI, h=2)
        P0 = R1[:, 0:1024].rearrange("p (v i k) -> p v i k", v=KV, i=NQ)
        P1 = R1[:, 1024:3072].rearrange("p (v i k) -> p v i k", v=KV, i=NQ)
        Ps = R1[:, 3072:3840].rearrange("p (v b k) -> p v b k", v=KV, b=2)
        R2 = sb("R2", [P, 4096])
        xin = R2[:, 0:3 * D].rearrange("p (n d) -> p n d", n=3)
        WBt = R2[:, :].rearrange("p (i r q) -> p i r q", i=NI, r=2)
        PT = R2[:, 0:3072].rearrange("p (n v q) -> p n v q", n=3, v=KV)
        PTc = R2[:, 3072:3584].rearrange("p (v b q) -> p v b q", v=KV, b=2)
        PTn = R2[:, 3584:4096].rearrange("p (v b q) -> p v b q", v=KV, b=2)
        R3 = sb("R3", [P, 2560])
        kc = R3[:, 0:1024].rearrange("p (b d) -> p b d", b=NB)
        h0 = R3[:, 1024:1024 + 2 * P].rearrange("p (r q) -> p r q", r=2)
        Ksb = R3[:, 0:2048].rearrange("p (i q) -> p i q", i=NI)
        ycp = R3[:, 0:1280].rearrange("p (m n) -> p m n", m=MT)
        yg = R3[:, 1280:2560].rearrange("p (m n) -> p m n", m=MT)
        WBq = sb("WBq", [P, 2, 4, P])
        Gm = sb("Gm", [P, 2, NI, T + 1, GC])
        Toep = sb("Toep", [P, G, P])
        Apow = sb("Apow", [P, DEPTH, 2, NI, T + 1])
        coef = sb("coef", [P, DEPTH, 2, NI])
        Bsb = sb("Bsb", [P, DEPTH, 2, NI, GC])
        Csb = sb("Csb", [P, DEPTH, 2, NI, GC])
        Bblk = sb("Bblk", [P, 2, NI, 2, GC])
        pt = sb("pt", [P, 2, 4 * GC * T])
        qT = sb("qT", [P, NQ, SEQ])
        qs = sb("qs", [P, NB, NQ, T])
        kT = sb("kT", [P, TOK])
        qraw, rt = hn, hf
        vtok = sb("vtok", [P, 3, P])
        ktok = sb("ktok", [P, 2, P])
        kcT = sb("kcT", [P, NB, WIN])
        vc = U[:, :, :].rearrange("p g j -> p (g j)")[:, 0:NB * P].rearrange("p (b q) -> p b q", b=NB)
        fin = sb("fin", [P, 2, 1 + NB, NI])
        stage = hn[:, :, :].rearrange("p a b -> p (a b)")[:, 0:4 * P].rearrange("p (n q) -> p n q", n=4)
        ga = sb("ga", [P, MT, TOK])
        gs = sb("gs", [P, MT, TOK])
        small = sb("small", [P, DEPTH, S_END])
        cur = sb("cur", [P, S_END])
        nbglu = sb("nbglu", [P, MT])
        fing = sb("fing", [P, KT])
        cT = sb("cT", [P, KT, CT])
        mod = sb("mod", [P, 3 * KT, CT])
        epsb = sb("epsb", [P, 1])
        sm = sb("sm", [P, 3, 5, 8])
        rec = sb("rec", [P, 2, 2, NI])
        wide = hn[:, :, :].rearrange("p a b -> p (a b)")[:, 0:JP * NI].rearrange("p (r i k) -> p r i k", r=2, i=NI)
        prod = hf[:, :, :].rearrange("p a b -> p (a b)")[:, 0:JP * NI].rearrange("p (r i k) -> p r i k", r=2, i=NI)
        Bbar = sb("Bbar", [P, 2, NI, GC])

        crow = R3[0:CT, 0:D]
        cexp = R3[0:CT, D:2 * D]
        rowsP = R1[0:2 * ROWS_L + KT, 0:P]
        rowsS = R1[0:3 * DEPTH * NI, P:2 * P]
        ldt = R1[0:DEPTH * NI, 2 * P:2 * P + 2]
        sel = R1[0:NQ, 330:330 + P]
        sinkc = R1[0:NQ, 320:324]
        Braw = R1[0:2 * DEPTH * NI, 512:512 + 2048]
        Craw = Gm[:, :, :, :, :].rearrange("p r i t c -> p (r i t c)")[:, 0:2048].rearrange(
            "p (n t d q) -> p n t d q", n=2 * DEPTH, t=4, d=2)
        rowsT = HY[:, 0:224]
        W = DEPTH * NI
        zz = HY[:, 256:256 + 20 * W].rearrange("p (n w) -> p n w", n=20)

        u_dram = nc.dram_tensor("u_turn", [G, GC, T, J], F32, kind="Internal").ap()
        y_dram = nc.dram_tensor("y_turn", [G, GC, T, J], F32, kind="Internal").ap()

        loaded = [sem(f"unit_loaded{s}") for s in range(RAW)]
        used = [sem(f"unit_used{s}") for s in range(RAW)]
        hi_done = sem("hi_done")
        const_in, cond_in, x_in, small_in, bc_in = (sem(n) for n in
                                                     ("const_in", "cond_in", "x_in", "small_in", "bc_in"))
        vcache_in = sem("vcache_in")
        cache_in, h0_in, skew_in = sem("cache_in"), sem("h0_in"), sem("skew_in")
        u_out, u_back, y_out, y_back = sem("u_out"), sem("u_back"), sem("y_out"), sem("y_back")
        kv_stored, state_stored, cache_copied, y_stored = (sem(n) for n in
                                                            ("kv_stored", "state_stored", "cache_copied", "y_stored"))
        ada_taken = sem("ada_taken")
        proj = Ring(banks[0:2], [sem(f"proj_filled{b}") for b in range(2)],
                    [sem(f"proj_emptied{b}") for b in range(2)], FIRST_PROJ_JOBS, PROJ_JOBS, [])
        work = Ring(banks[3:8], [sem(f"work_filled{b}") for b in range(5)],
                    [sem(f"work_emptied{b}") for b in range(5)], FIRST_JOBS, WORK_JOBS, LAST_JOBS)
        ada = banks[2][:, 0:3 * KT * CT].rearrange("p (m c) -> p m c", c=CT)
        dve_step, act_step, pool_step = sem("dve_step"), sem("act_step"), sem("pool_step")
        silu_c, silu_r = sem("silu_c"), sem("silu_r")
        sinks_in = sem("sinks_in")
        ldt_wide = sem("ldt_wide")
        ssm_exp = sem("ssm_exp")
        ssm_val = sem("ssm_val")
        ssm_ready = sem("ssm_ready")
        x_ready = sem("x_ready")
        sq_done, sq_added = sem("sq_done"), sem("sq_added")
        rstd_raw = sem("rstd_raw")
        norm_done = sem("norm_done")
        hp_done, hs_done = sem("hp_done"), sem("hs_done")
        hhi_done, h_ready = sem("hhi_done"), sem("h_ready")
        mod_ready = sem("mod_ready")
        mean_set = sem("mean_set")
        wb_ready, g_ready, zeros_set = sem("wb_ready"), sem("g_ready"), sem("zeros_set")
        H_ready, fin_ready = sem("H_ready"), sem("fin_ready")
        gate_exp = sem("gate_exp")
        max_ready, p_exp, p_ready = sem("max_ready"), sem("p_exp"), sem("p_ready")
        mixhi, mix_ready = sem("mixhi"), sem("mix_ready")
        y1_ready, y_sq, y_arg, y_exp = sem("y1_ready"), sem("y_sq"), sem("y_arg"), sem("y_exp")
        yg_ready, yghi, yglo = sem("yg_ready"), sem("yghi"), sem("yglo")
        gated, glu_exp = sem("gated"), sem("glu_exp")
        yn_ready = sem("yn_ready")

        block = ctx.enter_context(nc.Block())

        @block.sync
        def _(sp):
            def one_layer(l):
                return slice(l, l + 1) if isinstance(l, int) else bass.ds(l, 1)

            def load(l, unit):
                n, s = UNITS.index(unit), slot_of(unit)
                if not (isinstance(l, int) and l == 0) or n >= RAW:
                    sp.wait_ge(used[s], uses_at(l, unit) - 1)
                dst = raw[:, s, :].rearrange("p (k c) -> p k c", k=KT)
                own = one_layer(l)
                kind, m = unit.rstrip("0123456789"), int("0" + unit.lstrip("abcdefghijklmnopqrstuvwxyz"))
                if kind in ("ss", "gate"):
                    c0 = (m if kind == "ss" else 2 * KT + m) * P
                    src = a["w_ada"][own, :, c0:c0 + P].rearrange("o (k p) c -> p (o k) c", p=P)
                    sp.dma_start(dst, src).then_inc(loaded[s], 16)
                elif kind in ("q", "za"):
                    for kv in reversed(range(KV)):
                        c0 = (0 if kind == "q" else COL_ZA) + kv * NQ * HD + m * HD
                        src = a["w_in"][own, :, c0:c0 + HD].rearrange("o (k p) c -> p (o k) c", p=P)
                        sp.dma_start(dst[:, :, kv * HD:(kv + 1) * HD], src).then_inc(loaded[s], 16)
                elif kind in ("u", "k", "v", "zs"):
                    c0 = {"u": COL_U, "k": COL_K, "v": COL_V, "zs": COL_ZS}[kind] + m * P
                    src = a["w_in"][own, :, c0:c0 + P].rearrange("o (k p) c -> p (o k) c", p=P)
                    sp.dma_start(dst, src).then_inc(loaded[s], 16)
                elif kind == "glu":
                    src = a["w_glu"][own, :, m * 2 * P:(m + 1) * 2 * P].rearrange("o (k p) c -> p (o k) c", p=P)
                    sp.dma_start(raw[:, s, :].rearrange("p (k c) -> p k c", k=MT), src).then_inc(loaded[s], 16)
                else:
                    for kv in range(KV):
                        r0 = kv * NQ * HD
                        src = a["w_out"][own, r0:r0 + NQ * HD, m * P:(m + 1) * P].rearrange(
                            "o (k p) c -> p (o k) c", p=HD)
                        sp.dma_start(dst[kv * HD:(kv + 1) * HD, 0:MT, :], src).then_inc(loaded[s], 16)
                    src = a["w_out"][own, MT * P:, m * P:(m + 1) * P].rearrange("o (k p) c -> p (o k) c", p=P)
                    sp.dma_start(dst[:, MT:KT, :], src).then_inc(loaded[s], 16)

            def caches(l):
                own = one_layer(l)
                sp.dma_start(kc, a["cache_k"][own].rearrange("o b w v d -> w (o b) (v d)")).then_inc(cache_in, 16)
                for r, name in enumerate(("state_ssm_re", "state_ssm_im")):
                    src = a[name][own].rearrange("o b (i h) p -> (o b i) (h p)", h=2)
                    sp.dma_start(h0[:, r, :], src).then_inc(h0_in, 16)
                for name, dst in (("cache_k", out[6]), ("cache_v", out[7])):
                    sp.dma_start(dst[own, :, 0:WIN - T].rearrange("o b w v d -> (o b) (w v d)"),
                                 a[name][own, :, T:WIN].rearrange("o b w v d -> (o b) (w v d)")
                                 ).then_inc(cache_copied, 16)

            def skew(l):
                sp.wait_ge(zeros_set, 2)
                sp.wait_ge(*work.taken(l, "K3"))
                for s in range(T):
                    for h in range(2):
                        dst = Toep[s * GC:(s + 1) * GC, h::2, s * GC:P]
                        sp.dma_start(dst, Ksb[h * GC:(h + 1) * GC, :, 0:P - s * GC]).then_inc(skew_in, 16)

            def cached_values(l):
                sp.wait_ge(*work.ready(l, "y3"))
                sp.dma_start(vc, a["cache_v"][one_layer(l)].rearrange("o b w v d -> w (o b) (v d)"))\
                    .then_inc(vcache_in, 16)

            def first_units(l):
                for unit in UNITS[:RAW]:
                    load(l, unit)

            def rest_of_layer(l):
                for unit in UNITS[RAW:]:
                    load(l, unit)
                    if unit == "gate4":
                        cached_values(l)
                    if unit == "v":
                        caches(l)
                    if unit == "zs1":
                        skew(l)

            first_units(0)
            with sp.Fori(0, DEPTH - 1) as l:
                rest_of_layer(l)
                first_units(l + 1)
            rest_of_layer(DEPTH - 1)
            sp.wait_ge(cache_copied, DEPTH * 32)

        @block.tensor
        def _(pe):
            def mm(out_, lhsT, rhs, start, stop, free=False):
                return nc.tensor.matmul(out_, lhsT, rhs, start=start, stop=stop, skip_group_check=free)

            pe.wait_ge(const_in, 16)
            pe.wait_ge(silu_r, 1)
            b = work.bank("cT")
            for k in range(KT):
                ins = nc.tensor.transpose(b[:, k * CT:(k + 1) * CT], cexp[:, k * P:(k + 1) * P], ident[0:CT, 0:CT])
            ins.then_inc(work.filled("cT"), 1)
            b = work.bank("rowsT")
            pe.wait_ge(small_in, 16 * (7 * DEPTH + 1))
            pe.wait_ge(ldt_wide, 1)
            nc.tensor.transpose(b[:, 0:2 * ROWS_L + KT], rowsP, ident[0:2 * ROWS_L + KT, 0:2 * ROWS_L + KT])
            nc.tensor.transpose(b[:, P:P + 3 * W], rowsS, ident[0:3 * W, 0:3 * W]).then_inc(work.filled("rowsT"), 1)
            b = work.bank("sinks")
            pe.wait_ge(sinks_in, 48)
            mm(b[:, 0:DEPTH * KV], sel, sinkc, True, True).then_inc(work.filled("sinks"), 1)
            pe.wait_ge(bc_in, 16 * 12)
            for n in range(2):
                b = proj.bank(f"BT{n}")
                for c in range(8):
                    src = Braw[:, n * 8 + c:2048:GC]
                    ins = nc.tensor.transpose(b[:, c * 64:(c + 1) * 64], src, ident[0:64, 0:64])
                ins.then_inc(proj.filled(f"BT{n}"), 1)
            for n in range(4):
                pe.wait_ge(*work.room(0, f"CT{n}"))
                b = work.bank(f"CT{n}")
                for t in range(4):
                    ins = nc.tensor.transpose(b[:, t * P:(t + 1) * P],
                                              Craw[:, n, t].rearrange("p d q -> p (d q)"), ident)
                ins.then_inc(work.filled(f"CT{n}"), 1)
            pe.wait_ge(x_in, 32)
            for k in range(KT):
                pe.wait_ge(*work.room(0, f"xT{k}"))
                b = work.bank(f"xT{k}")
                for n, rows in enumerate((P, P, NS)):
                    ins = nc.tensor.transpose(b[:, n * P:n * P + rows], xin[0:rows, n, k * P:(k + 1) * P],
                                              ident[0:rows, 0:rows])
                ins.then_inc(work.filled(f"xT{k}"), 1)

            def sum_squares(l, job, layers):
                pe.wait_ge(*work.room(l, job))
                pe.wait_ge(sq_added, layers * KT)
                pe.wait_ge(mean_set, 2)
                mm(work.bank(job)[:, 0:TOK], mean[:, :], sqsum[:, :], True, True).then_inc(work.filled(job), 1)

            def ada_units(l, names, m0):
                for m, unit in enumerate(names):
                    s = slot_of(unit)
                    pe.wait_ge(loaded[s], loads_at(l, unit))
                    for k in range(KT):
                        ins = mm(ada[:, m0 + m, :], raw[:, s, k * P:(k + 1) * P], cT[:, k, :], k == 0, k == KT - 1)
                    ins.then_inc(used[s], 1)

            def split_passes(out_, unit, k, cols, rhs_k, first, last, moving=None):
                s = SPLIT.index(unit) % HL
                hi, lo = w_hi[:, s, cols], w_lo[:, s, cols]
                mm(out_, hi, h_hi[:, rhs_k, :], first, False)
                mm(out_, hi, h_lo[:, rhs_k, :], False, False)
                return mm(out_, lo, h_hi[:, rhs_k, :], False, last)

            def project(l, job):
                s = slot_of(job)
                pe.wait_ge(used[s], uses_at(l, job))
                pe.wait_ge(*proj.room(l, job))
                for k in range(KT):
                    ins = split_passes(proj.bank(job)[:, 0:TOK], job, k, slice(k * P, (k + 1) * P), k,
                                       k == 0, k == KT - 1)
                ins.then_inc(proj.filled(job), 1)

            def rope(l, n):
                job = f"rope{n}"
                pe.wait_ge(*work.room(l, job))
                pe.wait_ge(*proj.taken(l, f"q{n}" if n < 4 else "k"))
                mm(work.bank(job)[:, 0:TOK], rot, qraw[:, n % 2, :], True, True).then_inc(work.filled(job), 1)

            def turn_B(l, n):
                job, r, q = f"WB{n}", n % 2, n // 2
                pe.wait_ge(*work.room(l, job))
                pe.wait_ge(wb_ready, l * 8 + n + 1)
                b = work.bank(job)
                for i in range(4):
                    ins = nc.tensor.transpose(b[:, i * P:(i + 1) * P], WBq[:, n % 2, i, :], ident)
                ins.then_inc(work.filled(job), 1)

            def values(l):
                pe.wait_ge(used[slot_of("v")], uses_at(l, "v"))
                pe.wait_ge(*work.room(l, "v"))
                b, s = work.bank("v"), SPLIT.index("v") % HL
                for n, t0 in enumerate((0, P, TOK - P)):
                    for k in range(KT):
                        o, cols, toks = b[:, n * P:(n + 1) * P], slice(k * P, (k + 1) * P), slice(t0, t0 + P)
                        mm(o, h_hi[:, k, toks], w_hi[:, s, cols], k == 0, False)
                        mm(o, h_lo[:, k, toks], w_hi[:, s, cols], False, False)
                        ins = mm(o, h_hi[:, k, toks], w_lo[:, s, cols], False, k == KT - 1)
                ins.then_inc(work.filled("v"), 1)

            with pe.Fori(0, DEPTH) as l:
                sum_squares(l, "rms", l + 1)
                pe.wait_ge(*work.taken(0, "cT"))
                ada_units(l, [f"ss{m}" for m in range(16)], 0)

                pe.wait_ge(h_ready, (l + 1) * KT)
                for m in range(4):
                    project(l, f"u{m}")
                for m in range(4):
                    project(l, f"q{m}")
                    if m:
                        rope(l, m - 1)
                    turn_B(l, 2 * m)
                    turn_B(l, 2 * m + 1)
                project(l, "k")
                rope(l, 3)
                values(l)
                rope(l, 4)

                pe.wait_ge(h0_in, l * 32 + 32)
                pe.wait_ge(*work.room(l, "h0"))
                for r in range(2):
                    ins = nc.tensor.transpose(work.bank("h0")[:, r * P:(r + 1) * P], h0[:, r, :], ident)
                ins.then_inc(work.filled("h0"), 1)
                pe.wait_ge(cache_in, l * 16 + 16)
                for n in range(2):
                    pe.wait_ge(*work.room(l, f"kcT{n}"))
                    for q in range(4):
                        ins = nc.tensor.transpose(work.bank(f"kcT{n}")[:, q * P:(q + 1) * P], kc[:, n * 4 + q, :], ident)
                    ins.then_inc(work.filled(f"kcT{n}"), 1)

                pe.wait_ge(u_back, (l + 1) * 16 * T)
                for n in range(8):
                    job, r, q = f"S{n}", n % 2, n // 2
                    pe.wait_ge(*work.room(l, job))
                    pe.wait_ge(*work.taken(l, f"WB{n}"))
                    for i in range(4):
                        g = 2 * (4 * q + i)
                        ins = mm(work.bank(job)[:, i * 2 * J:(i + 1) * 2 * J], WBt[:, 4 * q + i, r, :],
                                 U[:, g:g + 2, :], True, True)
                    ins.then_inc(work.filled(job), 1)

                pe.wait_ge(g_ready, l + 1)
                for n in range(4):
                    job = f"K{n}"
                    pe.wait_ge(*work.room(l, job))
                    for q in range(4):
                        i = 4 * n + q
                        for r in range(2):
                            ins = mm(work.bank(job)[0:2 * GC, q * P:(q + 1) * P],
                                     Bblk[:, r, i].rearrange("p h c -> p (h c)"),
                                     Gm[:, r, i, 0:T].rearrange("p t c -> p (t c)"), r == 0, r == 1)
                    ins.then_inc(work.filled(job), 1)

                pe.wait_ge(*work.room(l, "ktok"))
                pe.wait_ge(*work.taken(l, "rope4"))
                b = work.bank("ktok")
                nc.tensor.transpose(b[:, 0:P], kT[:, P:2 * P], ident)
                nc.tensor.transpose(b[0:NS, P:2 * P], kT[:, SEQ:TOK], ident).then_inc(work.filled("ktok"), 1)

                for m in range(4):
                    project(l, f"za{m}")

                pe.wait_ge(H_ready, (l + 1) * 2)
                pe.wait_ge(skew_in, (l + 1) * 2 * T * 16)
                for n in range(4):
                    job = f"y{n}"
                    pe.wait_ge(*work.room(l, job))
                    for q in range(4):
                        i = 4 * n + q
                        o = work.bank(job)[:, q * 2 * J:(q + 1) * 2 * J]
                        for r in range(2):
                            mm(o, Gm[:, r, i, 1:T + 1].rearrange("p t c -> p (t c)"),
                               Hblk[:, r, i].rearrange("p h j -> p (h j)"), r == 0, False, True)
                        for h in range(2):
                            ins = mm(o[:, h * J:(h + 1) * J], Toep[:, 2 * i + h, :], U[:, 2 * i + h, :],
                                     False, h == 1, True)
                    ins.then_inc(work.filled(job), 1)
                pe.wait_ge(*work.room(l, "state"))
                pe.wait_ge(fin_ready, l + 1)
                b = work.bank("state")
                for r in range(2):
                    nc.tensor.transpose(b[:, r * P:(r + 1) * P],
                                        fin[:, r, 1:1 + NB, :].rearrange("p b i -> p (b i)"), ident)
                for r in range(2):
                    ins = nc.tensor.transpose(b[0:NI, (2 + r) * P:(3 + r) * P], fin[:, r, 0, :], ident)
                ins.then_inc(work.filled("state"), 1)

                for kv in range(KV):
                    rows = slice(kv * HD, (kv + 1) * HD)
                    job = f"sc0{kv}"
                    pe.wait_ge(*work.room(l, job))
                    for i in range(NQ):
                        ins = mm(work.bank(job)[:, i * P:(i + 1) * P], qT[rows, i, 0:P], kT[rows, 0:P], True, True)
                    ins.then_inc(work.filled(job), 1)
                for kv in range(KV):
                    rows = slice(kv * HD, (kv + 1) * HD)
                    for n in range(2):
                        job = f"sc1{2 * kv + n}"
                        pe.wait_ge(*work.room(l, job))
                        for q in range(2):
                            ins = mm(work.bank(job)[:, q * 2 * P:(q + 1) * 2 * P], qT[rows, 2 * n + q, P:SEQ],
                                     kT[rows, 0:SEQ], True, True)
                        ins.then_inc(work.filled(job), 1)
                for kv in range(KV):
                    rows = slice(kv * HD, (kv + 1) * HD)
                    job = f"ss{kv}"
                    pe.wait_ge(*work.room(l, job))
                    pe.wait_ge(*work.taken(l, "kcT0"))
                    pe.wait_ge(*work.taken(l, "kcT1"))
                    for hb in range(2):
                        o = work.bank(job)[:, hb * (WIN + NS):(hb + 1) * (WIN + NS)]
                        mm(o[:, WIN:], qs[rows, hb * 4:hb * 4 + 4].rearrange("p b i t -> p (b i t)"),
                           kT[rows, SEQ:TOK], True, True, True)
                        for q in range(4):
                            ins = mm(o[q * 32:(q + 1) * 32, 0:WIN],
                                     qs[rows, hb * 4 + q].rearrange("p i t -> p (i t)"),
                                     kcT[rows, hb * 4 + q, :], True, True, True)
                    ins.then_inc(work.filled(job), 1)

                for m in range(4):
                    project(l, f"zs{m}")

                pe.wait_ge(ada_taken, 2 * l + 1)
                ada_units(l, [f"gate{m}" for m in range(8)], 2 * KT)

                pe.wait_ge(p_ready, l * 3 + 1)
                for n in range(6):
                    if n == 2:
                        pe.wait_ge(p_ready, l * 3 + 2)
                    job, kv = f"PT{n}", n % 2
                    pe.wait_ge(*work.room(l, job))
                    for i in range(NQ):
                        src = P0[:, kv, i, :] if n < 2 else P1[:, kv, i, (n // 2 - 1) * P:(n // 2) * P]
                        ins = nc.tensor.transpose(work.bank(job)[:, i * P:(i + 1) * P], src, ident)
                    ins.then_inc(work.filled(job), 1)
                for job, parts in (("pv0", ((0, 0),)), ("pv1", ((1, 0), (2, 1)))):
                    pe.wait_ge(*work.room(l, job))
                    for n, _ in parts:
                        for kv in range(KV):
                            pe.wait_ge(*work.taken(l, f"PT{2 * n + kv}"))
                    pe.wait_ge(*work.taken(l, "v"))
                    for kv in range(KV):
                        for x, (n, tile) in enumerate(parts):
                            ins = mm(work.bank(job)[kv * HD:(kv + 1) * HD, :], vtok[:, tile, kv * HD:(kv + 1) * HD],
                                     PT[:, n, kv, :], x == 0, x == len(parts) - 1)
                    ins.then_inc(work.filled(job), 1)
                pe.wait_ge(p_ready, l * 3 + 3)
                pe.wait_ge(*work.room(l, "PTc"))
                pe.wait_ge(*work.room(l, "PTn"))
                for kv in range(KV):
                    for hb in range(2):
                        x = kv * 2 + hb
                        ins = nc.tensor.transpose(work.bank("PTc")[:, x * P:(x + 1) * P], Ps[:, kv, hb, 0:WIN], ident)
                ins.then_inc(work.filled("PTc"), 1)
                for kv in range(KV):
                    for hb in range(2):
                        x = kv * 2 + hb
                        ins = nc.tensor.transpose(work.bank("PTn")[0:NS, x * P:(x + 1) * P], Ps[:, kv, hb, WIN:], ident)
                ins.then_inc(work.filled("PTn"), 1)
                pe.wait_ge(*work.room(l, "pvs"))
                pe.wait_ge(*work.taken(l, "PTc"))
                pe.wait_ge(*work.taken(l, "PTn"))
                pe.wait_ge(vcache_in, l * 16 + 16)
                for kv in range(KV):
                    cols = slice(kv * HD, (kv + 1) * HD)
                    for hb in range(2):
                        o = work.bank("pvs")[cols, hb * P:(hb + 1) * P]
                        for q in range(4):
                            mm(o[:, q * 32:(q + 1) * 32], vc[:, hb * 4 + q, cols],
                               PTc[:, kv, hb, q * 32:(q + 1) * 32], hb == 0 and q == 0, False, True)
                        ins = mm(o, vtok[0:NS, 2, cols], PTn[0:NS, kv, hb, :], False, True, True)
                ins.then_inc(work.filled("pvs"), 1)

                pe.wait_ge(yglo, (l + 1) * MT)
                for m in range(4):
                    unit = f"glu{m // 2}"
                    pe.wait_ge(used[slot_of(unit)], uses_at(l, unit))
                    pe.wait_ge(*proj.room(l, f"glu{m}"))
                    for k in range(MT):
                        c0 = k * 2 * P + (m % 2) * P
                        ins = split_passes(proj.bank(f"glu{m}")[:, 0:TOK], unit, k, slice(c0, c0 + P), MT + k,
                                           k == 0, k == MT - 1)
                    ins.then_inc(proj.filled(f"glu{m}"), 1)

                pe.wait_ge(mix_ready, l * 7 + 3)
                for m in range(8):
                    unit = f"out{m}"
                    pe.wait_ge(used[slot_of(unit)], uses_at(l, unit))
                    pe.wait_ge(*proj.room(l, unit))
                    for k in range(KT):
                        if m == 0 and k >= MT:
                            pe.wait_ge(mix_ready, l * 7 + 4 + k - MT)
                        ins = split_passes(proj.bank(unit)[:, 0:TOK], unit, k, slice(k * P, (k + 1) * P), k,
                                           k == 0, k == KT - 1)
                    ins.then_inc(proj.filled(unit), 1)

            sum_squares(DEPTH, "rmsF", DEPTH + 1)
            pe.wait_ge(yn_ready, KT)
            for n in range(6):
                job, tile, half = f"yT{n}", n // 2, n % 2
                rows = P if tile < 2 else NS
                pe.wait_ge(*work.room(DEPTH, job))
                for q in range(4):
                    ins = nc.tensor.transpose(work.bank(job)[0:rows, q * P:(q + 1) * P],
                                              xT[:, half * 4 + q, tile * P:tile * P + rows], ident)
                ins.then_inc(work.filled(job), 1)

        @block.scalar
        def _(act):
            step = Steps(act, act_step)
            fn = nc.scalar.activation

            act.dma_start(crow[0:1, :], a["c_prompt"]).then_inc(cond_in, 16)
            act.dma_start(crow[1:CT, :], a["c_sample"]).then_inc(cond_in, 16)
            act.dma_start(const[:, :], a["constants"][:, 0:C_SEL]).then_inc(const_in, 16)
            xv = xin
            act.dma_start(xv[:, 0:2, :], a["x_prompt"][0].rearrange("(n p) d -> p n d", p=P)).then_inc(x_in, 16)
            act.dma_start(xv[0:NS, 2, :], a["x_sample"].rearrange("b t d -> (b t) d")).then_inc(x_in, 16)
            for l in range(DEPTH):
                r0 = l * ROWS_L
                for name, at, n in (("norm_g", S_G, KT), ("b_ada", S_BADA, 3 * KT), ("b_glu", S_BGLU, MT)):
                    act.dma_start(rowsP[r0 + at:r0 + at + n, :], a[name][l].rearrange("(r p) -> r p", p=P))\
                        .then_inc(small_in, 16)
                act.dma_start(rowsP[r0 + S_D:r0 + S_D + MT, :],
                              a["ssm_d"][l].rearrange("(r g) c -> r (g c)", r=MT)).then_inc(small_in, 16)
            act.dma_start(rowsP[2 * ROWS_L:2 * ROWS_L + KT, :], a["final_g"].rearrange("(r p) -> r p", p=P))\
                .then_inc(small_in, 16)
            for l in range(DEPTH):
                for n, name in enumerate(("ssm_a_re", "ssm_a_im")):
                    r0 = n * W + l * NI
                    act.dma_start(rowsS[r0:r0 + NI, :], a[name][l].rearrange("(i h) p -> i (h p)", h=2))\
                        .then_inc(small_in, 16)
                act.dma_start(ldt[l * NI:(l + 1) * NI, :], a["ssm_log_dt"][l].rearrange("(i h) -> i h", h=2))\
                    .then_inc(small_in, 16)
            act.dma_start(small[:, :, S_SINKP:S_SINKP + 8], a["attn_sinks"].unsqueeze(0).to_broadcast([P, DEPTH, 8]))\
                .then_inc(sinks_in, 16)
            act.dma_start(sel, a["constants"][0:NQ, C_SEL:C_END]).then_inc(sinks_in, 16)
            with nc.allow_non_contiguous_dma(reason="16 numbers"):
                act.dma_start(sinkc, a["attn_sinks"].rearrange("l (v i) -> i (l v)", i=NQ)).then_inc(sinks_in, 16)
            for l in range(DEPTH):
                for r, name in enumerate(("ssm_b_re", "ssm_b_im")):
                    r0 = (2 * l + r) * NI
                    act.dma_start(Braw[r0:r0 + NI, :], a[name][l].rearrange("(i h) p c -> i (h p c)", h=2))\
                        .then_inc(bc_in, 16)
                for r, name in enumerate(("ssm_c_re", "ssm_c_im")):
                    for d in range(2):
                        act.dma_start(Craw[:, 2 * l + r, :, d, :],
                                      a[name][l].rearrange("(t g) c p -> (g c) t p", t=4)).then_inc(bc_in, 16)

            act.wait_ge(cond_in, 32)
            fn(cexp, crow, ACT.Exp, scale=-1.0).then_inc(silu_c, 1)
            act.wait_ge(ssm_exp, 1)
            fn(zz[:, 3, :], rowsT[:, P + 2 * W:P + 3 * W], ACT.Exp).then_inc(ssm_val, 1)
            act.wait_ge(ssm_exp, 2)
            fn(zz[:, 6, :], zz[:, 4, :], ACT.Exp).then_inc(ssm_val, 1)
            act.wait_ge(ssm_exp, 3)
            fn(zz[:, 7, :], zz[:, 7, :], ACT.Sin).then_inc(ssm_val, 1)
            fn(zz[:, 8, :], zz[:, 8, :], ACT.Sin).then_inc(ssm_val, 1)
            for n in range(2):
                act.wait_ge(*proj.ready(0, f"BT{n}"))
                src = proj.bank(f"BT{n}")[:, :].rearrange("p (c w) -> p w c", c=8)
                dst = Bsb[:, :, :, :, n * 8:(n + 1) * 8].rearrange("p l r i c -> p (l r i) c")
                fn(dst, src, ACT.Copy).then_inc(proj.emptied(f"BT{n}"), 1)
            for n in range(4):
                l, r = n // 2, n % 2
                act.wait_ge(*work.ready(0, f"CT{n}"))
                for h in range(2):
                    rows = slice(h * NST, (h + 1) * NST)
                    src = work.bank(f"CT{n}")[rows, :].rearrange("p (i h c) -> p i h c", h=2, c=GC)[:, :, h, :]
                    ins = fn(Csb[rows, l, r], src, ACT.Copy, scale=(-1.0 if r else 1.0))
                    if h == 1:
                        ins.then_inc(work.emptied(f"CT{n}"), 1)
                    else:
                        step.add(ins)
            step.wait()

            for k in range(KT):
                act.wait_ge(*work.taken(0, f"xT{k}"))
                if k >= 2:
                    act.wait_ge(sq_added, k - 1)
                fn(sq[:, k % 2, :], xT[:, k, :], ACT.Square).then_inc(sq_done, 1)

            def hi_part(l, n):
                unit = SPLIT[n]
                act.wait_ge(loaded[slot_of(unit)], loads_at(l, unit))
                if n >= HL:
                    old = SPLIT[n - HL]
                    if old == "v":
                        act.wait_ge(*work.ready(l, "v"))
                    elif old.startswith("glu"):
                        act.wait_ge(*proj.ready(l, f"glu{2 * int(old[3:]) + 1}"))
                    else:
                        act.wait_ge(*proj.ready(l, old))
                fn(w_hi[:, n % HL, :], raw[:, slot_of(unit), :], ACT.Copy).then_inc(hi_done, 1)

            def root(l, job):
                act.wait_ge(*work.ready(l, job))
                fn(rstd[:, 1, :], work.bank(job)[:, 0:TOK], ACT.Identity, bias=epsb[:, 0:1])\
                    .then_inc(work.emptied(job), 1)
                act.wait_ge(*work.taken(l, job))
                step.add(fn(rstd[:, 0, :], rstd[:, 1, :], ACT.Ln))
                step.wait()
                fn(rstd[:, 0, :], rstd[:, 0, :], ACT.Exp, scale=-0.5).then_inc(rstd_raw, 1)

            act.wait_ge(mean_set, 2)
            with act.Fori(0, DEPTH) as l:
                step.restart()
                root(l, "rms")
                hi_part(l, 0)
                hi_part(l, 1)
                act.wait_ge(mod_ready, l + 1)
                for k in range(KT):
                    act.wait_ge(norm_done, l * KT + k + 1)
                    if k >= 2:
                        act.wait_ge(h_ready, l * KT + k - 1)
                    fn(hf[:, k % 2, 0:SEQ], hn[:, k % 2, 0:SEQ], ACT.Identity,
                       scale=mod[:, KT + k, 0:1], bias=mod[:, k, 0:1]).then_inc(hp_done, 1)
                    act.wait_ge(hs_done, l * KT + k + 1)
                    act.wait_ge(hp_done, l * KT + k + 1)
                    fn(h_hi[:, k, :], hf[:, k % 2, :], ACT.Copy).then_inc(hhi_done, 1)

                for m in range(4):
                    act.wait_ge(*proj.ready(l, f"u{m}"))
                    fn(u_sb[:, m], proj.bank(f"u{m}")[:, 0:TOK].rearrange("p (j t) -> p t j", t=T), ACT.Copy)\
                        .then_inc(proj.emptied(f"u{m}"), 1)
                    hi_part(l, m + 2)
                    act.wait_ge(*proj.taken(l, f"u{m}"))
                    act.dma_start(u_dram[m * 8:(m + 1) * 8].rearrange("g c t j -> (g c) (t j)"),
                                  u_sb[:, m].rearrange("p t j -> p (t j)")).then_inc(u_out, 16)

                def raw_rows(n, job):
                    act.wait_ge(*proj.ready(l, job))
                    if n >= 2:
                        act.wait_ge(*work.taken(l, f"rope{n - 2}"))
                    fn(qraw[:, n % 2, :], proj.bank(job)[:, 0:TOK], ACT.Copy).then_inc(proj.emptied(job), 1)

                def turned_B(n):
                    act.wait_ge(*work.ready(l, f"WB{n}"))
                    src = work.bank(f"WB{n}")[:, :].rearrange("p (i q) -> p i q", i=4)
                    fn(WBt[:, 4 * (n // 2):4 * (n // 2) + 4, n % 2, :], src, ACT.Copy)\
                        .then_inc(work.emptied(f"WB{n}"), 1)

                for m in range(4):
                    raw_rows(m, f"q{m}")
                    hi_part(l, 6 + m)
                    turned_B(2 * m)
                    turned_B(2 * m + 1)
                    if m == 0:
                        act.wait_ge(u_out, (l + 1) * 64)
                        for t in range(T):
                            act.dma_start(U[t * GC:(t + 1) * GC], u_dram[:, :, t, :].rearrange("g c j -> c g j"))\
                                .then_inc(u_back, 16)
                raw_rows(4, "k")
                hi_part(l, 10)

                act.wait_ge(*work.ready(l, "v"))
                step.add(fn(vtok[:, 0:2, :], work.bank("v")[:, 0:2 * P].rearrange("p (n q) -> p n q", n=2), ACT.Copy))
                fn(vtok[0:NS, 2, :], work.bank("v")[P - NS:P, 2 * P:3 * P], ACT.Copy).then_inc(work.emptied("v"), 1)
                hi_part(l, 11)
                for n in range(2):
                    act.wait_ge(*work.ready(l, f"kcT{n}"))
                    fn(kcT[:, 4 * n:4 * n + 4, :], work.bank(f"kcT{n}")[:, :].rearrange("p (b w) -> p b w", b=4),
                       ACT.Copy).then_inc(work.emptied(f"kcT{n}"), 1)
                for n in range(8):
                    job, r, q = f"S{n}", n % 2, n // 2
                    act.wait_ge(*work.ready(l, job))
                    for h in range(2):
                        rows = slice(h * NST, (h + 1) * NST)
                        src = work.bank(job)[rows, 0:8 * J].rearrange("p (i h j) -> p i h j", i=4, h=2)[:, :, h, :]
                        ins = fn(Ssb[rows, r, 4 * q:4 * q + 4, :], src, ACT.Copy)
                        if h == 1:
                            ins.then_inc(work.emptied(job), 1)
                        else:
                            step.add(ins)
                for n in range(4):
                    act.wait_ge(*work.ready(l, f"K{n}"))
                    fn(Ksb[0:2 * GC, 4 * n:4 * n + 4, :],
                       work.bank(f"K{n}")[0:2 * GC, :].rearrange("p (i q) -> p i q", i=4), ACT.Copy)\
                        .then_inc(work.emptied(f"K{n}"), 1)
                act.wait_ge(*work.ready(l, "ktok"))
                step.add(fn(ktok[:, 0, :], work.bank("ktok")[:, 0:P], ACT.Copy))
                fn(ktok[0:NS, 1, :], work.bank("ktok")[0:NS, P:2 * P], ACT.Copy).then_inc(work.emptied("ktok"), 1)
                step.wait()
                act.wait_ge(*work.taken(l, "ktok"))
                act.wait_ge(*work.taken(l, "v"))
                own = bass.ds(l, 1)
                for prompt, sample, src, new in ((out[2], out[6], ktok, 1), (out[3], out[7], vtok, 2)):
                    act.dma_start(prompt[own].rearrange("o b w v d -> (o b w) (v d)"), src[:, new - 1, :])\
                        .then_inc(kv_stored, 16)
                    act.dma_start(sample[own, :, WIN - T:WIN].rearrange("o b t v d -> (o b) t (v d)"),
                                  src[0:NS, new, :]).then_inc(kv_stored, 16)

                def gate(n, job):
                    act.wait_ge(*proj.ready(l, job))
                    if n >= 2:
                        before = f"za{n - 2}" if n - 2 < 4 else f"zs{n - 6}"
                        act.wait_ge(*proj.taken(l, before))
                    fn(ez[:, n % 2, :], proj.bank(job)[:, 0:TOK], ACT.Exp, scale=-1.0).then_inc(gate_exp, 1)

                for m in range(4):
                    gate(m, f"za{m}")
                    hi_part(l, 12 + m)
                for n in range(4):
                    act.wait_ge(*work.ready(l, f"y{n}"))
                    fn(Ysb[:, 8 * n:8 * n + 8, :], work.bank(f"y{n}")[:, 0:8 * J].rearrange("p (g j) -> p g j", g=8),
                       ACT.Copy).then_inc(work.emptied(f"y{n}"), 1)
                for n in range(4):
                    act.wait_ge(*work.taken(l, f"y{n}"))
                for t in range(T):
                    act.dma_start(y_dram[:, :, t, :].rearrange("g c j -> c g j"), Ysb[t * GC:(t + 1) * GC])\
                        .then_inc(y_out, 16)
                act.wait_ge(*work.ready(l, "state"))
                step.add(fn(stage[:, 0:2, :], work.bank("state")[:, 0:2 * P].rearrange("p (r q) -> p r q", r=2), ACT.Copy))
                fn(stage[0:NI, 2:4, :], work.bank("state")[0:NI, 2 * P:4 * P].rearrange("p (r q) -> p r q", r=2),
                   ACT.Copy).then_inc(work.emptied("state"), 1)
                gate(4, "zs0")
                hi_part(l, 16)
                step.wait()
                act.wait_ge(*work.taken(l, "state"))
                for r in range(2):
                    act.dma_start(out[8 + r][own].rearrange("o b (i h) p -> (o b i) (h p)", h=2), stage[:, r, :])\
                        .then_inc(state_stored, 16)
                    act.dma_start(out[4 + r][own].rearrange("o b (i h) p -> (o b i) (h p)", h=2), stage[0:NI, 2 + r, :])\
                        .then_inc(state_stored, 16)
                gate(5, "zs1")
                hi_part(l, 17)
                act.wait_ge(y_out, (l + 1) * 128)
                act.wait_ge(skew_in, (l + 1) * 2 * T * 16)
                for m in range(MT):
                    act.dma_start(ycp[:, m, :], y_dram[m * 8:(m + 1) * 8].rearrange("g c t j -> (g c) (t j)"))\
                        .then_inc(y_back, 16)
                gate(6, "zs2")
                hi_part(l, 18)
                gate(7, "zs3")
                hi_part(l, 19)

                for g, (buf, n) in enumerate(((P0, NQ), (P1, NQ), (Ps, 2))):
                    act.wait_ge(max_ready, l * 3 + g + 1)
                    for v in range(KV):
                        for i in range(n):
                            x = v * n + i
                            fn(buf[:, v, i, :], buf[:, v, i, :], ACT.Exp, scale=SCALE, bias=sm[:, g, 1, x:x + 1],
                               accum_out=sm[:, g, 2, x:x + 1])
                    fn(sm[:, g, 3, 0:KV * n], sm[:, g, 3, 0:KV * n], ACT.Exp).then_inc(p_exp, 1)

                for n in range(6):
                    act.wait_ge(*work.ready(l, f"PT{n}"))
                    fn(PT[:, n // 2, n % 2, :], work.bank(f"PT{n}")[:, :], ACT.Copy)\
                        .then_inc(work.emptied(f"PT{n}"), 1)
                act.wait_ge(*work.ready(l, "PTc"))
                fn(PTc, work.bank("PTc")[:, :].rearrange("p (v b q) -> p v b q", v=KV, b=2), ACT.Copy)\
                    .then_inc(work.emptied("PTc"), 1)
                act.wait_ge(*work.ready(l, "PTn"))
                fn(PTn[0:NS], work.bank("PTn")[0:NS, :].rearrange("p (v b q) -> p v b q", v=KV, b=2), ACT.Copy)\
                    .then_inc(work.emptied("PTn"), 1)

                for m in range(MT):
                    act.wait_ge(y1_ready, l * MT + m + 1)
                    if m >= 2:
                        act.wait_ge(yg_ready, l * MT + m - 1)
                    fn(ez[:, m % 2, :], ycp[:, m, :], ACT.Square).then_inc(y_sq, 1)
                    act.wait_ge(y_arg, l * MT + m + 1)
                    fn(ez[:, m % 2, :], ez[:, m % 2, :], ACT.Exp, scale=-GELU_B).then_inc(y_exp, 1)
                    act.wait_ge(yg_ready, l * MT + m + 1)
                    fn(h_hi[:, MT + m, :], yg[:, m, :], ACT.Copy).then_inc(yghi, 1)

                for job, toks in (("pv0", slice(0, P)), ("pv1", slice(P, SEQ)), ("pvs", slice(SEQ, TOK))):
                    act.wait_ge(*work.taken(l, job))
                    fn(h_hi[:, 0:MT, toks], ga[:, :, toks], ACT.Copy).then_inc(mixhi, 1)

                for m in range(MT):
                    act.wait_ge(*proj.taken(l, f"glu{m}"))
                    fn(ez[:, m % 2, :], ez[:, m % 2, :], ACT.Exp, scale=-1.0).then_inc(glu_exp, 1)
                    if m == 1:
                        hi_part(l, 20)
                    if m == 3:
                        hi_part(l, 21)
                for m in range(MT):
                    act.wait_ge(gated, l * MT + m + 1)
                    fn(h_hi[:, MT + m, :], gs[:, m, :], ACT.Copy).then_inc(mixhi, 1)
                for m in range(8):
                    act.wait_ge(x_ready, l * KT + m + 1)
                    if m >= 2:
                        act.wait_ge(sq_added, (l + 1) * KT + m - 1)
                    fn(sq[:, m % 2, :], xT[:, m, :], ACT.Square).then_inc(sq_done, 1)
                    if m < 6:
                        hi_part(l, 22 + m)
                act.wait_ge(kv_stored, (l + 1) * 64)
                act.wait_ge(state_stored, (l + 1) * 64)

            step.restart()
            root(DEPTH, "rmsF")
            ybuf = xin
            for n in range(6):
                job, tile, half = f"yT{n}", n // 2, n % 2
                rows = P if tile < 2 else NS
                act.wait_ge(*work.ready(DEPTH, job))
                fn(ybuf[0:rows, tile, half * 512:(half + 1) * 512], work.bank(job)[0:rows, :], ACT.Copy)\
                    .then_inc(work.emptied(job), 1)
            for n in range(6):
                act.wait_ge(*work.taken(DEPTH, f"yT{n}"))
            act.dma_start(out[0][0].rearrange("(n p) d -> p n d", p=P), ybuf[:, 0:2, :]).then_inc(y_stored, 16)
            act.dma_start(out[1].rearrange("b t d -> (b t) d"), ybuf[0:NS, 2, :]).then_inc(y_stored, 16)
            act.wait_ge(y_stored, 32)

        @block.vector
        def _(dve):
            step = Steps(dve, dve_step)
            v = nc.vector
            tt, ts, stt, cp = v.tensor_tensor, v.tensor_scalar, v.scalar_tensor_tensor, v.tensor_copy

            def own(ins):
                step.add(ins)
                step.wait()

            v.memset(mean[:, :], 1.0 / D).then_inc(mean_set, 1)
            v.memset(epsb[:, :], EPS).then_inc(mean_set, 1)
            step.add(v.memset(Apow[:, :, 0, :, 0:1], 1.0))
            step.add(v.memset(Apow[:, :, 1, :, 0:1], 0.0))
            dve.wait_ge(silu_c, 1)
            own(ts(cexp, cexp, 1.0, None, ALU.add))
            own(v.reciprocal(cexp, cexp))
            tt(cexp, crow, cexp, ALU.mult).then_inc(silu_r, 1)
            dve.wait_ge(small_in, 16 * (7 * DEPTH + 1))
            cp(rowsS[2 * W:3 * W, :].rearrange("p (h q) -> p h q", h=2),
               ldt.unsqueeze(2).to_broadcast([W, 2, NST])).then_inc(ldt_wide, 1)
            dve.wait_ge(*work.ready(0, "cT"))
            cp(cT[:, :, :], work.bank("cT")[:, 0:KT * CT].rearrange("p (k c) -> p k c", c=CT))\
                .then_inc(work.emptied("cT"), 1)
            dve.wait_ge(*work.ready(0, "rowsT"))
            step.add(cp(rowsT[:, 0:2 * ROWS_L + KT], work.bank("rowsT")[:, 0:2 * ROWS_L + KT]))
            cp(rowsT[:, P:P + 3 * W], work.bank("rowsT")[:, P:P + 3 * W]).then_inc(work.emptied("rowsT"), 1)
            step.wait()
            dve.wait_ge(*work.taken(0, "rowsT"))
            step.add(cp(small[:, :, 0:ROWS_L], rowsT[:, 0:2 * ROWS_L].rearrange("p (l r) -> p l r", l=DEPTH)))
            step.add(cp(fing[:, :], rowsT[:, 2 * ROWS_L:2 * ROWS_L + KT]))
            dve.wait_ge(*work.ready(0, "sinks"))
            cp(small[:, :, S_SINKS:S_SINKS + KV],
               work.bank("sinks")[:, 0:DEPTH * KV].rearrange("p (l s) -> p l s", l=DEPTH))\
                .then_inc(work.emptied("sinks"), 1)

            a_re, a_im = rowsT[:, P:P + W], rowsT[:, P + W:P + 2 * W]
            dt_, ard, th, mag, rs, rc = (zz[:, n, :] for n in (3, 4, 5, 6, 7, 8))
            k1, k2, t1, t2, den, nr = (zz[:, n, :] for n in (9, 10, 11, 12, 13, 14))
            dve.wait_ge(*work.taken(0, "rowsT"))
            step.wait()
            cp(zz[:, 0, :], a_re).then_inc(ssm_exp, 1)
            dve.wait_ge(ssm_val, 1)
            own(tt(th, a_im, dt_, ALU.mult))
            tt(ard, a_re, dt_, ALU.mult).then_inc(ssm_exp, 1)
            own(ts(k1, th, 1.0 / TWO_PI, ROUND, ALU.mult, ALU.add))
            own(ts(k1, k1, -ROUND, None, ALU.add))
            own(ts(k2, th, 1.0 / TWO_PI, 0.25, ALU.mult, ALU.add))
            own(ts(k2, k2, ROUND, None, ALU.add))
            own(ts(k2, k2, -ROUND, None, ALU.add))
            for r, k in ((rs, k1), (rc, k2)):
                own(stt(r, k, -PI_1, th, ALU.mult, ALU.add))
                own(stt(r, k, -PI_2, r, ALU.mult, ALU.add))
                own(stt(r, k, -PI_3, r, ALU.mult, ALU.add))
            own(ts(rs, rs, PI_SAFE, -PI_SAFE, ALU.min, ALU.max))
            own(ts(rc, rc, TWO_PI / 4, PI_SAFE, ALU.add, ALU.min))
            ts(rc, rc, -PI_SAFE, None, ALU.max).then_inc(ssm_exp, 1)
            own(tt(t1, a_re, a_re, ALU.mult))
            own(tt(t2, a_im, a_im, ALU.mult))
            own(tt(den, t1, t2, ALU.add))
            own(v.reciprocal(den, den))
            dve.wait_ge(ssm_val, 4)

            def power(r, n0, n1):
                return Apow[:, :, r, :, n0:n1]

            def flat(x):
                return x.rearrange("p (l i) -> p l i", l=DEPTH).unsqueeze(3)

            ar, ai = power(0, 1, 2), power(1, 1, 2)
            own(tt(ar, flat(mag), flat(rc), ALU.mult))
            own(tt(ai, flat(mag), flat(rs), ALU.mult))
            own(ts(flat(nr), ar, -1.0, None, ALU.add))
            own(tt(t1, nr, a_re, ALU.mult))
            own(tt(flat(t2), ai, flat(a_im), ALU.mult))
            own(tt(t1, t1, t2, ALU.add))
            own(tt(coef[:, :, 0, :].unsqueeze(3), flat(t1), flat(den), ALU.mult))
            own(tt(flat(t1), ai, flat(a_re), ALU.mult))
            own(tt(t2, nr, a_im, ALU.mult))
            own(tt(t1, t1, t2, ALU.subtract))
            own(tt(coef[:, :, 1, :].unsqueeze(3), flat(t1), flat(den), ALU.mult))
            for n in (1, 2, 4):
                q = [zz[:, 3 + 4 * x:3 + 4 * x + n, :].rearrange("p n w -> p (n w)").rearrange(
                    "p (l i n) -> p l i n", l=DEPTH, i=NI) for x in range(2)]
                base = [power(r, n, n + 1).to_broadcast([P, DEPTH, NI, n]) for r in range(2)]
                low = [power(r, 1, n + 1) for r in range(2)]
                for r in range(2):
                    step.add(tt(q[0], low[0], base[r], ALU.mult))
                    own(tt(q[1], low[1], base[1 - r], ALU.mult))
                    own(tt(power(r, n + 1, 2 * n + 1), q[0], q[1], ALU.add if r else ALU.subtract))
            sv = small[:, :, :]
            A8 = [power(r, T, T + 1).rearrange("p l i o -> p l (i o)") for r in range(2)]
            step.add(cp(sv[:, :, S_A8R:S_A8R + NI], A8[0]))
            step.add(ts(sv[:, :, S_A8I:S_A8I + NI], A8[1], -1.0, None, ALU.mult))
            step.add(cp(sv[:, :, S_A8I + NI:S_A8I + 2 * NI], A8[1]))
            q = [x.rearrange("p (l i) -> p l i", l=DEPTH) for x in (t1, t2)]
            step.add(tt(q[0], A8[0], A8[0], ALU.mult))
            own(tt(q[1], A8[1], A8[1], ALU.mult))
            own(tt(sv[:, :, S_A16R:S_A16R + NI], q[0], q[1], ALU.subtract))
            own(tt(q[0], A8[0], A8[1], ALU.mult))
            step.add(ts(sv[:, :, S_A16I:S_A16I + NI], q[0], -2.0, None, ALU.mult))
            step.add(ts(sv[:, :, S_A16I + NI:S_A16I + 2 * NI], q[0], 2.0, None, ALU.mult))
            step.wait()
            cp(zz[:, 0, 0:1], zz[:, 0, 1:2]).then_inc(ssm_ready, 1)

            def add_square(n, done):
                dve.wait_ge(sq_done, done)
                if n:
                    dve.wait_ge(sq_added, done - 1)
                    tt(sqsum[:, :], sqsum[:, :], sq[:, n % 2, :], ALU.add).then_inc(sq_added, 1)
                else:
                    cp(sqsum[:, :], sq[:, 0, :]).then_inc(sq_added, 1)

            for k in range(KT):
                dve.wait_ge(*work.ready(0, f"xT{k}"))
                cp(xT[:, k, :], work.bank(f"xT{k}")[:, 0:TOK]).then_inc(work.emptied(f"xT{k}"), 1)
                if k:
                    add_square(k - 1, k)
            add_square(KT - 1, KT)

            def newton(n):
                dve.wait_ge(rstd_raw, n)
                own(tt(sqsum[:, :], rstd[:, 0, :], rstd[:, 0, :], ALU.mult))
                own(tt(sqsum[:, :], sqsum[:, :], rstd[:, 1, :], ALU.mult))
                own(ts(sqsum[:, :], sqsum[:, :], -0.5, 1.5, ALU.mult, ALU.add))
                own(tt(rstd[:, 0, :], rstd[:, 0, :], sqsum[:, :], ALU.mult))

            def lo_part(l, n):
                unit = SPLIT[n]
                dve.wait_ge(hi_done, l * len(SPLIT) + n + 1)
                tt(w_lo[:, n % HL, :], raw[:, slot_of(unit), :], w_hi[:, n % HL, :].bitcast(F32), ALU.subtract)\
                    .then_inc(used[slot_of(unit)], 1)

            def samples(ap):
                return ap[..., SEQ:TOK].rearrange("p (b t) -> p b t", b=NB)

            def per_sample(m):
                return mod[:, m, 1:CT].unsqueeze(2).to_broadcast([P, NB, T])

            with dve.Fori(0, DEPTH) as l:
                step.restart()
                own(cp(cur[:, :], small[:, bass.ds(l, 1), :].rearrange("p o s -> p (o s)")))
                step.add(ts(nbglu[:, :], cur[:, S_BGLU:S_BGLU + MT], -1.0, None, ALU.mult))
                newton(l + 1)
                lo_part(l, 0)
                lo_part(l, 1)
                dve.wait_ge(used[slot_of("ss15")], uses_at(l, "ss15"))
                tt(mod[:, 0:2 * KT, :], ada[:, 0:2 * KT, :],
                   cur[:, S_BADA:S_BADA + 2 * KT].unsqueeze(2).to_broadcast([P, 2 * KT, CT]), ALU.add)\
                    .then_inc(ada_taken, 1)
                dve.wait_ge(ada_taken, 2 * l + 1)
                stt(mod[:, KT:2 * KT, :], mod[:, KT:2 * KT, :], 1.0,
                    cur[:, S_G:S_G + KT].unsqueeze(2).to_broadcast([P, KT, CT]), ALU.add, ALU.mult)\
                    .then_inc(mod_ready, 1)
                dve.wait_ge(mod_ready, l + 1)

                def norm(k):
                    if k >= 2:
                        dve.wait_ge(hp_done, l * KT + k - 1)
                    tt(hn[:, k % 2, :], xT[:, k, :], rstd[:, 0, :], ALU.mult).then_inc(norm_done, 1)

                norm(0)
                for k in range(KT):
                    dve.wait_ge(norm_done, l * KT + k + 1)
                    own(tt(samples(hf[:, k % 2, :]), samples(hn[:, k % 2, :]), per_sample(KT + k), ALU.mult))
                    tt(samples(hf[:, k % 2, :]), samples(hf[:, k % 2, :]), per_sample(k), ALU.add)\
                        .then_inc(hs_done, 1)
                    if k + 1 < KT:
                        norm(k + 1)
                    dve.wait_ge(hhi_done, l * KT + k + 1)
                    tt(h_lo[:, k, :], hf[:, k % 2, :], h_hi[:, k, :].bitcast(F32), ALU.subtract).then_inc(h_ready, 1)
                for m in range(4):
                    lo_part(l, m + 2)

                def rope(n):
                    job = f"rope{n}"
                    if n:
                        dve.wait_ge(*work.taken(l, f"rope{n - 1}"))
                    dve.wait_ge(*proj.taken(l, f"q{n}" if n < 4 else "k"))
                    step.add(tt(rt[:, 0, :], qraw[:, n % 2, :], cos, ALU.mult))
                    dve.wait_ge(*work.ready(l, job))
                    own(tt(rt[:, 1, :], work.bank(job)[:, 0:TOK], sin, ALU.mult))
                    if n < 4:
                        step.add(tt(qT[:, n, :], rt[:, 0, 0:SEQ], rt[:, 1, 0:SEQ], ALU.add))
                        tt(qs[:, :, n, :], samples(rt[:, 0, :]), samples(rt[:, 1, :]), ALU.add)\
                            .then_inc(work.emptied(job), 1)
                    else:
                        tt(kT[:, :], rt[:, 0, :], rt[:, 1, :], ALU.add).then_inc(work.emptied(job), 1)

                lo_part(l, 6)
                for m in range(3):
                    lo_part(l, 7 + m)
                    rope(m)
                lo_part(l, 10)
                rope(3)
                lo_part(l, 11)
                rope(4)

                dve.wait_ge(*work.ready(l, "h0"))
                cp(Hst[:, :, :, JP:J], work.bank("h0")[:, 0:2 * P].rearrange("p (r b i) -> p r i b", r=2, b=NB))\
                    .then_inc(work.emptied("h0"), 1)
                step.add(v.memset(Hst[:, :, :, 0:1], 0.0))
                for h in range(2):
                    step.add(v.memset(Hblk[h * NST:(h + 1) * NST, :, :, 1 - h, :], 0.0))
                dve.wait_ge(*work.taken(l, "h0"))
                dve.wait_ge(*work.taken(l, "S7"))
                step.wait()

                def wide_of(s0, n, shape):
                    re = cur[:, s0:s0 + NI].unsqueeze(1).unsqueeze(3).to_broadcast(shape)
                    im = cur[:, s0 + NI:s0 + 3 * NI].rearrange("p (r i) -> p r i", r=2).unsqueeze(3)\
                        .to_broadcast(shape)
                    return re, im

                half = [P, 2, NI, JP // 2]
                a8, a8i = wide_of(S_A8R, JP // 2, half)
                even, odd = Ssb[:, :, :, 0:JP:2], Ssb[:, :, :, 1:JP:2]
                step.add(tt(wide, even, a8, ALU.mult))
                own(tt(prod, Ssb[:, ::-1, :, 0:JP:2], a8i, ALU.mult))
                own(tt(wide, wide, odd, ALU.add))
                own(tt(wide, wide, prod, ALU.add))

                def silu(n, job, dst):
                    dve.wait_ge(gate_exp, l * 8 + n + 1)
                    e = ez[:, n % 2, :]
                    own(ts(e, e, 1.0, None, ALU.add))
                    own(v.reciprocal(e, e))
                    tt(dst, proj.bank(job)[:, 0:TOK], e, ALU.mult).then_inc(proj.emptied(job), 1)

                one = [P, 2, NI]
                a16 = cur[:, S_A16R:S_A16R + NI].unsqueeze(1).to_broadcast(one)
                a16i = cur[:, S_A16I:S_A16I + 2 * NI].rearrange("p (r i) -> p r i", r=2)
                own(cp(Hst[:, :, :, 2], wide[:, :, :, 0]))
                for k in range(1, JP // 2):
                    H = Hst[:, :, :, 2 * k]
                    last = k == JP // 2 - 1
                    step.add(tt(rec[:, 0], H, a16, ALU.mult))
                    step.add(tt(rec[:, 1], Hst[:, ::-1, :, 2 * k], a16i, ALU.mult))
                    step.wait()
                    own(tt(rec[:, 0], rec[:, 0], wide[:, :, :, k], ALU.add))
                    own(tt(fin[:, :, 0, :] if last else Hst[:, :, :, 2 * k + 2], rec[:, 0], rec[:, 1], ALU.add))
                    if k in (4, 8, 12):
                        silu(k // 4 - 1, f"za{k // 4 - 1}", ga[:, k // 4 - 1, :])
                        lo_part(l, 11 + k // 4)
                step.add(tt(Hst[:, :, :, 1:JP:2], Hst[:, :, :, 0:JP:2], a8, ALU.mult))
                own(tt(prod, Hst[:, ::-1, :, 0:JP:2], a8i, ALU.mult))
                own(tt(Hst[:, :, :, 1:JP:2], Hst[:, :, :, 1:JP:2], even, ALU.add))
                own(tt(Hst[:, :, :, 1:JP:2], Hst[:, :, :, 1:JP:2], prod, ALU.add))
                b8, b8i = wide_of(S_A8R, NB, [P, 2, NI, NB])
                part = [x[:, :, :, 0:NB] for x in (wide, prod)]
                step.add(tt(part[0], Hst[:, :, :, JP:J], b8, ALU.mult))
                own(tt(part[1], Hst[:, ::-1, :, JP:J], b8i, ALU.mult))
                own(tt(part[0], part[0], Ssb[:, :, :, JP:J], ALU.add))
                tt(fin[:, :, 1:1 + NB, :].rearrange("p r b i -> p r i b"), part[0], part[1], ALU.add)\
                    .then_inc(fin_ready, 1)
                for h in range(2):
                    rows = slice(h * NST, (h + 1) * NST)
                    cp(Hblk[rows, :, :, h, :], Hst[rows]).then_inc(H_ready, 1)
                silu(3, "za3", ga[:, 3, :])
                lo_part(l, 15)

                for kv in range(KV):
                    job = f"sc0{kv}"
                    dve.wait_ge(*work.ready(l, job))
                    tt(P0[:, kv], work.bank(job)[:, :].rearrange("p (i k) -> p i k", i=NQ),
                       const[:, C_MP + P:C_MP + 2 * P].unsqueeze(1).to_broadcast([P, NQ, P]), ALU.add)\
                        .then_inc(work.emptied(job), 1)
                for n in range(4):
                    job = f"sc1{n}"
                    dve.wait_ge(*work.ready(l, job))
                    tt(P1[:, n // 2, 2 * (n % 2):2 * (n % 2) + 2], work.bank(job)[:, :].rearrange("p (i k) -> p i k", i=2),
                       const[:, C_MP:C_MP + 2 * P].unsqueeze(1).to_broadcast([P, 2, 2 * P]), ALU.add)\
                        .then_inc(work.emptied(job), 1)
                for kv in range(KV):
                    job = f"ss{kv}"
                    dve.wait_ge(*work.ready(l, job))
                    tt(Ps[:, kv], work.bank(job)[:, 0:2 * (WIN + NS)].rearrange("p (b k) -> p b k", b=2),
                       const[:, C_MS:C_MS + 2 * (WIN + NS)].rearrange("p (b k) -> p b k", b=2), ALU.add)\
                        .then_inc(work.emptied(job), 1)

                def maximum(g):
                    buf, n = ((P0, NQ), (P1, NQ), (Ps, 2))[g]
                    job = ("sc01", "sc13", "ss1")[g]
                    dve.wait_ge(*work.taken(l, job))
                    x = KV * n
                    sink = (cur[:, S_SINKP:S_SINKP + 8] if g < 2
                            else cur[:, S_SINKS:S_SINKS + KV].unsqueeze(2).to_broadcast([P, KV, 2]))
                    s = [sm[:, g, q, 0:x] if g < 2 else sm[:, g, q, 0:x].rearrange("p (v b) -> p v b", v=KV)
                         for q in range(5)]
                    own(v.tensor_reduce(sm[:, g, 0, 0:x].rearrange("p (v i) -> p v i", v=KV), buf, AX.X, ALU.max))
                    own(stt(s[0], s[0], SCALE, sink, ALU.mult, ALU.max))
                    own(ts(s[1], s[0], -1.0, None, ALU.mult))
                    tt(s[3], sink, s[0], ALU.subtract).then_inc(max_ready, 1)

                def normalize(g):
                    buf, n = ((P0, NQ), (P1, NQ), (Ps, 2))[g]
                    x = KV * n
                    dve.wait_ge(p_exp, l * 3 + g + 1)
                    own(tt(sm[:, g, 2, 0:x], sm[:, g, 2, 0:x], sm[:, g, 3, 0:x], ALU.add))
                    own(v.reciprocal(sm[:, g, 4, 0:x], sm[:, g, 2, 0:x]))
                    r = sm[:, g, 4, 0:x].rearrange("p (v i) -> p v i", v=KV).unsqueeze(3)\
                        .to_broadcast([P, KV, n, buf.shape[3]])
                    tt(buf, buf, r, ALU.mult).then_inc(p_ready, 1)

                for n in range(4):
                    silu(4 + n, f"zs{n}", gs[:, n, :])
                    lo_part(l, 16 + n)
                    if n < 3:
                        maximum(n)
                for g in range(3):
                    normalize(g)

                for m in range(MT):
                    dve.wait_ge(y_back, (l + 1) * 64)
                    stt(ycp[:, m, :], u_sb[:, m].rearrange("p t j -> p (t j)"), cur[:, S_D + m:S_D + m + 1],
                        ycp[:, m, :], ALU.mult, ALU.add).then_inc(y1_ready, 1)
                dve.wait_ge(y1_ready, (l + 1) * MT)
                for m in range(MT):
                    e = ez[:, m % 2, :]
                    dve.wait_ge(y_sq, l * MT + m + 1)
                    own(ts(e, e, GELU_A, 1.0, ALU.mult, ALU.add))
                    own(tt(e, e, ycp[:, m, :], ALU.mult))
                    ts(e, e, -EXP_SAFE / GELU_B, None, ALU.max).then_inc(y_arg, 1)
                    dve.wait_ge(y_exp, l * MT + m + 1)
                    own(ts(e, e, 1.0, None, ALU.add))
                    own(v.reciprocal(e, e))
                    tt(yg[:, m, :], e, ycp[:, m, :], ALU.mult).then_inc(yg_ready, 1)
                    dve.wait_ge(yghi, l * MT + m + 1)
                    tt(h_lo[:, MT + m, :], yg[:, m, :], h_hi[:, MT + m, :].bitcast(F32), ALU.subtract)\
                        .then_inc(yglo, 1)

                for n, (job, toks) in enumerate((("pv0", slice(0, P)), ("pv1", slice(P, SEQ)), ("pvs", slice(SEQ, TOK)))):
                    dve.wait_ge(*work.ready(l, job))
                    if n < 2:
                        tt(ga[:, :, toks], work.bank(job)[:, :].rearrange("p (i q) -> p i q", i=NQ), ga[:, :, toks],
                           ALU.mult).then_inc(work.emptied(job), 1)
                    else:
                        g4 = ga[:, :, toks].rearrange("p i (b t) -> p i b t", b=NB)
                        tt(g4, work.bank(job)[:, 0:NS * NQ].rearrange("p (b i t) -> p i b t", b=NB, i=NQ), g4,
                           ALU.mult).then_inc(work.emptied(job), 1)
                    dve.wait_ge(mixhi, l * 7 + n + 1)
                    tt(h_lo[:, 0:MT, toks], ga[:, :, toks], h_hi[:, 0:MT, toks].bitcast(F32), ALU.subtract)\
                        .then_inc(mix_ready, 1)

                dve.wait_ge(used[slot_of("gate7")], uses_at(l, "gate7"))
                tt(mod[:, 2 * KT:3 * KT, :], ada[:, 2 * KT:3 * KT, :],
                   cur[:, S_BADA + 2 * KT:S_BADA + 3 * KT].unsqueeze(2).to_broadcast([P, KT, CT]), ALU.add)\
                    .then_inc(ada_taken, 1)

                for m in range(MT):
                    e = ez[:, m % 2, :]
                    dve.wait_ge(*proj.ready(l, f"glu{m}"))
                    if m == 0:
                        dve.wait_ge(yghi, (l + 1) * MT)
                    ts(e, proj.bank(f"glu{m}")[:, 0:TOK], nbglu[:, m:m + 1], -EXP_SAFE, ALU.subtract, ALU.max)\
                        .then_inc(proj.emptied(f"glu{m}"), 1)
                    dve.wait_ge(glu_exp, l * MT + m + 1)
                    own(ts(e, e, 1.0, None, ALU.add))
                    own(v.reciprocal(e, e))
                    own(tt(e, e, yg[:, m, :], ALU.mult))
                    dst = gs[:, m, :].rearrange("p (j t) -> p t j", t=T)
                    tt(dst, dst, e.rearrange("p (t j) -> p t j", t=T), ALU.mult).then_inc(gated, 1)
                    if m == 1:
                        lo_part(l, 20)
                    if m == 3:
                        lo_part(l, 21)
                for m in range(MT):
                    dve.wait_ge(mixhi, l * 7 + 4 + m)
                    tt(h_lo[:, MT + m, :], gs[:, m, :], h_hi[:, MT + m, :].bitcast(F32), ALU.subtract)\
                        .then_inc(mix_ready, 1)
                dve.wait_ge(ada_taken, 2 * l + 2)
                for m in range(8):
                    job = f"out{m}"
                    dve.wait_ge(*proj.ready(l, job))
                    b = proj.bank(job)
                    step.add(stt(xT[:, m, 0:SEQ], b[:, 0:SEQ], mod[:, 2 * KT + m, 0:1], xT[:, m, 0:SEQ],
                                 ALU.mult, ALU.add))
                    if m:
                        dve.wait_ge(x_ready, l * KT + m)
                    tt(rt[:, 0, 0:NS].rearrange("p (b t) -> p b t", b=NB), samples(b[:, 0:TOK]),
                       per_sample(2 * KT + m), ALU.mult).then_inc(proj.emptied(job), 1)
                    dve.wait_ge(*proj.taken(l, job))
                    tt(xT[:, m, SEQ:TOK], xT[:, m, SEQ:TOK], rt[:, 0, 0:NS], ALU.add).then_inc(x_ready, 1)
                    if m < 6:
                        lo_part(l, 22 + m)
                    if m:
                        add_square(m - 1, (l + 1) * KT + m)
                add_square(KT - 1, (l + 1) * KT + KT)
                dve.wait_ge(state_stored, (l + 1) * 64)

            step.restart()
            newton(DEPTH + 1)
            for k in range(KT):
                stt(xT[:, k, :], xT[:, k, :], fing[:, k:k + 1], rstd[:, 0, :], ALU.mult, ALU.mult)\
                    .then_inc(yn_ready, 1)

        @block.gpsimd
        def _(pool):
            step = Steps(pool, pool_step)
            tt = nc.gpsimd.tensor_tensor

            def own(ins):
                step.add(ins)
                step.wait()

            nc.gpsimd.memset(Bblk[:, :, :, :, :], 0.0).then_inc(zeros_set, 1)
            nc.gpsimd.memset(Toep[:, :, :], 0.0).then_inc(zeros_set, 1)
            pool.wait_ge(zeros_set, 2)
            pool.wait_ge(ssm_ready, 1)
            pool.wait_ge(*proj.taken(0, "BT1"))
            pool.wait_ge(*work.taken(0, "CT3"))

            def prepare(l, before):
                one = bass.ds(l, 1)

                def flat(ap):
                    return ap.rearrange("p o i x -> p (o i) x")

                for r in range(2):
                    cr = [coef[:, one, q, :].rearrange("p o i -> p (o i)").unsqueeze(2).to_broadcast([P, NI, GC])
                          for q in (0, 1)]
                    b = [flat(Bsb[:, one, q]) for q in ((0, 1) if r == 0 else (1, 0))]
                    t = [pt[:, q, 0:NI * GC].rearrange("p (i c) -> p i c", i=NI) for q in range(2)]
                    step.add(tt(t[0], b[0], cr[0], ALU.mult))
                    own(tt(t[1], b[1], cr[1], ALU.mult))
                    own(tt(Bbar[:, r], t[0], t[1], ALU.add if r else ALU.subtract))

                def turned(n):
                    r, i0 = n % 2, 4 * (n // 2)
                    if n >= 2:
                        pool.wait_ge(*work.ready(l, f"WB{n - 2}"))
                    elif before is not None:
                        pool.wait_ge(*work.ready(before, f"WB{n + 6}"))
                    shape = [P, 4, T, GC]
                    t = [pt[:, q, 0:4 * T * GC].rearrange("p (i s c) -> p i s c", i=4, s=T) for q in range(2)]
                    for q in range(2):
                        A = Apow[:, one, q, i0:i0 + 4, T - 1::-1].rearrange("p o i s -> p (o i) s").unsqueeze(3)\
                            .to_broadcast(shape)
                        B = Bbar[:, q if r == 0 else 1 - q, i0:i0 + 4, :].unsqueeze(2).to_broadcast(shape)
                        step.add(tt(t[q], A, B, ALU.mult))
                    step.wait()
                    tt(WBq[:, n % 2].rearrange("p i (s c) -> p i s c", s=T), t[0], t[1],
                       ALU.add if r else ALU.subtract).then_inc(wb_ready, 1)
                    pool.wait_ge(wb_ready, l * 8 + n + 1)

                turned(0)
                turned(1)
                if before is not None:
                    pool.wait_ge(*work.ready(before, "y3"))
                for h in range(2):
                    rows = slice(h * NST, (h + 1) * NST)
                    own(nc.gpsimd.tensor_copy(Bblk[rows, :, :, h, :], Bbar[rows]))
                for i0 in range(0, NI, 2):
                    shape = [P, 2, T + 1, GC]
                    t = [pt[:, q, 0:2 * (T + 1) * GC].rearrange("p (i s c) -> p i s c", i=2, s=T + 1)
                         for q in range(2)]
                    for r in range(2):
                        for q in range(2):
                            A = Apow[:, one, q, i0:i0 + 2, :].rearrange("p o i s -> p (o i) s").unsqueeze(3)\
                                .to_broadcast(shape)
                            C = Csb[:, one, q if r == 0 else 1 - q, i0:i0 + 2, :].rearrange("p o i c -> p (o i) c")\
                                .unsqueeze(2).to_broadcast(shape)
                            step.add(tt(t[q], A, C, ALU.mult))
                        step.wait()
                        ins = tt(Gm[:, r, i0:i0 + 2], t[0], t[1], ALU.subtract if r else ALU.add)
                        if (i0, r) == (NI - 2, 1):
                            ins.then_inc(g_ready, 1)
                            pool.wait_ge(g_ready, l + 1)
                        else:
                            own(ins)
                for n in range(2, 8):
                    turned(n)

            prepare(0, None)
            with pool.Fori(0, DEPTH - 1) as before:
                step.restart()
                prepare(before + 1, before)


NAMES = ["x_prompt", "x_sample", "cache_k", "cache_v", "state_ssm_re", "state_ssm_im", "c_prompt", "c_sample",
         "norm_g", "w_ada", "b_ada", "w_in", "attn_sinks", "ssm_a_re", "ssm_a_im", "ssm_log_dt",
         "ssm_b_re", "ssm_b_im", "ssm_c_re", "ssm_c_im", "ssm_d", "w_glu", "b_glu", "w_out", "final_g"]
OUTS = [(1, SEQ, D), (NB, T, D), (DEPTH, 1, WIN, KV, HD), (DEPTH, 1, WIN, KV, HD), (DEPTH, 1, G, NST),
        (DEPTH, 1, G, NST), (DEPTH, NB, WIN, KV, HD), (DEPTH, NB, WIN, KV, HD), (DEPTH, NB, G, NST),
        (DEPTH, NB, G, NST)]


def kernel(**inputs):
    import concourse.bacc as bacc
    from concourse.bass_utils import run_bass_kernel_spmd

    nc = bacc.Bacc("TRN2", target_bir_lowering=False, num_devices=1, dynamic_dma_scratch_size=1024)
    arrays = {f"in_{n}": np.ascontiguousarray(inputs[n]) for n in NAMES}
    arrays["in_constants"] = constants()
    a = {n[3:]: nc.dram_tensor(n, x.shape, mybir.dt.from_np(x.dtype), kind="ExternalInput").ap()
         for n, x in arrays.items()}
    out = [nc.dram_tensor(f"out_{i}", s, F32, kind="ExternalOutput").ap() for i, s in enumerate(OUTS)]
    build(nc, a, out)
    r = run_bass_kernel_spmd(nc, [arrays], core_ids=[0])
    return tuple(r.results[0][f"out_{i}"] for i in range(len(OUTS)))
```

```python
from contextlib import ExitStack

import numpy as np

import concourse.bass as bass
from concourse import mybir
from concourse.alu_op_type import AluOpType as ALU

F32 = mybir.dt.float32
F32R = mybir.dt.float32r
ACT = mybir.ActivationFunctionType
AX = mybir.AxisListType

P = 128
D = 1024
KT = D // P
DEPTH = 2
SEQ = 256
NB = 8
T = 8
NS = NB * T
TOK = SEQ + NS
J = TOK // T
JP = SEQ // T
HD = 64
NQ = 4
KV = 2
WIN = 128
IN_W = 2304
COL_K, COL_V, COL_ZA, COL_U, COL_ZS = 512, 640, 768, 1280, 1792
NI = 16
GC = 16
NST = 64
G = 2 * NI
MT = 4
PAST = 1024
EPS = 1e-6
NEG = -1e30
CT = 1 + NB
SCALE = HD ** -0.5
ROT = HD // 4
GELU_A = 0.044715
GELU_B = 0.7978845608028654
TWO_PI = 6.283185307179586
PI_1, PI_2 = 6.28125, 0.0019350051879882812
PI_3 = TWO_PI - PI_1 - PI_2
PI_SAFE = 3.1415925
ROUND = 12582912.0

C_ID, C_ROT, C_COS, C_SIN = 0, 128, 256, 576
C_MP, C_MS, C_SEL, C_END = 896, 1152, 1536, 1664

S_G, S_BADA, S_BGLU, S_D, S_SINKP, S_SINKS = 0, 8, 32, 36, 40, 48
S_A8R, S_A8I, S_A16R, S_A16I, S_END = 50, 66, 98, 114, 146
ROWS_L = 40

AC = 512
ADA_SS, ADA_GATE = (0, 2, 1, 3), (4, 5)
AROW = 32

UNITS = ([f"ss{m}" for m in range(16)] + [f"u{m}" for m in range(4)] + [f"q{m}" for m in range(4)]
         + ["k", "v"] + [f"za{m}" for m in range(4)] + [f"zs{m}" for m in range(4)]
         + ["glu0", "glu1"] + [f"gate{m}" for m in range(8)] + [f"out{m}" for m in range(8)])
RAW = 4
SPLIT = [u for u in UNITS if not u.startswith(("ss", "gate"))]
HL = 2
DMAS = {u: 2 if u[0] == "q" or u[:2] == "za" else 3 if u.startswith("out") else 1 for u in UNITS}

PROJ_JOBS = ([f"u{m}" for m in range(4)] + [f"q{m}" for m in range(4)] + ["k"]
             + [f"za{m}" for m in range(4)] + [f"zs{m}" for m in range(4)]
             + [f"glu{m}" for m in range(4)] + [f"out{m}" for m in range(8)])
FIRST_PROJ_JOBS = ["BT0", "BT1", "sinks"]
FIRST_JOBS = (["cT", "rowsT"] + [f"CT{n}" for n in range(4)]
              + [f"xT{k}" for k in range(KT)])
WORK_JOBS = (["rms"] + [x for c in ADA_SS for x in (f"am{c}", f"at{c}")]
             + ["WB0", "WB1", "rope0", "WB2", "WB3", "rope1", "WB4", "WB5", "rope2", "WB6", "WB7",
                "rope3", "v", "rope4", "h0", "kcT0", "kcT1"]
             + [f"S{n}" for n in range(8)] + [f"K{n}" for n in range(4)] + ["ktok"]
             + [f"y{n}" for n in range(4)] + ["state"]
             + ["sc00", "sc01", "sc10", "sc11", "sc12", "sc13", "ss0", "ss1"]
             + [x for c in ADA_GATE for x in (f"am{c}", f"at{c}")]
             + [f"PT{n}" for n in range(6)] + ["pv0", "pv1", "PTc", "PTn", "pvs"])
LAST_JOBS = ["rmsF"] + [f"yT{n}" for n in range(6)]


def constants():
    c = np.zeros((P, C_END), np.float32)
    c[:, C_ID:C_ID + P] = np.eye(P, dtype=np.float32)
    half = ROT // 2
    inv = (np.float32(500000.0) ** (-np.arange(half, dtype=np.float32) / np.float32(half))).astype(np.float32)
    pos = np.concatenate([np.arange(SEQ), np.tile(PAST + np.arange(T), NB)]).astype(np.float32)
    ang = pos[None, :] * inv[:, None]
    c[:, C_COS:C_COS + TOK] = 1.0
    for kv in range(KV):
        a = kv * HD
        for d in range(half):
            c[a + d, C_COS:C_COS + TOK] = c[a + d + half, C_COS:C_COS + TOK] = np.cos(ang[d])
            c[a + d, C_SIN:C_SIN + TOK] = -np.sin(ang[d])
            c[a + d + half, C_SIN:C_SIN + TOK] = np.sin(ang[d])
            c[a + d + half, C_ROT + a + d] = c[a + d, C_ROT + a + d + half] = 1.0
    r = np.arange(P)
    diff = P + r[:, None] - np.arange(2 * P)[None, :]
    c[:, C_MP:C_MP + 2 * P] = np.where((diff >= 0) & (diff <= WIN), 0.0, NEG)
    b4, t = r // 32, r % T
    for half_b in range(2):
        m = np.full((P, WIN + NS), NEG, np.float32)
        m[:, :WIN][np.arange(WIN)[None, :] >= t[:, None]] = 0.0
        col = np.arange(NS)
        m[:, WIN:][(col[None, :] // T == (half_b * 4 + b4)[:, None]) & (col[None, :] % T <= t[:, None])] = 0.0
        c[:, C_MS + half_b * (WIN + NS):C_MS + (half_b + 1) * (WIN + NS)] = m
    for i in range(NQ):
        c[i, C_SEL:C_SEL + P] = (r // T % NQ == i)
    return c


class Ring:

    def __init__(self, banks, filled, emptied, first, layer, last):
        self.banks, self.n = banks, len(banks)
        self._filled, self._emptied = filled, emptied
        self.first, self.layer, self.last = first, layer, last

    def _at(self, l, job):
        n = self.n
        of = [sum(1 for q in range(len(x)) if q % n == b) for x in (self.first, self.layer) for b in range(n)]
        if job in self.layer:
            q = self.layer.index(job)
            return q % n, of[q % n] + l * of[n + q % n] + q // n
        if job in self.first:
            q = self.first.index(job)
            return q % n, q // n
        q = self.last.index(job)
        return q % n, of[q % n] + DEPTH * of[n + q % n] + q // n

    def bank(self, job):
        for x in (self.first, self.layer, self.last):
            if job in x:
                return self.banks[x.index(job) % self.n]

    def room(self, l, job):
        b, k = self._at(l, job)
        return self._emptied[b], k

    def ready(self, l, job):
        b, k = self._at(l, job)
        return self._filled[b], k + 1

    def taken(self, l, job):
        b, k = self._at(l, job)
        return self._emptied[b], k + 1

    def filled(self, job):
        return self._filled[self._at(0, job)[0]]

    def emptied(self, job):
        return self._emptied[self._at(0, job)[0]]


class Steps:

    def __init__(self, eng, sem):
        self.eng, self.sem, self.n = eng, sem, 0

    def add(self, ins):
        self.n += 1
        ins.then_inc(self.sem, 1)

    def wait(self):
        self.eng.wait_ge(self.sem, self.n)

    def restart(self):
        if self.n:
            self.wait()
        self.eng.sem_clear(self.sem)
        self.n = 0


def slot_of(unit):
    return UNITS.index(unit) % RAW


def loads_at(l, unit):
    s = slot_of(unit)
    own = [u for u in UNITS if slot_of(u) == s]
    return l * (16 * sum(DMAS[u] for u in own)) + 16 * sum(DMAS[u] for u in own[:own.index(unit) + 1])


def uses_at(l, unit):
    return l * (len(UNITS) // RAW) + UNITS.index(unit) // RAW + 1


def build(nc, a, out):
    ctx = ExitStack()
    with ctx:
        def sb(name, shape, dt=F32):
            return ctx.enter_context(nc.sbuf_tensor(name, shape, dt))

        def sem(name):
            return ctx.enter_context(nc.semaphore(name))

        banks = [ctx.enter_context(nc.psum_tensor(f"bank{b}", [P, 512], F32)) for b in range(8)]

        const = sb("const", [P, C_SEL])
        ident = const[:, C_ID:C_ID + P]
        rot = const[:, C_ROT:C_ROT + P]
        cos, sin = const[:, C_COS:C_COS + TOK], const[:, C_SIN:C_SIN + TOK]
        mean = sb("mean", [P, P])
        raw = sb("raw", [P, RAW, D])
        w_hi = sb("w_hi", [P, HL, D], F32R)
        w_lo = sb("w_lo", [P, HL, D], F32R)
        xT = sb("xT", [P, KT, TOK])
        h_hi = sb("h_hi", [P, KT, TOK], F32R)
        h_lo = sb("h_lo", [P, KT, TOK], F32R)
        hn = sb("hn", [P, 2, TOK])
        hf = sb("hf", [P, 2, TOK])
        ez = sb("ez", [P, 2, TOK])
        sq = ez
        sqsum = sb("sqsum", [P, TOK])
        rstd = sb("rstd", [P, 2, TOK])
        u_sb = sb("u_sb", [P, MT, T, J])
        U = sb("U", [P, G, J])
        HY = sb("HY", [P, 2 * NI * J])
        Hst = HY[:, :].rearrange("p (r i j) -> p r i j", r=2, i=NI)
        Ysb = HY[:, 0:G * J].rearrange("p (g j) -> p g j", g=G)
        R1 = sb("R1", [P, 4096])
        Ssb = R1[:, 0:1280].rearrange("p (r i j) -> p r i j", r=2, i=NI)
        Hblk = R1[:, 1280:1280 + 2560].rearrange("p (r i h j) -> p r i h j", r=2, i=NI, h=2)
        xn = R1[:, 0:KT * TOK].rearrange("p (k n) -> p k n", k=KT)
        P0 = R1[:, 0:1024].rearrange("p (v i k) -> p v i k", v=KV, i=NQ)
        P1 = R1[:, 1024:3072].rearrange("p (v i k) -> p v i k", v=KV, i=NQ)
        Ps = R1[:, 3072:3840].rearrange("p (v b k) -> p v b k", v=KV, b=2)
        R2 = sb("R2", [P, 4096])
        xin = R2[:, 0:3 * D].rearrange("p (n d) -> p n d", n=3)
        WBt = R2[:, :].rearrange("p (i r q) -> p i r q", i=NI, r=2)
        PT = R2[:, 0:3072].rearrange("p (n v q) -> p n v q", n=3, v=KV)
        PTc = R2[:, 3072:3584].rearrange("p (v b q) -> p v b q", v=KV, b=2)
        PTn = R2[:, 3584:4096].rearrange("p (v b q) -> p v b q", v=KV, b=2)
        R3 = sb("R3", [P, 2560])
        kc = R3[:, 0:1024].rearrange("p (b d) -> p b d", b=NB)
        h0 = R3[:, 1024:1024 + 2 * P].rearrange("p (r q) -> p r q", r=2)
        Ksb = R3[:, 0:2048].rearrange("p (i q) -> p i q", i=NI)
        ycp = R3[:, 0:1280].rearrange("p (m n) -> p m n", m=MT)
        yg = R3[:, 1280:2560].rearrange("p (m n) -> p m n", m=MT)
        WBq = sb("WBq", [P, 2, 4, P])
        Gm = sb("Gm", [P, 2, NI, T + 1, GC])
        Toep = sb("Toep", [P, G, P])
        Apow = sb("Apow", [P, DEPTH, 2, NI, T + 1])
        coef = sb("coef", [P, DEPTH, 2, NI])
        Bsb = sb("Bsb", [P, DEPTH, 2, NI, GC])
        Csb = sb("Csb", [P, DEPTH, 2, NI, GC])
        Bblk = sb("Bblk", [P, 2, NI, 2, GC])
        pt = sb("pt", [P, 2, 4 * GC * T])
        qT = sb("qT", [P, NQ, SEQ])
        qs = sb("qs", [P, NB, NQ, T])
        kT = sb("kT", [P, TOK])
        qraw, rt = hn, hf
        vtok = sb("vtok", [P, 3, P])
        ktok = R3[:, 2048:2048 + 2 * P].rearrange("p (n q) -> p n q", n=2)
        kcT = sb("kcT", [P, NB, WIN])
        vc = U[:, :, :].rearrange("p g j -> p (g j)")[:, 0:NB * P].rearrange("p (b q) -> p b q", b=NB)
        fin = sb("fin", [P, 2, 1 + NB, NI])
        stage = hn[:, :, :].rearrange("p a b -> p (a b)")[:, 0:4 * P].rearrange("p (n q) -> p n q", n=4)
        ga = sb("ga", [P, MT, TOK])
        gs = sb("gs", [P, MT, TOK])
        small = sb("small", [P, DEPTH, S_END])
        cur = sb("cur", [P, S_END])
        hbglu = sb("hbglu", [P, MT])
        fing = sb("fing", [P, KT])
        cT = sb("cT", [P, KT, AROW])
        mod = sb("mod", [P, 3 * KT, CT])
        epsb = sb("epsb", [P, 1])
        sm = sb("sm", [P, 3, 5, 8])
        rec = sb("rec", [P, 2, 2, NI])
        arow = hn[:, :, :].rearrange("p a b -> p (a b)")[:, 0:AC]
        wide = hn[:, :, :].rearrange("p a b -> p (a b)")[:, 0:JP * NI].rearrange("p (r i k) -> p r i k", r=2, i=NI)
        prod = hf[:, :, :].rearrange("p a b -> p (a b)")[:, 0:JP * NI].rearrange("p (r i k) -> p r i k", r=2, i=NI)
        Bbar = sb("Bbar", [P, 2, NI, GC])

        crow = R3[0:CT, 0:D]
        cexp = R3[0:CT, D:2 * D]
        rowsP = R1[0:2 * ROWS_L + KT, 0:P]
        rowsS = R1[0:3 * DEPTH * NI, P:2 * P]
        ldt = R1[0:DEPTH * NI, 2 * P:2 * P + 2]
        sel = R1[0:NQ, 330:330 + P]
        sinkc = R1[0:NQ, 320:324]
        Braw = R1[0:2 * DEPTH * NI, 512:512 + 2048]
        Craw = Gm[:, :, :, :, :].rearrange("p r i t c -> p (r i t c)")[:, 0:2048].rearrange(
            "p (n t d q) -> p n t d q", n=2 * DEPTH, t=4, d=2)
        rowsT = HY[:, 0:224]
        W = DEPTH * NI
        zz = HY[:, 256:256 + 20 * W].rearrange("p (n w) -> p n w", n=20)

        u_dram = nc.dram_tensor("u_turn", [G, GC, T, J], F32, kind="Internal").ap()
        y_dram = nc.dram_tensor("y_turn", [G, GC, T, J], F32, kind="Internal").ap()

        loaded = [sem(f"unit_loaded{s}") for s in range(RAW)]
        used = [sem(f"unit_used{s}") for s in range(RAW)]
        hi_done = sem("hi_done")
        const_in, cond_in, x_in, small_in, bc_in = (sem(n) for n in
                                                     ("const_in", "cond_in", "x_in", "small_in", "bc_in"))
        vcache_in = sem("vcache_in")
        cache_in, h0_in, skew_in = sem("cache_in"), sem("h0_in"), sem("skew_in")
        u_out, u_back, y_out, y_back = sem("u_out"), sem("u_back"), sem("y_out"), sem("y_back")
        kv_stored, state_stored, cache_copied, y_stored = (sem(n) for n in
                                                            ("kv_stored", "state_stored", "cache_copied", "y_stored"))
        proj = Ring(banks[0:3], [sem(f"proj_filled{b}") for b in range(3)],
                    [sem(f"proj_emptied{b}") for b in range(3)], FIRST_PROJ_JOBS, PROJ_JOBS, [])
        work = Ring(banks[3:8], [sem(f"work_filled{b}") for b in range(5)],
                    [sem(f"work_emptied{b}") for b in range(5)], FIRST_JOBS, WORK_JOBS, LAST_JOBS)
        dve_step, act_step, pool_step = sem("dve_step"), sem("act_step"), sem("pool_step")
        silu_c, silu_r = sem("silu_c"), sem("silu_r")
        sinks_in = sem("sinks_in")
        ldt_wide = sem("ldt_wide")
        ssm_exp = sem("ssm_exp")
        ssm_val = sem("ssm_val")
        ssm_ready = sem("ssm_ready")
        x_ready = sem("x_ready")
        sq_done, sq_added = sem("sq_done"), sem("sq_added")
        rstd_raw = sem("rstd_raw")
        norm_done = sem("norm_done")
        hp_done, hs_done = sem("hp_done"), sem("hs_done")
        hhi_done, h_ready = sem("hhi_done"), sem("h_ready")
        mod_ready = sem("mod_ready")
        mean_set = sem("mean_set")
        wb_ready, g_ready, zeros_set = sem("wb_ready"), sem("g_ready"), sem("zeros_set")
        H_ready, fin_ready = sem("H_ready"), sem("fin_ready")
        gate_tanh = sem("gate_tanh")
        max_ready, p_exp, p_ready = sem("max_ready"), sem("p_exp"), sem("p_ready")
        mixhi, mix_ready = sem("mixhi"), sem("mix_ready")
        y1_ready, y_sq, y_arg, y_tanh = sem("y1_ready"), sem("y_sq"), sem("y_arg"), sem("y_tanh")
        yg_ready, yghi, yglo = sem("yg_ready"), sem("yghi"), sem("yglo")
        gated = sem("gated")
        yn_ready = sem("yn_ready")

        block = ctx.enter_context(nc.Block())

        @block.sync
        def _(sp):
            def one_layer(l):
                return slice(l, l + 1) if isinstance(l, int) else bass.ds(l, 1)

            def load(l, unit):
                n, s = UNITS.index(unit), slot_of(unit)
                if not (isinstance(l, int) and l == 0) or n >= RAW:
                    sp.wait_ge(used[s], uses_at(l, unit) - 1)
                dst = raw[:, s, :].rearrange("p (k c) -> p k c", k=KT)
                own = one_layer(l)
                kind, m = unit.rstrip("0123456789"), int("0" + unit.lstrip("abcdefghijklmnopqrstuvwxyz"))
                if kind in ("ss", "gate"):
                    c0, r0 = (ADA_SS if kind == "ss" else ADA_GATE)[m // 4] * AC, m % 4 * 2 * P
                    src = a["w_ada"][own, r0:r0 + 2 * P, c0:c0 + AC].rearrange("o (k p) c -> p (o k) c", p=P)
                    sp.dma_start(raw[:, s, :].rearrange("p (k c) -> p k c", k=2), src).then_inc(loaded[s], 16)
                elif kind in ("q", "za"):
                    for kv in reversed(range(KV)):
                        c0 = (0 if kind == "q" else COL_ZA) + kv * NQ * HD + m * HD
                        src = a["w_in"][own, :, c0:c0 + HD].rearrange("o (k p) c -> p (o k) c", p=P)
                        sp.dma_start(dst[:, :, kv * HD:(kv + 1) * HD], src).then_inc(loaded[s], 16)
                elif kind in ("u", "k", "v", "zs"):
                    c0 = {"u": COL_U, "k": COL_K, "v": COL_V, "zs": COL_ZS}[kind] + m * P
                    src = a["w_in"][own, :, c0:c0 + P].rearrange("o (k p) c -> p (o k) c", p=P)
                    sp.dma_start(dst, src).then_inc(loaded[s], 16)
                elif kind == "glu":
                    src = a["w_glu"][own, :, m * 2 * P:(m + 1) * 2 * P].rearrange("o (k p) c -> p (o k) c", p=P)
                    sp.dma_start(raw[:, s, :].rearrange("p (k c) -> p k c", k=MT), src).then_inc(loaded[s], 16)
                else:
                    for kv in range(KV):
                        r0 = kv * NQ * HD
                        src = a["w_out"][own, r0:r0 + NQ * HD, m * P:(m + 1) * P].rearrange(
                            "o (k p) c -> p (o k) c", p=HD)
                        sp.dma_start(dst[kv * HD:(kv + 1) * HD, 0:MT, :], src).then_inc(loaded[s], 16)
                    src = a["w_out"][own, MT * P:, m * P:(m + 1) * P].rearrange("o (k p) c -> p (o k) c", p=P)
                    sp.dma_start(dst[:, MT:KT, :], src).then_inc(loaded[s], 16)

            def caches(l):
                own = one_layer(l)
                sp.dma_start(kc, a["cache_k"][own].rearrange("o b w v d -> w (o b) (v d)")).then_inc(cache_in, 16)
                for r, name in enumerate(("state_ssm_re", "state_ssm_im")):
                    src = a[name][own].rearrange("o b (i h) p -> (o b i) (h p)", h=2)
                    sp.dma_start(h0[:, r, :], src).then_inc(h0_in, 16)
                for name, dst in (("cache_k", out[6]), ("cache_v", out[7])):
                    sp.dma_start(dst[own, :, 0:WIN - T].rearrange("o b w v d -> (o b) (w v d)"),
                                 a[name][own, :, T:WIN].rearrange("o b w v d -> (o b) (w v d)")
                                 ).then_inc(cache_copied, 16)

            def skew(l):
                sp.wait_ge(zeros_set, 2)
                sp.wait_ge(*work.taken(l, "K3"))
                for s in range(T):
                    for h in range(2):
                        dst = Toep[s * GC:(s + 1) * GC, h::2, s * GC:P]
                        sp.dma_start(dst, Ksb[h * GC:(h + 1) * GC, :, 0:P - s * GC]).then_inc(skew_in, 16)

            def cached_values(l):
                sp.wait_ge(*work.ready(l, "y3"))
                sp.dma_start(vc, a["cache_v"][one_layer(l)].rearrange("o b w v d -> w (o b) (v d)"))\
                    .then_inc(vcache_in, 16)

            def first_units(l):
                for unit in UNITS[:RAW]:
                    load(l, unit)

            def rest_of_layer(l):
                for unit in UNITS[RAW:]:
                    load(l, unit)
                    if unit == "gate4":
                        cached_values(l)
                    if unit == "v":
                        caches(l)
                    if unit == "zs1":
                        skew(l)

            first_units(0)
            with sp.Fori(0, DEPTH - 1) as l:
                rest_of_layer(l)
                first_units(l + 1)
            rest_of_layer(DEPTH - 1)
            sp.wait_ge(cache_copied, DEPTH * 32)

        @block.tensor
        def _(pe):
            def mm(out_, lhsT, rhs, start, stop, free=False):
                return nc.tensor.matmul(out_, lhsT, rhs, start=start, stop=stop, skip_group_check=free)

            pe.wait_ge(const_in, 16)
            pe.wait_ge(silu_r, 1)
            b = work.bank("cT")
            for k in range(KT):
                ins = nc.tensor.transpose(b[:, k * CT:(k + 1) * CT], cexp[:, k * P:(k + 1) * P], ident[0:CT, 0:CT])
            ins.then_inc(work.filled("cT"), 1)
            b = work.bank("rowsT")
            pe.wait_ge(small_in, 16 * (7 * DEPTH + 1))
            pe.wait_ge(ldt_wide, 1)
            nc.tensor.transpose(b[:, 0:2 * ROWS_L + KT], rowsP, ident[0:2 * ROWS_L + KT, 0:2 * ROWS_L + KT])
            nc.tensor.transpose(b[:, P:P + 3 * W], rowsS, ident[0:3 * W, 0:3 * W]).then_inc(work.filled("rowsT"), 1)
            b = proj.bank("sinks")
            pe.wait_ge(sinks_in, 48)
            mm(b[:, 0:DEPTH * KV], sel, sinkc, True, True).then_inc(proj.filled("sinks"), 1)
            pe.wait_ge(bc_in, 16 * 12)
            for n in range(2):
                b = proj.bank(f"BT{n}")
                for c in range(8):
                    src = Braw[:, n * 8 + c:2048:GC]
                    ins = nc.tensor.transpose(b[:, c * 64:(c + 1) * 64], src, ident[0:64, 0:64])
                ins.then_inc(proj.filled(f"BT{n}"), 1)
            for n in range(4):
                pe.wait_ge(*work.room(0, f"CT{n}"))
                b = work.bank(f"CT{n}")
                for t in range(4):
                    ins = nc.tensor.transpose(b[:, t * P:(t + 1) * P],
                                              Craw[:, n, t].rearrange("p d q -> p (d q)"), ident)
                ins.then_inc(work.filled(f"CT{n}"), 1)
            pe.wait_ge(x_in, 32)
            for k in range(KT):
                pe.wait_ge(*work.room(0, f"xT{k}"))
                b = work.bank(f"xT{k}")
                for n, rows in enumerate((P, P, NS)):
                    ins = nc.tensor.transpose(b[:, n * P:n * P + rows], xin[0:rows, n, k * P:(k + 1) * P],
                                              ident[0:rows, 0:rows])
                ins.then_inc(work.filled(f"xT{k}"), 1)

            def sum_squares(l, job, layers):
                pe.wait_ge(*work.room(l, job))
                pe.wait_ge(sq_added, layers * KT)
                pe.wait_ge(mean_set, 3)
                mm(work.bank(job)[:, 0:TOK], mean[:, :], sqsum[:, :], True, True).then_inc(work.filled(job), 1)

            def modulation(l, kind, x):
                c = (ADA_SS if kind == "ss" else ADA_GATE)[x]
                pe.wait_ge(*work.room(l, f"am{c}"))
                b = work.bank(f"am{c}")
                for n in range(4):
                    unit = f"{kind}{4 * x + n}"
                    s = slot_of(unit)
                    pe.wait_ge(loaded[s], loads_at(l, unit))
                    for k in (2 * n, 2 * n + 1):
                        j = k % 4
                        ins = mm(b[j * AROW:(j + 1) * AROW, :], cT[:, k, :],
                                 raw[:, s, k % 2 * AC:(k % 2 + 1) * AC], k < 4, k >= 4, True)
                    ins.then_inc(used[s] if n < 3 else work.filled(f"am{c}"), 1)
                pe.wait_ge(*work.taken(l, f"am{c}"))
                pe.wait_ge(*work.room(l, f"at{c}"))
                for q in range(4):
                    ins = nc.tensor.transpose(work.bank(f"at{c}")[:, q * P:(q + 1) * P], arow[:, q * P:(q + 1) * P],
                                              ident)
                    if q == 0:
                        ins.then_inc(used[s], 1)
                ins.then_inc(work.filled(f"at{c}"), 1)

            def split_passes(out_, unit, k, cols, rhs_k, first, last, moving=None):
                s = SPLIT.index(unit) % HL
                hi, lo = w_hi[:, s, cols], w_lo[:, s, cols]
                mm(out_, hi, h_hi[:, rhs_k, :], first, False)
                mm(out_, hi, h_lo[:, rhs_k, :], False, False)
                return mm(out_, lo, h_hi[:, rhs_k, :], False, last)

            def project(l, job):
                s = slot_of(job)
                pe.wait_ge(used[s], uses_at(l, job))
                pe.wait_ge(*proj.room(l, job))
                for k in range(KT):
                    ins = split_passes(proj.bank(job)[:, 0:TOK], job, k, slice(k * P, (k + 1) * P), k,
                                       k == 0, k == KT - 1)
                ins.then_inc(proj.filled(job), 1)

            def project_two(l, jobs):
                for job in jobs:
                    pe.wait_ge(used[slot_of(job)], uses_at(l, job))
                    pe.wait_ge(*proj.room(l, job))
                for k in range(KT):
                    pe.wait_ge(h_ready, l * KT + k + 1)
                    for job in jobs:
                        ins = split_passes(proj.bank(job)[:, 0:TOK], job, k, slice(k * P, (k + 1) * P), k,
                                           k == 0, k == KT - 1)
                        if k == KT - 1:
                            ins.then_inc(proj.filled(job), 1)

            def rope(l, n):
                job = f"rope{n}"
                pe.wait_ge(*work.room(l, job))
                pe.wait_ge(*proj.taken(l, f"q{n}" if n < 4 else "k"))
                mm(work.bank(job)[:, 0:TOK], rot, qraw[:, n % 2, :], True, True).then_inc(work.filled(job), 1)

            def turn_B(l, n):
                job, r, q = f"WB{n}", n % 2, n // 2
                pe.wait_ge(*work.room(l, job))
                pe.wait_ge(wb_ready, l * 8 + n + 1)
                b = work.bank(job)
                for i in range(4):
                    ins = nc.tensor.transpose(b[:, i * P:(i + 1) * P], WBq[:, n % 2, i, :], ident)
                ins.then_inc(work.filled(job), 1)

            def values(l):
                pe.wait_ge(used[slot_of("v")], uses_at(l, "v"))
                pe.wait_ge(*work.room(l, "v"))
                b, s = work.bank("v"), SPLIT.index("v") % HL
                for n, t0 in enumerate((0, P, TOK - P)):
                    for k in range(KT):
                        o, cols, toks = b[:, n * P:(n + 1) * P], slice(k * P, (k + 1) * P), slice(t0, t0 + P)
                        mm(o, h_hi[:, k, toks], w_hi[:, s, cols], k == 0, False)
                        mm(o, h_lo[:, k, toks], w_hi[:, s, cols], False, False)
                        ins = mm(o, h_hi[:, k, toks], w_lo[:, s, cols], False, k == KT - 1)
                ins.then_inc(work.filled("v"), 1)

            with pe.Fori(0, DEPTH) as l:
                sum_squares(l, "rms", l + 1)
                pe.wait_ge(*work.taken(0, "cT"))
                for x in range(4):
                    modulation(l, "ss", x)

                project_two(l, ("u0", "u1"))
                for m in range(2, 4):
                    project(l, f"u{m}")
                for m in range(4):
                    project(l, f"q{m}")
                    if m:
                        rope(l, m - 1)
                    turn_B(l, 2 * m)
                    turn_B(l, 2 * m + 1)
                project(l, "k")
                rope(l, 3)
                values(l)
                rope(l, 4)

                pe.wait_ge(h0_in, l * 32 + 32)
                pe.wait_ge(*work.room(l, "h0"))
                for r in range(2):
                    ins = nc.tensor.transpose(work.bank("h0")[:, r * P:(r + 1) * P], h0[:, r, :], ident)
                ins.then_inc(work.filled("h0"), 1)
                pe.wait_ge(cache_in, l * 16 + 16)
                for n in range(2):
                    pe.wait_ge(*work.room(l, f"kcT{n}"))
                    for q in range(4):
                        ins = nc.tensor.transpose(work.bank(f"kcT{n}")[:, q * P:(q + 1) * P], kc[:, n * 4 + q, :], ident)
                    ins.then_inc(work.filled(f"kcT{n}"), 1)

                pe.wait_ge(u_back, (l + 1) * 16 * T)
                for n in range(8):
                    job, r, q = f"S{n}", n % 2, n // 2
                    pe.wait_ge(*work.room(l, job))
                    pe.wait_ge(*work.taken(l, f"WB{n}"))
                    for i in range(4):
                        g = 2 * (4 * q + i)
                        ins = mm(work.bank(job)[:, i * 2 * J:(i + 1) * 2 * J], WBt[:, 4 * q + i, r, :],
                                 U[:, g:g + 2, :], True, True)
                    ins.then_inc(work.filled(job), 1)

                pe.wait_ge(g_ready, l + 1)
                for n in range(4):
                    job = f"K{n}"
                    pe.wait_ge(*work.room(l, job))
                    for q in range(4):
                        i = 4 * n + q
                        for r in range(2):
                            ins = mm(work.bank(job)[0:2 * GC, q * P:(q + 1) * P],
                                     Bblk[:, r, i].rearrange("p h c -> p (h c)"),
                                     Gm[:, r, i, 0:T].rearrange("p t c -> p (t c)"), r == 0, r == 1)
                    ins.then_inc(work.filled(job), 1)

                pe.wait_ge(*work.room(l, "ktok"))
                pe.wait_ge(*work.taken(l, "rope4"))
                b = work.bank("ktok")
                nc.tensor.transpose(b[:, 0:P], kT[:, P:2 * P], ident)
                nc.tensor.transpose(b[0:NS, P:2 * P], kT[:, SEQ:TOK], ident).then_inc(work.filled("ktok"), 1)

                for m in range(4):
                    project(l, f"za{m}")

                pe.wait_ge(H_ready, (l + 1) * 2)
                pe.wait_ge(skew_in, (l + 1) * 2 * T * 16)
                for n in range(4):
                    job = f"y{n}"
                    pe.wait_ge(*work.room(l, job))
                    for q in range(4):
                        i = 4 * n + q
                        o = work.bank(job)[:, q * 2 * J:(q + 1) * 2 * J]
                        for r in range(2):
                            mm(o, Gm[:, r, i, 1:T + 1].rearrange("p t c -> p (t c)"),
                               Hblk[:, r, i].rearrange("p h j -> p (h j)"), r == 0 and q == 0, False, True)
                    for q in range(4):
                        i = 4 * n + q
                        o = work.bank(job)[:, q * 2 * J:(q + 1) * 2 * J]
                        for h in range(2):
                            for c in range(4):
                                rows = slice(c * 32, (c + 1) * 32)
                                ins = mm(o[rows, h * J:(h + 1) * J], Toep[:, 2 * i + h, rows], U[:, 2 * i + h, :],
                                         False, h == 1, True)
                    ins.then_inc(work.filled(job), 1)
                pe.wait_ge(*work.room(l, "state"))
                pe.wait_ge(fin_ready, l + 1)
                b = work.bank("state")
                for r in range(2):
                    nc.tensor.transpose(b[:, r * P:(r + 1) * P],
                                        fin[:, r, 1:1 + NB, :].rearrange("p b i -> p (b i)"), ident)
                for r in range(2):
                    ins = nc.tensor.transpose(b[0:NI, (2 + r) * P:(3 + r) * P], fin[:, r, 0, :], ident)
                ins.then_inc(work.filled("state"), 1)

                for kv in range(KV):
                    rows = slice(kv * HD, (kv + 1) * HD)
                    job = f"sc0{kv}"
                    pe.wait_ge(*work.room(l, job))
                    for i in range(NQ):
                        ins = mm(work.bank(job)[:, i * P:(i + 1) * P], qT[rows, i, 0:P], kT[rows, 0:P], True, True)
                    ins.then_inc(work.filled(job), 1)
                for kv in range(KV):
                    rows = slice(kv * HD, (kv + 1) * HD)
                    for n in range(2):
                        job = f"sc1{2 * kv + n}"
                        pe.wait_ge(*work.room(l, job))
                        for q in range(2):
                            ins = mm(work.bank(job)[:, q * 2 * P:(q + 1) * 2 * P], qT[rows, 2 * n + q, P:SEQ],
                                     kT[rows, 0:SEQ], True, True)
                        ins.then_inc(work.filled(job), 1)
                for kv in range(KV):
                    rows = slice(kv * HD, (kv + 1) * HD)
                    job = f"ss{kv}"
                    pe.wait_ge(*work.room(l, job))
                    pe.wait_ge(*work.taken(l, "kcT0"))
                    pe.wait_ge(*work.taken(l, "kcT1"))
                    for hb in range(2):
                        o = work.bank(job)[:, hb * (WIN + NS):(hb + 1) * (WIN + NS)]
                        mm(o[:, WIN:], qs[rows, hb * 4:hb * 4 + 4].rearrange("p b i t -> p (b i t)"),
                           kT[rows, SEQ:TOK], True, True, True)
                        for q in range(4):
                            ins = mm(o[q * 32:(q + 1) * 32, 0:WIN],
                                     qs[rows, hb * 4 + q].rearrange("p i t -> p (i t)"),
                                     kcT[rows, hb * 4 + q, :], True, True, True)
                    ins.then_inc(work.filled(job), 1)

                pe.wait_ge(*work.taken(l, "v"))
                for m in range(4):
                    project(l, f"zs{m}")

                for x in range(2):
                    modulation(l, "gate", x)

                pe.wait_ge(yglo, (l + 1) * MT)
                for m in range(4):
                    unit = f"glu{m // 2}"
                    pe.wait_ge(used[slot_of(unit)], uses_at(l, unit))
                    pe.wait_ge(*proj.room(l, f"glu{m}"))
                    for k in range(MT):
                        c0 = k * 2 * P + (m % 2) * P
                        ins = split_passes(proj.bank(f"glu{m}")[:, 0:TOK], unit, k, slice(c0, c0 + P), MT + k,
                                           k == 0, k == MT - 1)
                    ins.then_inc(proj.filled(f"glu{m}"), 1)

                pe.wait_ge(p_ready, l * 3 + 1)
                for n in range(6):
                    if n == 2:
                        pe.wait_ge(p_ready, l * 3 + 2)
                    job, kv = f"PT{n}", n % 2
                    pe.wait_ge(*work.room(l, job))
                    for i in range(NQ):
                        src = P0[:, kv, i, :] if n < 2 else P1[:, kv, i, (n // 2 - 1) * P:(n // 2) * P]
                        ins = nc.tensor.transpose(work.bank(job)[:, i * P:(i + 1) * P], src, ident)
                    ins.then_inc(work.filled(job), 1)
                for job, parts in (("pv0", ((0, 0),)), ("pv1", ((1, 0), (2, 1)))):
                    pe.wait_ge(*work.room(l, job))
                    for n, _ in parts:
                        for kv in range(KV):
                            pe.wait_ge(*work.taken(l, f"PT{2 * n + kv}"))
                    for kv in range(KV):
                        for x, (n, tile) in enumerate(parts):
                            ins = mm(work.bank(job)[kv * HD:(kv + 1) * HD, :], vtok[:, tile, kv * HD:(kv + 1) * HD],
                                     PT[:, n, kv, :], x == 0, x == len(parts) - 1)
                    ins.then_inc(work.filled(job), 1)
                pe.wait_ge(p_ready, l * 3 + 3)
                pe.wait_ge(*work.room(l, "PTc"))
                pe.wait_ge(*work.room(l, "PTn"))
                for kv in range(KV):
                    for hb in range(2):
                        x = kv * 2 + hb
                        ins = nc.tensor.transpose(work.bank("PTc")[:, x * P:(x + 1) * P], Ps[:, kv, hb, 0:WIN], ident)
                ins.then_inc(work.filled("PTc"), 1)
                for kv in range(KV):
                    for hb in range(2):
                        x = kv * 2 + hb
                        ins = nc.tensor.transpose(work.bank("PTn")[0:NS, x * P:(x + 1) * P], Ps[:, kv, hb, WIN:], ident)
                ins.then_inc(work.filled("PTn"), 1)
                pe.wait_ge(*work.room(l, "pvs"))
                pe.wait_ge(*work.taken(l, "PTc"))
                pe.wait_ge(*work.taken(l, "PTn"))
                pe.wait_ge(vcache_in, l * 16 + 16)
                for kv in range(KV):
                    cols = slice(kv * HD, (kv + 1) * HD)
                    for hb in range(2):
                        o = work.bank("pvs")[cols, hb * P:(hb + 1) * P]
                        for q in range(4):
                            mm(o[:, q * 32:(q + 1) * 32], vc[:, hb * 4 + q, cols],
                               PTc[:, kv, hb, q * 32:(q + 1) * 32], hb == 0 and q == 0, False, True)
                        ins = mm(o, vtok[0:NS, 2, cols], PTn[0:NS, kv, hb, :], False, True, True)
                ins.then_inc(work.filled("pvs"), 1)

                for m in range(8):
                    unit = f"out{m}"
                    pe.wait_ge(used[slot_of(unit)], uses_at(l, unit))
                    pe.wait_ge(*proj.room(l, unit))
                    for k in (4, 5, 6, 7, 0, 1, 2, 3):
                        if m == 0:
                            pe.wait_ge(mix_ready, l * 7 + (k - MT + 1 if k >= MT else 7))
                        ins = split_passes(proj.bank(unit)[:, 0:TOK], unit, k, slice(k * P, (k + 1) * P), k,
                                           k == 4, k == 3)
                    ins.then_inc(proj.filled(unit), 1)

            sum_squares(DEPTH, "rmsF", DEPTH + 1)
            pe.wait_ge(yn_ready, KT)
            for n in range(6):
                job, tile, half = f"yT{n}", n // 2, n % 2
                rows = P if tile < 2 else NS
                pe.wait_ge(*work.room(DEPTH, job))
                for q in range(4):
                    ins = nc.tensor.transpose(work.bank(job)[0:rows, q * P:(q + 1) * P],
                                              xT[:, half * 4 + q, tile * P:tile * P + rows], ident)
                ins.then_inc(work.filled(job), 1)

        @block.scalar
        def _(act):
            step = Steps(act, act_step)
            fn = nc.scalar.activation

            act.dma_start(crow[0:1, :], a["c_prompt"]).then_inc(cond_in, 16)
            act.dma_start(crow[1:CT, :], a["c_sample"]).then_inc(cond_in, 16)
            act.dma_start(const[:, :], a["constants"][:, 0:C_SEL]).then_inc(const_in, 16)
            xv = xin
            act.dma_start(xv[:, 0:2, :], a["x_prompt"][0].rearrange("(n p) d -> p n d", p=P)).then_inc(x_in, 16)
            act.dma_start(xv[0:NS, 2, :], a["x_sample"].rearrange("b t d -> (b t) d")).then_inc(x_in, 16)
            for l in range(DEPTH):
                r0 = l * ROWS_L
                for name, at, n in (("norm_g", S_G, KT), ("b_ada", S_BADA, 3 * KT), ("b_glu", S_BGLU, MT)):
                    act.dma_start(rowsP[r0 + at:r0 + at + n, :], a[name][l].rearrange("(r p) -> r p", p=P))\
                        .then_inc(small_in, 16)
                act.dma_start(rowsP[r0 + S_D:r0 + S_D + MT, :],
                              a["ssm_d"][l].rearrange("(r g) c -> r (g c)", r=MT)).then_inc(small_in, 16)
            act.dma_start(rowsP[2 * ROWS_L:2 * ROWS_L + KT, :], a["final_g"].rearrange("(r p) -> r p", p=P))\
                .then_inc(small_in, 16)
            for l in range(DEPTH):
                for n, name in enumerate(("ssm_a_re", "ssm_a_im")):
                    r0 = n * W + l * NI
                    act.dma_start(rowsS[r0:r0 + NI, :], a[name][l].rearrange("(i h) p -> i (h p)", h=2))\
                        .then_inc(small_in, 16)
                act.dma_start(ldt[l * NI:(l + 1) * NI, :], a["ssm_log_dt"][l].rearrange("(i h) -> i h", h=2))\
                    .then_inc(small_in, 16)
            act.dma_start(small[:, :, S_SINKP:S_SINKP + 8], a["attn_sinks"].unsqueeze(0).to_broadcast([P, DEPTH, 8]))\
                .then_inc(sinks_in, 16)
            act.dma_start(sel, a["constants"][0:NQ, C_SEL:C_END]).then_inc(sinks_in, 16)
            with nc.allow_non_contiguous_dma(reason="16 numbers"):
                act.dma_start(sinkc, a["attn_sinks"].rearrange("l (v i) -> i (l v)", i=NQ)).then_inc(sinks_in, 16)
            for l in range(DEPTH):
                for r, name in enumerate(("ssm_b_re", "ssm_b_im")):
                    r0 = (2 * l + r) * NI
                    act.dma_start(Braw[r0:r0 + NI, :], a[name][l].rearrange("(i h) p c -> i (h p c)", h=2))\
                        .then_inc(bc_in, 16)
                for r, name in enumerate(("ssm_c_re", "ssm_c_im")):
                    for d in range(2):
                        act.dma_start(Craw[:, 2 * l + r, :, d, :],
                                      a[name][l].rearrange("(t g) c p -> (g c) t p", t=4)).then_inc(bc_in, 16)

            act.wait_ge(cond_in, 32)
            fn(cexp, crow, ACT.Exp, scale=-1.0).then_inc(silu_c, 1)
            act.wait_ge(ssm_exp, 1)
            fn(zz[:, 3, :], rowsT[:, P + 2 * W:P + 3 * W], ACT.Exp).then_inc(ssm_val, 1)
            act.wait_ge(ssm_exp, 2)
            fn(zz[:, 6, :], zz[:, 4, :], ACT.Exp).then_inc(ssm_val, 1)
            act.wait_ge(ssm_exp, 3)
            fn(zz[:, 7, :], zz[:, 7, :], ACT.Sin).then_inc(ssm_val, 1)
            fn(zz[:, 8, :], zz[:, 8, :], ACT.Sin).then_inc(ssm_val, 1)
            for n in range(2):
                act.wait_ge(*proj.ready(0, f"BT{n}"))
                src = proj.bank(f"BT{n}")[:, :].rearrange("p (c w) -> p w c", c=8)
                dst = Bsb[:, :, :, :, n * 8:(n + 1) * 8].rearrange("p l r i c -> p (l r i) c")
                fn(dst, src, ACT.Copy).then_inc(proj.emptied(f"BT{n}"), 1)
            for n in range(4):
                l, r = n // 2, n % 2
                act.wait_ge(*work.ready(0, f"CT{n}"))
                for h in range(2):
                    rows = slice(h * NST, (h + 1) * NST)
                    src = work.bank(f"CT{n}")[rows, :].rearrange("p (i h c) -> p i h c", h=2, c=GC)[:, :, h, :]
                    ins = fn(Csb[rows, l, r], src, ACT.Copy, scale=(-1.0 if r else 1.0))
                    if h == 1:
                        ins.then_inc(work.emptied(f"CT{n}"), 1)
                    else:
                        step.add(ins)
            step.wait()

            for k in range(KT):
                act.wait_ge(*work.taken(0, f"xT{k}"))
                if k >= 2:
                    act.wait_ge(sq_added, k - 1)
                fn(sq[:, k % 2, :], xT[:, k, :], ACT.Square).then_inc(sq_done, 1)

            def hi_part(l, n):
                unit = SPLIT[n]
                act.wait_ge(loaded[slot_of(unit)], loads_at(l, unit))
                if n >= HL:
                    old = SPLIT[n - HL]
                    if old == "v":
                        act.wait_ge(*work.ready(l, "v"))
                    elif old.startswith("glu"):
                        act.wait_ge(*proj.ready(l, f"glu{2 * int(old[3:]) + 1}"))
                    else:
                        act.wait_ge(*proj.ready(l, old))
                fn(w_hi[:, n % HL, :], raw[:, slot_of(unit), :], ACT.Copy).then_inc(hi_done, 1)

            def root(l, job):
                act.wait_ge(*work.ready(l, job))
                fn(rstd[:, 1, :], work.bank(job)[:, 0:TOK], ACT.Identity, bias=epsb[:, 0:1])\
                    .then_inc(work.emptied(job), 1)
                act.wait_ge(*work.taken(l, job))
                step.add(fn(rstd[:, 0, :], rstd[:, 1, :], ACT.Ln))
                step.wait()
                fn(rstd[:, 0, :], rstd[:, 0, :], ACT.Exp, scale=-0.5).then_inc(rstd_raw, 1)

            act.wait_ge(mean_set, 3)
            def modulation_rows(l, c):
                act.wait_ge(*work.ready(l, f"am{c}"))
                order = ADA_SS + ADA_GATE
                if c != order[0]:
                    act.wait_ge(*work.ready(l, f"at{order[order.index(c) - 1]}"))
                fn(arow, work.bank(f"am{c}")[:, :], ACT.Copy).then_inc(work.emptied(f"am{c}"), 1)

            with act.Fori(0, DEPTH) as l:
                step.restart()
                root(l, "rms")
                modulation_rows(l, ADA_SS[0])
                modulation_rows(l, ADA_SS[1])
                for k in range(KT):
                    if k == 4:
                        modulation_rows(l, ADA_SS[2])
                        modulation_rows(l, ADA_SS[3])
                        hi_part(l, 0)
                        hi_part(l, 1)
                    act.wait_ge(mod_ready, l * 6 + (2 if k < 4 else 4))
                    act.wait_ge(norm_done, l * KT + k + 1)
                    if k >= 2:
                        act.wait_ge(h_ready, l * KT + k - 1)
                    fn(hf[:, k % 2, 0:SEQ], xn[:, k, 0:SEQ], ACT.Identity,
                       scale=mod[:, KT + k, 0:1], bias=mod[:, k, 0:1]).then_inc(hp_done, 1)
                    act.wait_ge(hs_done, l * KT + k + 1)
                    act.wait_ge(hp_done, l * KT + k + 1)
                    fn(h_hi[:, k, :], hf[:, k % 2, :], ACT.Copy).then_inc(hhi_done, 1)

                for m in range(4):
                    act.wait_ge(*proj.ready(l, f"u{m}"))
                    fn(u_sb[:, m], proj.bank(f"u{m}")[:, 0:TOK].rearrange("p (j t) -> p t j", t=T), ACT.Copy)\
                        .then_inc(proj.emptied(f"u{m}"), 1)
                    hi_part(l, m + 2)
                    act.wait_ge(*proj.taken(l, f"u{m}"))
                    act.dma_start(u_dram[m * 8:(m + 1) * 8].rearrange("g c t j -> (g c) (t j)"),
                                  u_sb[:, m].rearrange("p t j -> p (t j)")).then_inc(u_out, 16)

                def raw_rows(n, job):
                    act.wait_ge(*proj.ready(l, job))
                    if n >= 2:
                        act.wait_ge(*work.taken(l, f"rope{n - 2}"))
                    fn(qraw[:, n % 2, :], proj.bank(job)[:, 0:TOK], ACT.Copy).then_inc(proj.emptied(job), 1)

                def turned_B(n):
                    act.wait_ge(*work.ready(l, f"WB{n}"))
                    src = work.bank(f"WB{n}")[:, :].rearrange("p (i q) -> p i q", i=4)
                    fn(WBt[:, 4 * (n // 2):4 * (n // 2) + 4, n % 2, :], src, ACT.Copy)\
                        .then_inc(work.emptied(f"WB{n}"), 1)

                for m in range(4):
                    raw_rows(m, f"q{m}")
                    hi_part(l, 6 + m)
                    turned_B(2 * m)
                    turned_B(2 * m + 1)
                    if m == 0:
                        act.wait_ge(u_out, (l + 1) * 64)
                        for t in range(T):
                            act.dma_start(U[t * GC:(t + 1) * GC], u_dram[:, :, t, :].rearrange("g c j -> c g j"))\
                                .then_inc(u_back, 16)
                raw_rows(4, "k")
                hi_part(l, 10)

                act.wait_ge(*work.ready(l, "v"))
                step.add(fn(vtok[:, 0:2, :], work.bank("v")[:, 0:2 * P].rearrange("p (n q) -> p n q", n=2), ACT.Copy))
                fn(vtok[0:NS, 2, :], work.bank("v")[P - NS:P, 2 * P:3 * P], ACT.Copy).then_inc(work.emptied("v"), 1)
                hi_part(l, 11)
                for n in range(2):
                    act.wait_ge(*work.ready(l, f"kcT{n}"))
                    fn(kcT[:, 4 * n:4 * n + 4, :], work.bank(f"kcT{n}")[:, :].rearrange("p (b w) -> p b w", b=4),
                       ACT.Copy).then_inc(work.emptied(f"kcT{n}"), 1)
                for n in range(8):
                    job, r, q = f"S{n}", n % 2, n // 2
                    act.wait_ge(*work.ready(l, job))
                    for h in range(2):
                        rows = slice(h * NST, (h + 1) * NST)
                        src = work.bank(job)[rows, 0:8 * J].rearrange("p (i h j) -> p i h j", i=4, h=2)[:, :, h, :]
                        ins = fn(Ssb[rows, r, 4 * q:4 * q + 4, :], src, ACT.Copy)
                        if h == 1:
                            ins.then_inc(work.emptied(job), 1)
                        else:
                            step.add(ins)
                for n in range(4):
                    act.wait_ge(*work.ready(l, f"K{n}"))
                    fn(Ksb[0:2 * GC, 4 * n:4 * n + 4, :],
                       work.bank(f"K{n}")[0:2 * GC, :].rearrange("p (i q) -> p i q", i=4), ACT.Copy)\
                        .then_inc(work.emptied(f"K{n}"), 1)
                act.wait_ge(*work.ready(l, "ktok"))
                step.add(fn(ktok[:, 0, :], work.bank("ktok")[:, 0:P], ACT.Copy))
                fn(ktok[0:NS, 1, :], work.bank("ktok")[0:NS, P:2 * P], ACT.Copy).then_inc(work.emptied("ktok"), 1)
                step.wait()
                act.wait_ge(*work.taken(l, "ktok"))
                act.wait_ge(*work.taken(l, "v"))
                own = bass.ds(l, 1)
                for prompt, sample, src, new in ((out[2], out[6], ktok, 1), (out[3], out[7], vtok, 2)):
                    act.dma_start(prompt[own].rearrange("o b w v d -> (o b w) (v d)"), src[:, new - 1, :])\
                        .then_inc(kv_stored, 16)
                    act.dma_start(sample[own, :, WIN - T:WIN].rearrange("o b t v d -> (o b) t (v d)"),
                                  src[0:NS, new, :]).then_inc(kv_stored, 16)

                def gate(n, job):
                    act.wait_ge(*proj.ready(l, job))
                    if n >= 2:
                        before = f"za{n - 2}" if n - 2 < 4 else f"zs{n - 6}"
                        act.wait_ge(*proj.taken(l, before))
                    fn(ez[:, n % 2, :], proj.bank(job)[:, 0:TOK], ACT.Tanh, scale=0.5).then_inc(gate_tanh, 1)

                for m in range(4):
                    gate(m, f"za{m}")
                    hi_part(l, 12 + m)
                for n in range(4):
                    act.wait_ge(*work.ready(l, f"y{n}"))
                    fn(Ysb[:, 8 * n:8 * n + 8, :], work.bank(f"y{n}")[:, 0:8 * J].rearrange("p (g j) -> p g j", g=8),
                       ACT.Copy).then_inc(work.emptied(f"y{n}"), 1)
                for n in range(4):
                    act.wait_ge(*work.taken(l, f"y{n}"))
                for t in range(T):
                    act.dma_start(y_dram[:, :, t, :].rearrange("g c j -> c g j"), Ysb[t * GC:(t + 1) * GC])\
                        .then_inc(y_out, 16)
                act.wait_ge(*work.ready(l, "state"))
                step.add(fn(stage[:, 0:2, :], work.bank("state")[:, 0:2 * P].rearrange("p (r q) -> p r q", r=2), ACT.Copy))
                fn(stage[0:NI, 2:4, :], work.bank("state")[0:NI, 2 * P:4 * P].rearrange("p (r q) -> p r q", r=2),
                   ACT.Copy).then_inc(work.emptied("state"), 1)
                gate(4, "zs0")
                hi_part(l, 16)
                step.wait()
                act.wait_ge(*work.taken(l, "state"))
                for r in range(2):
                    act.dma_start(out[8 + r][own].rearrange("o b (i h) p -> (o b i) (h p)", h=2), stage[:, r, :])\
                        .then_inc(state_stored, 16)
                    act.dma_start(out[4 + r][own].rearrange("o b (i h) p -> (o b i) (h p)", h=2), stage[0:NI, 2 + r, :])\
                        .then_inc(state_stored, 16)
                gate(5, "zs1")
                hi_part(l, 17)
                act.wait_ge(y_out, (l + 1) * 128)
                act.wait_ge(skew_in, (l + 1) * 2 * T * 16)
                for m in range(MT):
                    act.dma_start(ycp[:, m, :], y_dram[m * 8:(m + 1) * 8].rearrange("g c t j -> (g c) (t j)"))\
                        .then_inc(y_back, 16)
                gate(6, "zs2")
                hi_part(l, 18)
                gate(7, "zs3")
                hi_part(l, 19)

                act.wait_ge(state_stored, (l + 1) * 64)
                modulation_rows(l, 4)
                modulation_rows(l, 5)

                for pair in ((0, 1), (2, 3)):
                    for m in pair:
                        act.wait_ge(y1_ready, l * MT + m + 1)
                        if m >= 2:
                            act.wait_ge(yg_ready, l * MT + m - 1)
                        fn(ez[:, m % 2, :], ycp[:, m, :], ACT.Square).then_inc(y_sq, 1)
                    for m in pair:
                        act.wait_ge(y_arg, l * MT + m + 1)
                        fn(ez[:, m % 2, :], ez[:, m % 2, :], ACT.Tanh, scale=GELU_B).then_inc(y_tanh, 1)
                    for m in pair:
                        act.wait_ge(yg_ready, l * MT + m + 1)
                        fn(h_hi[:, MT + m, :], yg[:, m, :], ACT.Copy, scale=0.5).then_inc(yghi, 1)

                def exponentials(g):
                    buf, n = ((P0, NQ), (P1, NQ), (Ps, 2))[g]
                    act.wait_ge(max_ready, l * 3 + g + 1)
                    for v in range(KV):
                        for i in range(n):
                            x = v * n + i
                            fn(buf[:, v, i, :], buf[:, v, i, :], ACT.Exp, scale=SCALE, bias=sm[:, g, 1, x:x + 1],
                               accum_out=sm[:, g, 2, x:x + 1])
                    fn(sm[:, g, 3, 0:KV * n], sm[:, g, 3, 0:KV * n], ACT.Exp).then_inc(p_exp, 1)

                exponentials(0)
                exponentials(1)
                for pair in ((0, 1), (2, 3)):
                    for m in pair:
                        act.wait_ge(*proj.ready(l, f"glu{m}"))
                        if m < 2:
                            act.wait_ge(yg_ready, (l + 1) * MT)
                        else:
                            act.wait_ge(gated, l * MT + m - 1)
                        fn(ez[:, m % 2, :], proj.bank(f"glu{m}")[:, 0:TOK], ACT.Tanh, scale=0.5,
                           bias=hbglu[:, m:m + 1]).then_inc(proj.emptied(f"glu{m}"), 1)
                    hi_part(l, 20 + pair[0] // 2)
                exponentials(2)

                for n in range(6):
                    act.wait_ge(*work.ready(l, f"PT{n}"))
                    fn(PT[:, n // 2, n % 2, :], work.bank(f"PT{n}")[:, :], ACT.Copy)\
                        .then_inc(work.emptied(f"PT{n}"), 1)
                for m in range(MT):
                    act.wait_ge(gated, l * MT + m + 1)
                    fn(h_hi[:, MT + m, :], gs[:, m, :], ACT.Copy, scale=0.125).then_inc(mixhi, 1)
                act.wait_ge(*work.ready(l, "PTc"))
                fn(PTc, work.bank("PTc")[:, :].rearrange("p (v b q) -> p v b q", v=KV, b=2), ACT.Copy)\
                    .then_inc(work.emptied("PTc"), 1)
                act.wait_ge(*work.ready(l, "PTn"))
                fn(PTn[0:NS], work.bank("PTn")[0:NS, :].rearrange("p (v b q) -> p v b q", v=KV, b=2), ACT.Copy)\
                    .then_inc(work.emptied("PTn"), 1)
                for job, toks in (("pv0", slice(0, P)), ("pv1", slice(P, SEQ)), ("pvs", slice(SEQ, TOK))):
                    act.wait_ge(*work.taken(l, job))
                    fn(h_hi[:, 0:MT, toks], ga[:, :, toks], ACT.Copy, scale=0.5).then_inc(mixhi, 1)

                for m in range(8):
                    act.wait_ge(x_ready, l * KT + m + 1)
                    if m >= 2:
                        act.wait_ge(sq_added, (l + 1) * KT + m - 1)
                    fn(sq[:, m % 2, :], xT[:, m, :], ACT.Square).then_inc(sq_done, 1)
                    if m < 6:
                        hi_part(l, 22 + m)
                act.wait_ge(kv_stored, (l + 1) * 64)

            step.restart()
            root(DEPTH, "rmsF")
            ybuf = xin
            for n in range(6):
                job, tile, half = f"yT{n}", n // 2, n % 2
                rows = P if tile < 2 else NS
                act.wait_ge(*work.ready(DEPTH, job))
                fn(ybuf[0:rows, tile, half * 512:(half + 1) * 512], work.bank(job)[0:rows, :], ACT.Copy)\
                    .then_inc(work.emptied(job), 1)
            for n in range(6):
                act.wait_ge(*work.taken(DEPTH, f"yT{n}"))
            act.dma_start(out[0][0].rearrange("(n p) d -> p n d", p=P), ybuf[:, 0:2, :]).then_inc(y_stored, 16)
            act.dma_start(out[1].rearrange("b t d -> (b t) d"), ybuf[0:NS, 2, :]).then_inc(y_stored, 16)
            act.wait_ge(y_stored, 32)

        @block.vector
        def _(dve):
            step = Steps(dve, dve_step)
            v = nc.vector
            tt, ts, stt, cp = v.tensor_tensor, v.tensor_scalar, v.scalar_tensor_tensor, v.tensor_copy

            def own(ins):
                step.add(ins)
                step.wait()

            v.memset(mean[:, :], 1.0 / D).then_inc(mean_set, 1)
            v.memset(epsb[:, :], EPS).then_inc(mean_set, 1)
            v.memset(cT[:, :, CT:], 0.0).then_inc(mean_set, 1)
            step.add(v.memset(Apow[:, :, 0, :, 0:1], 1.0))
            step.add(v.memset(Apow[:, :, 1, :, 0:1], 0.0))
            dve.wait_ge(silu_c, 1)
            own(ts(cexp, cexp, 1.0, None, ALU.add))
            own(v.reciprocal(cexp, cexp))
            tt(cexp, crow, cexp, ALU.mult).then_inc(silu_r, 1)
            dve.wait_ge(small_in, 16 * (7 * DEPTH + 1))
            cp(rowsS[2 * W:3 * W, :].rearrange("p (h q) -> p h q", h=2),
               ldt.unsqueeze(2).to_broadcast([W, 2, NST])).then_inc(ldt_wide, 1)
            dve.wait_ge(*work.ready(0, "cT"))
            cp(cT[:, :, 0:CT], work.bank("cT")[:, 0:KT * CT].rearrange("p (k c) -> p k c", c=CT))\
                .then_inc(work.emptied("cT"), 1)
            dve.wait_ge(*work.ready(0, "rowsT"))
            step.add(cp(rowsT[:, 0:2 * ROWS_L + KT], work.bank("rowsT")[:, 0:2 * ROWS_L + KT]))
            cp(rowsT[:, P:P + 3 * W], work.bank("rowsT")[:, P:P + 3 * W]).then_inc(work.emptied("rowsT"), 1)
            step.wait()
            dve.wait_ge(*work.taken(0, "rowsT"))
            step.add(cp(small[:, :, 0:ROWS_L], rowsT[:, 0:2 * ROWS_L].rearrange("p (l r) -> p l r", l=DEPTH)))
            step.add(cp(fing[:, :], rowsT[:, 2 * ROWS_L:2 * ROWS_L + KT]))
            dve.wait_ge(*proj.ready(0, "sinks"))
            cp(small[:, :, S_SINKS:S_SINKS + KV],
               proj.bank("sinks")[:, 0:DEPTH * KV].rearrange("p (l s) -> p l s", l=DEPTH))\
                .then_inc(proj.emptied("sinks"), 1)

            a_re, a_im = rowsT[:, P:P + W], rowsT[:, P + W:P + 2 * W]
            dt_, ard, th, mag, rs, rc = (zz[:, n, :] for n in (3, 4, 5, 6, 7, 8))
            k1, k2, t1, t2, den, nr = (zz[:, n, :] for n in (9, 10, 11, 12, 13, 14))
            dve.wait_ge(*work.taken(0, "rowsT"))
            step.wait()
            cp(zz[:, 0, :], a_re).then_inc(ssm_exp, 1)
            dve.wait_ge(ssm_val, 1)
            own(tt(th, a_im, dt_, ALU.mult))
            tt(ard, a_re, dt_, ALU.mult).then_inc(ssm_exp, 1)
            own(ts(k1, th, 1.0 / TWO_PI, ROUND, ALU.mult, ALU.add))
            own(ts(k1, k1, -ROUND, None, ALU.add))
            own(ts(k2, th, 1.0 / TWO_PI, 0.25, ALU.mult, ALU.add))
            own(ts(k2, k2, ROUND, None, ALU.add))
            own(ts(k2, k2, -ROUND, None, ALU.add))
            for r, k in ((rs, k1), (rc, k2)):
                own(stt(r, k, -PI_1, th, ALU.mult, ALU.add))
                own(stt(r, k, -PI_2, r, ALU.mult, ALU.add))
                own(stt(r, k, -PI_3, r, ALU.mult, ALU.add))
            own(ts(rs, rs, PI_SAFE, -PI_SAFE, ALU.min, ALU.max))
            own(ts(rc, rc, TWO_PI / 4, PI_SAFE, ALU.add, ALU.min))
            ts(rc, rc, -PI_SAFE, None, ALU.max).then_inc(ssm_exp, 1)
            own(tt(t1, a_re, a_re, ALU.mult))
            own(tt(t2, a_im, a_im, ALU.mult))
            own(tt(den, t1, t2, ALU.add))
            own(v.reciprocal(den, den))
            dve.wait_ge(ssm_val, 4)

            def power(r, n0, n1):
                return Apow[:, :, r, :, n0:n1]

            def flat(x):
                return x.rearrange("p (l i) -> p l i", l=DEPTH).unsqueeze(3)

            ar, ai = power(0, 1, 2), power(1, 1, 2)
            own(tt(ar, flat(mag), flat(rc), ALU.mult))
            own(tt(ai, flat(mag), flat(rs), ALU.mult))
            own(ts(flat(nr), ar, -1.0, None, ALU.add))
            own(tt(t1, nr, a_re, ALU.mult))
            own(tt(flat(t2), ai, flat(a_im), ALU.mult))
            own(tt(t1, t1, t2, ALU.add))
            own(tt(coef[:, :, 0, :].unsqueeze(3), flat(t1), flat(den), ALU.mult))
            own(tt(flat(t1), ai, flat(a_re), ALU.mult))
            own(tt(t2, nr, a_im, ALU.mult))
            own(tt(t1, t1, t2, ALU.subtract))
            own(tt(coef[:, :, 1, :].unsqueeze(3), flat(t1), flat(den), ALU.mult))
            for n in (1, 2, 4):
                q = [zz[:, 3 + 4 * x:3 + 4 * x + n, :].rearrange("p n w -> p (n w)").rearrange(
                    "p (l i n) -> p l i n", l=DEPTH, i=NI) for x in range(2)]
                base = [power(r, n, n + 1).to_broadcast([P, DEPTH, NI, n]) for r in range(2)]
                low = [power(r, 1, n + 1) for r in range(2)]
                for r in range(2):
                    step.add(tt(q[0], low[0], base[r], ALU.mult))
                    own(tt(q[1], low[1], base[1 - r], ALU.mult))
                    own(tt(power(r, n + 1, 2 * n + 1), q[0], q[1], ALU.add if r else ALU.subtract))
            sv = small[:, :, :]
            A8 = [power(r, T, T + 1).rearrange("p l i o -> p l (i o)") for r in range(2)]
            step.add(cp(sv[:, :, S_A8R:S_A8R + NI], A8[0]))
            step.add(ts(sv[:, :, S_A8I:S_A8I + NI], A8[1], -1.0, None, ALU.mult))
            step.add(cp(sv[:, :, S_A8I + NI:S_A8I + 2 * NI], A8[1]))
            q = [x.rearrange("p (l i) -> p l i", l=DEPTH) for x in (t1, t2)]
            step.add(tt(q[0], A8[0], A8[0], ALU.mult))
            own(tt(q[1], A8[1], A8[1], ALU.mult))
            own(tt(sv[:, :, S_A16R:S_A16R + NI], q[0], q[1], ALU.subtract))
            own(tt(q[0], A8[0], A8[1], ALU.mult))
            step.add(ts(sv[:, :, S_A16I:S_A16I + NI], q[0], -2.0, None, ALU.mult))
            step.add(ts(sv[:, :, S_A16I + NI:S_A16I + 2 * NI], q[0], 2.0, None, ALU.mult))
            step.wait()
            cp(zz[:, 0, 0:1], zz[:, 0, 1:2]).then_inc(ssm_ready, 1)

            def add_square(n, done):
                dve.wait_ge(sq_done, done)
                if n:
                    dve.wait_ge(sq_added, done - 1)
                    tt(sqsum[:, :], sqsum[:, :], sq[:, n % 2, :], ALU.add).then_inc(sq_added, 1)
                else:
                    cp(sqsum[:, :], sq[:, 0, :]).then_inc(sq_added, 1)

            for k in range(KT):
                dve.wait_ge(*work.ready(0, f"xT{k}"))
                cp(xT[:, k, :], work.bank(f"xT{k}")[:, 0:TOK]).then_inc(work.emptied(f"xT{k}"), 1)
                if k:
                    add_square(k - 1, k)
            add_square(KT - 1, KT)

            def newton(n):
                dve.wait_ge(rstd_raw, n)
                own(tt(sqsum[:, :], rstd[:, 0, :], rstd[:, 0, :], ALU.mult))
                own(tt(sqsum[:, :], sqsum[:, :], rstd[:, 1, :], ALU.mult))
                own(ts(sqsum[:, :], sqsum[:, :], -0.5, 1.5, ALU.mult, ALU.add))
                own(tt(rstd[:, 0, :], rstd[:, 0, :], sqsum[:, :], ALU.mult))

            def lo_part(l, n):
                unit = SPLIT[n]
                dve.wait_ge(hi_done, l * len(SPLIT) + n + 1)
                tt(w_lo[:, n % HL, :], raw[:, slot_of(unit), :], w_hi[:, n % HL, :].bitcast(F32), ALU.subtract)\
                    .then_inc(used[slot_of(unit)], 1)

            def samples(ap):
                return ap[..., SEQ:TOK].rearrange("p (b t) -> p b t", b=NB)

            def per_sample(m):
                return mod[:, m, 1:CT].unsqueeze(2).to_broadcast([P, NB, T])

            def modulation_of(l, x):
                c = (ADA_SS + ADA_GATE)[x]
                dst = mod[:, 4 * c:4 * c + 4, :]
                dve.wait_ge(*work.ready(l, f"at{c}"))
                src = work.bank(f"at{c}")[:, :].rearrange("p (q j c) -> p q c j", j=4, c=AROW)[:, :, 0:CT, :]
                v.tensor_reduce(dst, src, AX.X, ALU.add).then_inc(work.emptied(f"at{c}"), 1)
                dve.wait_ge(*work.taken(l, f"at{c}"))
                bias = cur[:, S_BADA + 4 * c:S_BADA + 4 * c + 4].unsqueeze(2).to_broadcast([P, 4, CT])
                if c in (2, 3):
                    own(tt(dst, dst, bias, ALU.add))
                    g = cur[:, S_G + 4 * (c - 2):S_G + 4 * (c - 1)].unsqueeze(2).to_broadcast([P, 4, CT])
                    stt(dst, dst, 1.0, g, ALU.add, ALU.mult).then_inc(mod_ready, 1)
                else:
                    tt(dst, dst, bias, ALU.add).then_inc(mod_ready, 1)

            with dve.Fori(0, DEPTH) as l:
                step.restart()
                own(cp(cur[:, :], small[:, bass.ds(l, 1), :].rearrange("p o s -> p (o s)")))
                step.add(ts(hbglu[:, :], cur[:, S_BGLU:S_BGLU + MT], 0.5, None, ALU.mult))
                newton(l + 1)
                step.wait()
                for k in range(KT):
                    tt(xn[:, k, :], xT[:, k, :], rstd[:, 0, :], ALU.mult).then_inc(norm_done, 1)
                modulation_of(l, 0)
                modulation_of(l, 1)
                for k in range(KT):
                    if k == 4:
                        modulation_of(l, 2)
                        modulation_of(l, 3)
                        lo_part(l, 0)
                        lo_part(l, 1)
                    dve.wait_ge(mod_ready, l * 6 + (2 if k < 4 else 4))
                    dve.wait_ge(norm_done, l * KT + k + 1)
                    if k >= 2:
                        dve.wait_ge(h_ready, l * KT + k - 1)
                    own(tt(samples(hf[:, k % 2, :]), samples(xn[:, k, :]), per_sample(KT + k), ALU.mult))
                    tt(samples(hf[:, k % 2, :]), samples(hf[:, k % 2, :]), per_sample(k), ALU.add)\
                        .then_inc(hs_done, 1)
                    dve.wait_ge(hhi_done, l * KT + k + 1)
                    tt(h_lo[:, k, :], hf[:, k % 2, :], h_hi[:, k, :].bitcast(F32), ALU.subtract).then_inc(h_ready, 1)
                for m in range(4):
                    lo_part(l, m + 2)

                def rope(n):
                    job = f"rope{n}"
                    if n:
                        dve.wait_ge(*work.taken(l, f"rope{n - 1}"))
                    dve.wait_ge(*proj.taken(l, f"q{n}" if n < 4 else "k"))
                    step.add(tt(rt[:, 0, :], qraw[:, n % 2, :], cos, ALU.mult))
                    dve.wait_ge(*work.ready(l, job))
                    own(tt(rt[:, 1, :], work.bank(job)[:, 0:TOK], sin, ALU.mult))
                    if n < 4:
                        step.add(tt(qT[:, n, :], rt[:, 0, 0:SEQ], rt[:, 1, 0:SEQ], ALU.add))
                        tt(qs[:, :, n, :], samples(rt[:, 0, :]), samples(rt[:, 1, :]), ALU.add)\
                            .then_inc(work.emptied(job), 1)
                    else:
                        tt(kT[:, :], rt[:, 0, :], rt[:, 1, :], ALU.add).then_inc(work.emptied(job), 1)

                lo_part(l, 6)
                for m in range(3):
                    lo_part(l, 7 + m)
                    rope(m)
                lo_part(l, 10)
                rope(3)
                lo_part(l, 11)
                rope(4)

                dve.wait_ge(*work.ready(l, "h0"))
                cp(Hst[:, :, :, JP:J], work.bank("h0")[:, 0:2 * P].rearrange("p (r b i) -> p r i b", r=2, b=NB))\
                    .then_inc(work.emptied("h0"), 1)
                step.add(v.memset(Hst[:, :, :, 0:1], 0.0))
                for h in range(2):
                    step.add(v.memset(Hblk[h * NST:(h + 1) * NST, :, :, 1 - h, :], 0.0))
                dve.wait_ge(*work.taken(l, "h0"))
                dve.wait_ge(*work.taken(l, "S7"))
                step.wait()

                def wide_of(s0, n, shape):
                    re = cur[:, s0:s0 + NI].unsqueeze(1).unsqueeze(3).to_broadcast(shape)
                    im = cur[:, s0 + NI:s0 + 3 * NI].rearrange("p (r i) -> p r i", r=2).unsqueeze(3)\
                        .to_broadcast(shape)
                    return re, im

                half = [P, 2, NI, JP // 2]
                a8, a8i = wide_of(S_A8R, JP // 2, half)
                even, odd = Ssb[:, :, :, 0:JP:2], Ssb[:, :, :, 1:JP:2]
                step.add(tt(wide, even, a8, ALU.mult))
                own(tt(prod, Ssb[:, ::-1, :, 0:JP:2], a8i, ALU.mult))
                own(tt(wide, wide, odd, ALU.add))
                own(tt(wide, wide, prod, ALU.add))

                def silu(n, job, dst):
                    dve.wait_ge(gate_tanh, l * 8 + n + 1)
                    stt(dst, ez[:, n % 2, :], 1.0, proj.bank(job)[:, 0:TOK], ALU.add, ALU.mult).then_inc(proj.emptied(job), 1)

                one = [P, 2, NI]
                a16 = cur[:, S_A16R:S_A16R + NI].unsqueeze(1).to_broadcast(one)
                a16i = cur[:, S_A16I:S_A16I + 2 * NI].rearrange("p (r i) -> p r i", r=2)
                own(cp(Hst[:, :, :, 2], wide[:, :, :, 0]))
                for k in range(1, JP // 2):
                    H = Hst[:, :, :, 2 * k]
                    last = k == JP // 2 - 1
                    step.add(tt(rec[:, 0], H, a16, ALU.mult))
                    step.add(tt(rec[:, 1], Hst[:, ::-1, :, 2 * k], a16i, ALU.mult))
                    step.wait()
                    own(tt(rec[:, 0], rec[:, 0], wide[:, :, :, k], ALU.add))
                    own(tt(fin[:, :, 0, :] if last else Hst[:, :, :, 2 * k + 2], rec[:, 0], rec[:, 1], ALU.add))
                    if k in (4, 8, 12):
                        silu(k // 4 - 1, f"za{k // 4 - 1}", ga[:, k // 4 - 1, :])
                        lo_part(l, 11 + k // 4)
                step.add(tt(Hst[:, :, :, 1:JP:2], Hst[:, :, :, 0:JP:2], a8, ALU.mult))
                own(tt(prod, Hst[:, ::-1, :, 0:JP:2], a8i, ALU.mult))
                own(tt(Hst[:, :, :, 1:JP:2], Hst[:, :, :, 1:JP:2], even, ALU.add))
                own(tt(Hst[:, :, :, 1:JP:2], Hst[:, :, :, 1:JP:2], prod, ALU.add))
                b8, b8i = wide_of(S_A8R, NB, [P, 2, NI, NB])
                part = [x[:, :, :, 0:NB] for x in (wide, prod)]
                step.add(tt(part[0], Hst[:, :, :, JP:J], b8, ALU.mult))
                own(tt(part[1], Hst[:, ::-1, :, JP:J], b8i, ALU.mult))
                own(tt(part[0], part[0], Ssb[:, :, :, JP:J], ALU.add))
                tt(fin[:, :, 1:1 + NB, :].rearrange("p r b i -> p r i b"), part[0], part[1], ALU.add)\
                    .then_inc(fin_ready, 1)
                for h in range(2):
                    rows = slice(h * NST, (h + 1) * NST)
                    cp(Hblk[rows, :, :, h, :], Hst[rows]).then_inc(H_ready, 1)
                silu(3, "za3", ga[:, 3, :])
                lo_part(l, 15)

                for kv in range(KV):
                    job = f"sc0{kv}"
                    dve.wait_ge(*work.ready(l, job))
                    tt(P0[:, kv], work.bank(job)[:, :].rearrange("p (i k) -> p i k", i=NQ),
                       const[:, C_MP + P:C_MP + 2 * P].unsqueeze(1).to_broadcast([P, NQ, P]), ALU.add)\
                        .then_inc(work.emptied(job), 1)
                for n in range(4):
                    job = f"sc1{n}"
                    dve.wait_ge(*work.ready(l, job))
                    tt(P1[:, n // 2, 2 * (n % 2):2 * (n % 2) + 2], work.bank(job)[:, :].rearrange("p (i k) -> p i k", i=2),
                       const[:, C_MP:C_MP + 2 * P].unsqueeze(1).to_broadcast([P, 2, 2 * P]), ALU.add)\
                        .then_inc(work.emptied(job), 1)
                for kv in range(KV):
                    job = f"ss{kv}"
                    dve.wait_ge(*work.ready(l, job))
                    tt(Ps[:, kv], work.bank(job)[:, 0:2 * (WIN + NS)].rearrange("p (b k) -> p b k", b=2),
                       const[:, C_MS:C_MS + 2 * (WIN + NS)].rearrange("p (b k) -> p b k", b=2), ALU.add)\
                        .then_inc(work.emptied(job), 1)

                def maximum(g):
                    buf, n = ((P0, NQ), (P1, NQ), (Ps, 2))[g]
                    job = ("sc01", "sc13", "ss1")[g]
                    dve.wait_ge(*work.taken(l, job))
                    x = KV * n
                    sink = (cur[:, S_SINKP:S_SINKP + 8] if g < 2
                            else cur[:, S_SINKS:S_SINKS + KV].unsqueeze(2).to_broadcast([P, KV, 2]))
                    s = [sm[:, g, q, 0:x] if g < 2 else sm[:, g, q, 0:x].rearrange("p (v b) -> p v b", v=KV)
                         for q in range(5)]
                    own(v.tensor_reduce(sm[:, g, 0, 0:x].rearrange("p (v i) -> p v i", v=KV), buf, AX.X, ALU.max))
                    own(stt(s[0], s[0], SCALE, sink, ALU.mult, ALU.max))
                    own(ts(s[1], s[0], -1.0, None, ALU.mult))
                    tt(s[3], sink, s[0], ALU.subtract).then_inc(max_ready, 1)

                def normalize(g):
                    buf, n = ((P0, NQ), (P1, NQ), (Ps, 2))[g]
                    x = KV * n
                    dve.wait_ge(p_exp, l * 3 + g + 1)
                    own(tt(sm[:, g, 2, 0:x], sm[:, g, 2, 0:x], sm[:, g, 3, 0:x], ALU.add))
                    own(v.reciprocal(sm[:, g, 4, 0:x], sm[:, g, 2, 0:x]))
                    r = sm[:, g, 4, 0:x].rearrange("p (v i) -> p v i", v=KV).unsqueeze(3)\
                        .to_broadcast([P, KV, n, buf.shape[3]])
                    tt(buf, buf, r, ALU.mult).then_inc(p_ready, 1)

                lo_part(l, 16)
                for n in range(4):
                    silu(4 + n, f"zs{n}", gs[:, n, :])
                    if n < 3:
                        lo_part(l, 17 + n)
                dve.wait_ge(y_back, (l + 1) * 64)
                dve.wait_ge(kv_stored, (l + 1) * 64)
                for m in range(MT):
                    stt(ycp[:, m, :], u_sb[:, m].rearrange("p t j -> p (t j)"), cur[:, S_D + m:S_D + m + 1],
                        ycp[:, m, :], ALU.mult, ALU.add).then_inc(y1_ready, 1)
                dve.wait_ge(y1_ready, (l + 1) * MT)
                maximum(0)
                modulation_of(l, 4)
                modulation_of(l, 5)
                for pair in ((0, 1), (2, 3)):
                    for m in pair:
                        e = ez[:, m % 2, :]
                        dve.wait_ge(y_sq, l * MT + m + 1)
                        own(ts(e, e, GELU_A, 1.0, ALU.mult, ALU.add))
                        tt(e, e, ycp[:, m, :], ALU.mult).then_inc(y_arg, 1)
                    maximum(1 + pair[0] // 2)
                    for m in pair:
                        dve.wait_ge(y_tanh, l * MT + m + 1)
                        stt(yg[:, m, :], ez[:, m % 2, :], 1.0, ycp[:, m, :], ALU.add, ALU.mult).then_inc(yg_ready, 1)
                    for m in pair:
                        dve.wait_ge(yghi, l * MT + m + 1)
                        stt(h_lo[:, MT + m, :], yg[:, m, :], 0.5, h_hi[:, MT + m, :].bitcast(F32), ALU.mult,
                            ALU.subtract).then_inc(yglo, 1)

                for pair in ((0, 1), (2, 3)):
                    normalize(pair[0] // 2)
                    for m in pair:
                        e = ez[:, m % 2, :]
                        dve.wait_ge(*proj.taken(l, f"glu{m}"))
                        own(stt(e, e, 1.0, yg[:, m, :], ALU.add, ALU.mult))
                        dst = gs[:, m, :].rearrange("p (j t) -> p t j", t=T)
                        tt(dst, dst, e.rearrange("p (t j) -> p t j", t=T), ALU.mult).then_inc(gated, 1)
                    lo_part(l, 20 + pair[0] // 2)
                normalize(2)
                for m in range(MT):
                    dve.wait_ge(mixhi, l * 7 + 1 + m)
                    stt(h_lo[:, MT + m, :], gs[:, m, :], 0.125, h_hi[:, MT + m, :].bitcast(F32), ALU.mult, ALU.subtract)\
                        .then_inc(mix_ready, 1)

                for n, (job, toks) in enumerate((("pv0", slice(0, P)), ("pv1", slice(P, SEQ)), ("pvs", slice(SEQ, TOK)))):
                    dve.wait_ge(*work.ready(l, job))
                    if n < 2:
                        tt(ga[:, :, toks], work.bank(job)[:, :].rearrange("p (i q) -> p i q", i=NQ), ga[:, :, toks],
                           ALU.mult).then_inc(work.emptied(job), 1)
                    else:
                        g4 = ga[:, :, toks].rearrange("p i (b t) -> p i b t", b=NB)
                        tt(g4, work.bank(job)[:, 0:NS * NQ].rearrange("p (b i t) -> p i b t", b=NB, i=NQ), g4,
                           ALU.mult).then_inc(work.emptied(job), 1)
                    dve.wait_ge(mixhi, l * 7 + 4 + n + 1)
                    stt(h_lo[:, 0:MT, toks], ga[:, :, toks], 0.5, h_hi[:, 0:MT, toks].bitcast(F32), ALU.mult,
                        ALU.subtract).then_inc(mix_ready, 1)

                dve.wait_ge(mod_ready, (l + 1) * 6)
                for m in range(8):
                    job = f"out{m}"
                    dve.wait_ge(*proj.ready(l, job))
                    b = proj.bank(job)
                    step.add(stt(xT[:, m, 0:SEQ], b[:, 0:SEQ], mod[:, 2 * KT + m, 0:1], xT[:, m, 0:SEQ],
                                 ALU.mult, ALU.add))
                    if m:
                        dve.wait_ge(x_ready, l * KT + m)
                    tt(rt[:, 0, 0:NS].rearrange("p (b t) -> p b t", b=NB), samples(b[:, 0:TOK]),
                       per_sample(2 * KT + m), ALU.mult).then_inc(proj.emptied(job), 1)
                    dve.wait_ge(*proj.taken(l, job))
                    tt(xT[:, m, SEQ:TOK], xT[:, m, SEQ:TOK], rt[:, 0, 0:NS], ALU.add).then_inc(x_ready, 1)
                    if m < 6:
                        lo_part(l, 22 + m)
                    if m:
                        add_square(m - 1, (l + 1) * KT + m)
                add_square(KT - 1, (l + 1) * KT + KT)

            step.restart()
            newton(DEPTH + 1)
            for k in range(KT):
                stt(xT[:, k, :], xT[:, k, :], fing[:, k:k + 1], rstd[:, 0, :], ALU.mult, ALU.mult)\
                    .then_inc(yn_ready, 1)

        @block.gpsimd
        def _(pool):
            step = Steps(pool, pool_step)
            tt = nc.gpsimd.tensor_tensor

            def own(ins):
                step.add(ins)
                step.wait()

            nc.gpsimd.memset(Bblk[:, :, :, :, :], 0.0).then_inc(zeros_set, 1)
            nc.gpsimd.memset(Toep[:, :, :], 0.0).then_inc(zeros_set, 1)
            pool.wait_ge(zeros_set, 2)
            pool.wait_ge(ssm_ready, 1)
            pool.wait_ge(*proj.taken(0, "BT1"))
            pool.wait_ge(*work.taken(0, "CT3"))

            def prepare(l, before):
                one = bass.ds(l, 1)

                def flat(ap):
                    return ap.rearrange("p o i x -> p (o i) x")

                for r in range(2):
                    cr = [coef[:, one, q, :].rearrange("p o i -> p (o i)").unsqueeze(2).to_broadcast([P, NI, GC])
                          for q in (0, 1)]
                    b = [flat(Bsb[:, one, q]) for q in ((0, 1) if r == 0 else (1, 0))]
                    t = [pt[:, q, 0:NI * GC].rearrange("p (i c) -> p i c", i=NI) for q in range(2)]
                    step.add(tt(t[0], b[0], cr[0], ALU.mult))
                    own(tt(t[1], b[1], cr[1], ALU.mult))
                    own(tt(Bbar[:, r], t[0], t[1], ALU.add if r else ALU.subtract))

                def turned(n):
                    r, i0 = n % 2, 4 * (n // 2)
                    if n >= 2:
                        pool.wait_ge(*work.ready(l, f"WB{n - 2}"))
                    elif before is not None:
                        pool.wait_ge(*work.ready(before, f"WB{n + 6}"))
                    shape = [P, 4, T, GC]
                    t = [pt[:, q, 0:4 * T * GC].rearrange("p (i s c) -> p i s c", i=4, s=T) for q in range(2)]
                    for q in range(2):
                        A = Apow[:, one, q, i0:i0 + 4, T - 1::-1].rearrange("p o i s -> p (o i) s").unsqueeze(3)\
                            .to_broadcast(shape)
                        B = Bbar[:, q if r == 0 else 1 - q, i0:i0 + 4, :].unsqueeze(2).to_broadcast(shape)
                        step.add(tt(t[q], A, B, ALU.mult))
                    step.wait()
                    tt(WBq[:, n % 2].rearrange("p i (s c) -> p i s c", s=T), t[0], t[1],
                       ALU.add if r else ALU.subtract).then_inc(wb_ready, 1)
                    pool.wait_ge(wb_ready, l * 8 + n + 1)

                turned(0)
                turned(1)
                if before is not None:
                    pool.wait_ge(*work.ready(before, "y3"))
                for h in range(2):
                    rows = slice(h * NST, (h + 1) * NST)
                    own(nc.gpsimd.tensor_copy(Bblk[rows, :, :, h, :], Bbar[rows]))
                for i0 in range(0, NI, 2):
                    shape = [P, 2, T + 1, GC]
                    t = [pt[:, q, 0:2 * (T + 1) * GC].rearrange("p (i s c) -> p i s c", i=2, s=T + 1)
                         for q in range(2)]
                    for r in range(2):
                        for q in range(2):
                            A = Apow[:, one, q, i0:i0 + 2, :].rearrange("p o i s -> p (o i) s").unsqueeze(3)\
                                .to_broadcast(shape)
                            C = Csb[:, one, q if r == 0 else 1 - q, i0:i0 + 2, :].rearrange("p o i c -> p (o i) c")\
                                .unsqueeze(2).to_broadcast(shape)
                            step.add(tt(t[q], A, C, ALU.mult))
                        step.wait()
                        ins = tt(Gm[:, r, i0:i0 + 2], t[0], t[1], ALU.subtract if r else ALU.add)
                        if (i0, r) == (NI - 2, 1):
                            ins.then_inc(g_ready, 1)
                            pool.wait_ge(g_ready, l + 1)
                        else:
                            own(ins)
                for n in range(2, 8):
                    turned(n)

            prepare(0, None)
            with pool.Fori(0, DEPTH - 1) as before:
                step.restart()
                prepare(before + 1, before)


NAMES = ["x_prompt", "x_sample", "cache_k", "cache_v", "state_ssm_re", "state_ssm_im", "c_prompt", "c_sample",
         "norm_g", "w_ada", "b_ada", "w_in", "attn_sinks", "ssm_a_re", "ssm_a_im", "ssm_log_dt",
         "ssm_b_re", "ssm_b_im", "ssm_c_re", "ssm_c_im", "ssm_d", "w_glu", "b_glu", "w_out", "final_g"]
OUTS = [(1, SEQ, D), (NB, T, D), (DEPTH, 1, WIN, KV, HD), (DEPTH, 1, WIN, KV, HD), (DEPTH, 1, G, NST),
        (DEPTH, 1, G, NST), (DEPTH, NB, WIN, KV, HD), (DEPTH, NB, WIN, KV, HD), (DEPTH, NB, G, NST),
        (DEPTH, NB, G, NST)]


def kernel(**inputs):
    import concourse.bacc as bacc
    from concourse.bass_utils import run_bass_kernel_spmd

    nc = bacc.Bacc("TRN2", target_bir_lowering=False, num_devices=1, dynamic_dma_scratch_size=1024)
    arrays = {f"in_{n}": np.ascontiguousarray(inputs[n]) for n in NAMES}
    arrays["in_constants"] = constants()
    a = {n[3:]: nc.dram_tensor(n, x.shape, mybir.dt.from_np(x.dtype), kind="ExternalInput").ap()
         for n, x in arrays.items()}
    out = [nc.dram_tensor(f"out_{i}", s, F32, kind="ExternalOutput").ap() for i, s in enumerate(OUTS)]
    build(nc, a, out)
    r = run_bass_kernel_spmd(nc, [arrays], core_ids=[0])
    return tuple(r.results[0][f"out_{i}"] for i in range(len(OUTS)))
```

```python
from contextlib import ExitStack

import numpy as np

import concourse.bass as bass
from concourse import mybir
from concourse.alu_op_type import AluOpType as ALU

F32 = mybir.dt.float32
F32R = mybir.dt.float32r
ACT = mybir.ActivationFunctionType
AX = mybir.AxisListType

P = 128
D = 1024
KT = D // P
DEPTH = 2
SEQ = 256
NB = 8
T = 8
NS = NB * T
TOK = SEQ + NS
J = TOK // T
JP = SEQ // T
PAD = 16
NPAIR = 2 * J + PAD
HD = 64
NQ = 4
KV = 2
WIN = 128
COL_K, COL_V, COL_ZA, COL_U, COL_ZS = 512, 640, 768, 1280, 1792
NI = 16
GC = 16
NST = 64
G = 2 * NI
MT = 4
PAST = 1024
EPS = 1e-6
NEG = -1e30
CT = 1 + NB
SCALE = HD ** -0.5
ROT = HD // 4
GELU_A = 0.044715
GELU_B = 0.7978845608028654
TWO_PI = 6.283185307179586
PI_1, PI_2 = 6.28125, 0.0019350051879882812
PI_3 = TWO_PI - PI_1 - PI_2
PI_SAFE = 3.1415925
ROUND = 12582912.0

C_ID, C_ROT, C_COS, C_SIN = 0, 128, 256, 576
C_MP, C_MS, C_SEL, C_END = 896, 1152, 1536, 1664

S_G, S_BADA, S_BGLU, S_D, S_SINKP, S_SINKS = 0, 8, 32, 36, 40, 48
S_A8R, S_A8I, S_A16R, S_A16I, S_END = 50, 66, 98, 114, 146
R_G, R_BADA, R_BGLU, R_D, R_FIN, R_END = (0, DEPTH * KT, 4 * DEPTH * KT, 4 * DEPTH * KT + DEPTH * MT,
                                          4 * DEPTH * KT + 2 * DEPTH * MT, 4 * DEPTH * KT + 2 * DEPTH * MT + KT)

AC = 512
ADA_SS, ADA_GATE = (0, 2, 1, 3), (4, 5)
AROW = 32

UNITS = ([f"ss{m}" for m in range(2, 16)] + ["u2", "u3"]
         + [f"q{m}" for m in range(4)] + ["k", "v"]
         + [x for m in range(4) for x in (f"za{m}", f"gate{m}")]
         + [x for m in range(4) for x in (f"zs{m}", f"gate{4 + m}")]
         + ["glu0", "glu1"] + [f"out{m}" for m in range(8)])
RAW = 4
EARLY = ["ss0", "ss1", "u0", "u1"]
EARLY_AT = "out3"
CACHES_AT = "q1"
SKEW_AT = ["za1", "gate1", "gate1", "za2", "za2", "gate2", "gate2", "za3"]
GATES_AT = (8, 12)
SPLIT = [u for u in EARLY + UNITS if not u.startswith(("ss", "gate"))]
HL = 2
DMAS = {u: 2 if u[0] == "q" or u[:2] == "za" else 3 if u.startswith("out") else 1 for u in UNITS}

PROJ_JOBS = ([f"u{m}" for m in range(4)] + [f"q{m}" for m in range(4)] + ["k", "v"]
             + [f"za{m}" for m in range(4)] + [f"zs{m}" for m in range(4)]
             + [f"glu{m}" for m in range(4)] + [f"out{m}" for m in range(8)])
FIRST_PROJ_JOBS = ["BT0", "BT1"]
FIRST_ADA_JOBS = ["sinks"]
FIRST_JOBS = (["cT", "rowsT"] + [f"xT{k}" for k in range(KT)] + [f"CT{n}" for n in range(4)])
ADA_JOBS = [x for c in ADA_SS + ADA_GATE for x in (f"am{c}", f"at{c}")]
WORK_JOBS = (["rms"]
             + ["WB0", "WB1", "WB2", "WB3", "WB4", "WB5", "rope0", "WB6", "rope1", "WB7", "h0", "rope2"]
             + [f"S{n}" for n in range(8)] + ["kcT0", "kcT1"] + [f"K{n}" for n in range(4)]
             + ["rope3", "rope4", "vT", "ktok", "sc00", "sc01"] + [f"y{n}" for n in range(4)] + ["state"]
             + ["sc10", "sc11", "sc12", "sc13", "ss0", "ss1"]
             + [f"PT{n}" for n in range(6)] + ["PTc", "PTn", "pv0", "pv1", "pvs"])
TURNED_AFTER = {11: (0, 1), 15: (2, 3), "q0": (4, 5), "q1": (6,), "q2": (7,), "q3": ()}
LAST_PROJ_JOBS = ["yT4", "yT5"]
LAST_JOBS = ["yT0", "yT1", "yT2", "rmsF", "yT3"]


def constants():
    c = np.zeros((P, C_END), np.float32)
    c[:, C_ID:C_ID + P] = np.eye(P, dtype=np.float32)
    half = ROT // 2
    inv = (np.float32(500000.0) ** (-np.arange(half, dtype=np.float32) / np.float32(half))).astype(np.float32)
    pos = np.concatenate([np.arange(SEQ), np.tile(PAST + np.arange(T), NB)]).astype(np.float32)
    ang = pos[None, :] * inv[:, None]
    c[:, C_COS:C_COS + TOK] = 1.0
    for kv in range(KV):
        a = kv * HD
        for d in range(half):
            c[a + d, C_COS:C_COS + TOK] = c[a + d + half, C_COS:C_COS + TOK] = np.cos(ang[d])
            c[a + d, C_SIN:C_SIN + TOK] = -np.sin(ang[d])
            c[a + d + half, C_SIN:C_SIN + TOK] = np.sin(ang[d])
            c[a + d + half, C_ROT + a + d] = c[a + d, C_ROT + a + d + half] = 1.0
    r = np.arange(P)
    diff = P + r[:, None] - np.arange(2 * P)[None, :]
    c[:, C_MP:C_MP + 2 * P] = np.where((diff >= 0) & (diff <= WIN), 0.0, NEG)
    b4, t = r // 32, r % T
    for half_b in range(2):
        m = np.full((P, WIN + NS), NEG, np.float32)
        m[:, :WIN][np.arange(WIN)[None, :] >= t[:, None]] = 0.0
        col = np.arange(NS)
        m[:, WIN:][(col[None, :] // T == (half_b * 4 + b4)[:, None]) & (col[None, :] % T <= t[:, None])] = 0.0
        c[:, C_MS + half_b * (WIN + NS):C_MS + (half_b + 1) * (WIN + NS)] = m
    for i in range(NQ):
        c[i, C_SEL:C_SEL + P] = (r // T % NQ == i)
    return c


class Ring:

    def __init__(self, banks, filled, emptied, first, layer, last):
        self.banks, self.n = banks, len(banks)
        self._filled, self._emptied = filled, emptied
        self.first, self.layer, self.last = first, layer, last

    def _at(self, l, job):
        n = self.n
        of = [sum(1 for q in range(len(x)) if q % n == b) for x in (self.first, self.layer) for b in range(n)]
        if job in self.layer:
            q = self.layer.index(job)
            return q % n, of[q % n] + l * of[n + q % n] + q // n
        if job in self.first:
            q = self.first.index(job)
            return q % n, q // n
        q = self.last.index(job)
        return q % n, of[q % n] + DEPTH * of[n + q % n] + q // n

    def bank(self, job):
        for x in (self.first, self.layer, self.last):
            if job in x:
                return self.banks[x.index(job) % self.n]

    def room(self, l, job):
        b, k = self._at(l, job)
        return self._emptied[b], k

    def ready(self, l, job):
        b, k = self._at(l, job)
        return self._filled[b], k + 1

    def taken(self, l, job):
        b, k = self._at(l, job)
        return self._emptied[b], k + 1

    def filled(self, job):
        return self._filled[self._at(0, job)[0]]

    def emptied(self, job):
        return self._emptied[self._at(0, job)[0]]


class Steps:

    def __init__(self, eng, sem):
        self.eng, self.sem, self.n = eng, sem, 0

    def add(self, ins):
        self.n += 1
        ins.then_inc(self.sem, 1)

    def wait(self):
        self.eng.wait_ge(self.sem, self.n)

    def restart(self):
        if self.n:
            self.wait()
        self.eng.sem_clear(self.sem)
        self.n = 0


def slot_of(unit):
    return UNITS.index(unit) % RAW


def loads_at(l, unit):
    if unit in EARLY:
        return l * 16 + 16
    s = slot_of(unit)
    own = [u for u in UNITS if slot_of(u) == s]
    return l * (16 * sum(DMAS[u] for u in own)) + 16 * sum(DMAS[u] for u in own[:own.index(unit) + 1])


def uses_at(l, unit):
    if unit in EARLY:
        return l + 1
    return l * (len(UNITS) // RAW) + UNITS.index(unit) // RAW + 1


def build(nc, a, out):
    ctx = ExitStack()
    with ctx:
        def sb(name, shape, dt=F32):
            return ctx.enter_context(nc.sbuf_tensor(name, shape, dt))

        def sem(name):
            return ctx.enter_context(nc.semaphore(name))

        banks = [ctx.enter_context(nc.psum_tensor(f"bank{b}", [P, 512], F32)) for b in range(8)]

        const = sb("const", [P, C_SEL])
        ident = const[:, C_ID:C_ID + P]
        rot = const[:, C_ROT:C_ROT + P]
        cos, sin = const[:, C_COS:C_COS + TOK], const[:, C_SIN:C_SIN + TOK]
        mean = sb("mean", [P, P])
        raw = sb("raw", [P, RAW, D])
        w_hi = sb("w_hi", [P, HL, D], F32R)
        w_lo = sb("w_lo", [P, HL, D], F32R)
        xT = sb("xT", [P, KT, TOK])
        h_hi = sb("h_hi", [P, KT, TOK], F32R)
        h_lo = sb("h_lo", [P, KT, TOK], F32R)
        hn = sb("hn", [P, 2, TOK])
        hf = sb("hf", [P, 2, TOK])
        ez = sb("ez", [P, 2, TOK])
        sq = ez
        sqsum = sb("sqsum", [P, TOK])
        rstd = sb("rstd", [P, 2, TOK])
        u_sb = sb("u_sb", [P, MT, T, J])
        Upad = sb("U", [P, G * J + NPAIR - 2 * J])
        U = Upad[:, 0:G * J].rearrange("p (g j) -> p g j", g=G)
        HY = sb("HY", [P, 2 * NI * J])
        Hst = HY[:, :].rearrange("p (r i j) -> p r i j", r=2, i=NI)
        Ysb = HY[:, 0:G * J].rearrange("p (g j) -> p g j", g=G)
        R1 = sb("R1", [P, 4096])
        Ssb = R1[:, 0:1280].rearrange("p (r i j) -> p r i j", r=2, i=NI)
        Hblk = R1[:, 1280:1280 + 2560].rearrange("p (r i h j) -> p r i h j", r=2, i=NI, h=2)
        Hpad = R1[:, 1280 + 2560:1280 + 2560 + PAD]
        xn = R1[:, 0:KT * TOK].rearrange("p (k n) -> p k n", k=KT)
        P0 = R1[:, 0:1024].rearrange("p (v i k) -> p v i k", v=KV, i=NQ)
        P1 = R1[:, 1024:3072].rearrange("p (v i k) -> p v i k", v=KV, i=NQ)
        Ps = R1[:, 3072:3840].rearrange("p (v b k) -> p v b k", v=KV, b=2)
        R2 = sb("R2", [P, 4096])
        xin = R2[:, 0:3 * D].rearrange("p (n d) -> p n d", n=3)
        ybuf = xin
        WB = R2[:, :].rearrange("p (n r i q) -> p n r i q", n=4, r=2, i=4)
        PT = R2[:, 0:3072].rearrange("p (n v q) -> p n v q", n=3, v=KV)
        PTc = R2[:, 3072:3584].rearrange("p (v b q) -> p v b q", v=KV, b=2)
        PTn = R2[:, 3584:4096].rearrange("p (v b q) -> p v b q", v=KV, b=2)
        R3 = sb("R3", [P, 2560])
        kc = R3[:, 0:1024].rearrange("p (b d) -> p b d", b=NB)
        h0 = R3[:, 1024:1024 + 2 * P].rearrange("p (r q) -> p r q", r=2)
        Ksb = R3[:, 0:2048].rearrange("p (i q) -> p i q", i=NI)
        ycp = R3[:, 0:1280].rearrange("p (m n) -> p m n", m=MT)
        yg = R3[:, 1280:2560].rearrange("p (m n) -> p m n", m=MT)
        scan = sb("scan", [P, 2, JP * NI])
        Gm = sb("Gm", [P, 2, NI, T + 1, GC])
        Toep = sb("Toep", [P, G, P])
        Apow = sb("Apow", [P, DEPTH, 2, NI, T + 1])
        coef = sb("coef", [P, DEPTH, 2, NI])
        Bsb = sb("Bsb", [P, DEPTH, 2, NI, GC])
        Csb = sb("Csb", [P, DEPTH, 2, NI, GC])
        Bblk = sb("Bblk", [P, 2, NI, 2, GC])
        pt = sb("pt", [P, 2, 4 * GC * T])
        qT = sb("qT", [P, NQ, SEQ])
        qs = sb("qs", [P, NB, NQ, T])
        kT = sb("kT", [P, TOK])
        qraw, rt = hn, hf
        vtok = sb("vtok", [P, 3, P])
        ktok = R3[:, 2048:2048 + 2 * P].rearrange("p (n q) -> p n q", n=2)
        kcT = sb("kcT", [P, NB, WIN])
        vc = U[:, :, :].rearrange("p g j -> p (g j)")[:, 0:NB * P].rearrange("p (b q) -> p b q", b=NB)
        early = [qT[:, :, :].rearrange("p i n -> p (i n)"), kcT[:, :, :].rearrange("p b n -> p (b n)"),
                 R3[:, 0:D], R3[:, D:2 * D]]
        fin = sb("fin", [P, 2, 1 + NB, NI])
        stage = hn[:, :, :].rearrange("p a b -> p (a b)")[:, 0:4 * P].rearrange("p (n q) -> p n q", n=4)
        ga = sb("ga", [P, MT, TOK])
        gs = sb("gs", [P, MT, TOK])
        small = sb("small", [P, DEPTH, S_END])
        cur = sb("cur", [P, S_END])
        hbglu = sb("hbglu", [P, MT])
        fing = sb("fing", [P, KT])
        cT = sb("cT", [P, KT, AROW])
        mod = sb("mod", [P, 3 * KT, CT])
        epsb = sb("epsb", [P, 1])
        warm = sb("warm", [P, 1])
        sm = sb("sm", [P, 3, 5, 8])
        rec = sb("rec", [P, 2, 2, NI])
        arow = hn[:, :, :].rearrange("p a b -> p (a b)")[:, 0:AC]
        wide = scan[:, 0, :].rearrange("p (r i k) -> p r i k", r=2, i=NI)
        prod = scan[:, 1, :].rearrange("p (r i k) -> p r i k", r=2, i=NI)
        ge = scan[:, :, 0:TOK]
        Bbar = sb("Bbar", [P, 2, NI, GC])

        crow = R3[0:CT, 0:D]
        cexp = R3[0:CT, D:2 * D]
        rowsP = R1[0:R_END, 0:P]
        rowsS = R1[0:3 * DEPTH * NI, P:2 * P]
        ldt = R1[0:DEPTH * NI, 2 * P:2 * P + 2]
        sel = R1[0:NQ, 330:330 + P]
        sinkc = R1[0:NQ, 320:324]
        Braw = R1[0:2 * DEPTH * NI, 512:512 + 2048]
        Craw = Gm[:, :, :, :, :].rearrange("p r i t c -> p (r i t c)")[:, 0:2048].rearrange(
            "p (n t d q) -> p n t d q", n=2 * DEPTH, t=4, d=2)
        rowsT = HY[:, 0:224]
        W = DEPTH * NI
        zz = HY[:, 256:256 + 20 * W].rearrange("p (n w) -> p n w", n=20)

        u_dram = nc.dram_tensor("u_turn", [G, GC, T, J], F32, kind="Internal").ap()
        y_dram = nc.dram_tensor("y_turn", [G, GC, T, J], F32, kind="Internal").ap()

        loaded = [sem(f"unit_loaded{s}") for s in range(RAW)]
        used = [sem(f"unit_used{s}") for s in range(RAW)]
        early_in = [sem(f"{unit}_loaded") for unit in EARLY]
        early_used = [sem(f"{unit}_used") for unit in EARLY]

        def place(unit):
            return early[EARLY.index(unit)] if unit in EARLY else raw[:, slot_of(unit), :]

        def loaded_of(unit):
            return early_in[EARLY.index(unit)] if unit in EARLY else loaded[slot_of(unit)]

        def used_of(unit):
            return early_used[EARLY.index(unit)] if unit in EARLY else used[slot_of(unit)]

        hi_done = sem("hi_done")
        const_in, cond_in, x_in, small_in, bc_in = (sem(n) for n in
                                                     ("const_in", "cond_in", "x_in", "small_in", "bc_in"))
        vcache_in = sem("vcache_in")
        cache_in, h0_in, skew_in = sem("cache_in"), sem("h0_in"), sem("skew_in")
        u_out, u_back, y_out, y_back = sem("u_out"), sem("u_back"), sem("y_out"), sem("y_back")
        kv_stored, state_stored, cache_copied, y_stored = (sem(n) for n in
                                                            ("kv_stored", "state_stored", "cache_copied", "y_stored"))
        proj = Ring(banks[0:2], [sem(f"proj_filled{b}") for b in range(2)],
                    [sem(f"proj_emptied{b}") for b in range(2)], FIRST_PROJ_JOBS, PROJ_JOBS, LAST_PROJ_JOBS)
        ada = Ring(banks[2:3], [sem("ada_filled")], [sem("ada_emptied")], FIRST_ADA_JOBS, ADA_JOBS, [])
        work = Ring(banks[3:8], [sem(f"work_filled{b}") for b in range(5)],
                    [sem(f"work_emptied{b}") for b in range(5)], FIRST_JOBS, WORK_JOBS, LAST_JOBS)
        def output_ring(n):
            return proj if f"yT{n}" in LAST_PROJ_JOBS else work

        dve_step, act_step, pool_step = sem("dve_step"), sem("act_step"), sem("pool_step")
        silu_c, silu_r = sem("silu_c"), sem("silu_r")
        sinks_in = sem("sinks_in")
        ldt_wide = sem("ldt_wide")
        ssm_exp = sem("ssm_exp")
        ssm_val = sem("ssm_val")
        ssm_ready = sem("ssm_ready")
        x_ready = sem("x_ready")
        sq_done, sq_added = sem("sq_done"), sem("sq_added")
        rstd_raw = sem("rstd_raw")
        norm_done = sem("norm_done")
        hp_done, hs_done = sem("hp_done"), sem("hs_done")
        hhi_done, h_ready = sem("hhi_done"), sem("h_ready")
        mod_ready = sem("mod_ready")
        mean_set = sem("mean_set")
        wb_ready, g_ready, zeros_set = sem("wb_ready"), sem("g_ready"), sem("zeros_set")
        H_ready, fin_ready = sem("H_ready"), sem("fin_ready")
        gate_tanh = sem("gate_tanh")
        max_ready, p_exp, p_ready = sem("max_ready"), sem("p_exp"), sem("p_ready")
        mixhi, mix_ready = sem("mixhi"), sem("mix_ready")
        y1_ready, y_sq, y_arg, y_tanh = sem("y1_ready"), sem("y_sq"), sem("y_arg"), sem("y_tanh")
        yg_ready, yghi, yglo = sem("yg_ready"), sem("yghi"), sem("yglo")
        gated = sem("gated")
        yn_ready, rstd_done = sem("yn_ready"), sem("rstd_done")

        block = ctx.enter_context(nc.Block())

        @block.sync
        def _(sp):
            def one_layer(l):
                return slice(l, l + 1) if isinstance(l, int) else bass.ds(l, 1)

            def ada_rows(l, kind, m):
                c0, r0 = (ADA_SS if kind == "ss" else ADA_GATE)[m // 4] * AC, m % 4 * 2 * P
                return a["w_ada"][one_layer(l), r0:r0 + 2 * P, c0:c0 + AC].rearrange("o (k p) c -> p (o k) c", p=P)

            def early_units(l):
                for m in range(2):
                    sp.dma_start(place(f"ss{m}").rearrange("p (k c) -> p k c", k=2), ada_rows(l, "ss", m))\
                        .then_inc(loaded_of(f"ss{m}"), 16)
                for m in range(2):
                    src = a["w_in"][one_layer(l), :, COL_U + m * P:COL_U + (m + 1) * P].rearrange(
                        "o (k p) c -> p (o k) c", p=P)
                    sp.dma_start(place(f"u{m}").rearrange("p (k c) -> p k c", k=KT), src)\
                        .then_inc(loaded_of(f"u{m}"), 16)

            def load(l, unit):
                n, s = UNITS.index(unit), slot_of(unit)
                if not (isinstance(l, int) and l == 0) or n >= RAW:
                    sp.wait_ge(used[s], uses_at(l, unit) - 1)
                dst = raw[:, s, :].rearrange("p (k c) -> p k c", k=KT)
                own = one_layer(l)
                kind, m = unit.rstrip("0123456789"), int("0" + unit.lstrip("abcdefghijklmnopqrstuvwxyz"))
                if kind in ("ss", "gate"):
                    sp.dma_start(raw[:, s, :].rearrange("p (k c) -> p k c", k=2), ada_rows(l, kind, m))\
                        .then_inc(loaded[s], 16)
                elif kind in ("q", "za"):
                    for kv in reversed(range(KV)):
                        c0 = (0 if kind == "q" else COL_ZA) + kv * NQ * HD + m * HD
                        src = a["w_in"][own, :, c0:c0 + HD].rearrange("o (k p) c -> p (o k) c", p=P)
                        sp.dma_start(dst[:, :, kv * HD:(kv + 1) * HD], src).then_inc(loaded[s], 16)
                elif kind in ("u", "k", "v", "zs"):
                    c0 = {"u": COL_U, "k": COL_K, "v": COL_V, "zs": COL_ZS}[kind] + m * P
                    src = a["w_in"][own, :, c0:c0 + P].rearrange("o (k p) c -> p (o k) c", p=P)
                    sp.dma_start(dst, src).then_inc(loaded[s], 16)
                elif kind == "glu":
                    src = a["w_glu"][own, :, m * 2 * P:(m + 1) * 2 * P].rearrange("o (k p) c -> p (o k) c", p=P)
                    sp.dma_start(raw[:, s, :].rearrange("p (k c) -> p k c", k=MT), src).then_inc(loaded[s], 16)
                else:
                    for kv in range(KV):
                        r0 = kv * NQ * HD
                        src = a["w_out"][own, r0:r0 + NQ * HD, m * P:(m + 1) * P].rearrange(
                            "o (k p) c -> p (o k) c", p=HD)
                        sp.dma_start(dst[kv * HD:(kv + 1) * HD, 0:MT, :], src).then_inc(loaded[s], 16)
                    src = a["w_out"][own, MT * P:, m * P:(m + 1) * P].rearrange("o (k p) c -> p (o k) c", p=P)
                    sp.dma_start(dst[:, MT:KT, :], src).then_inc(loaded[s], 16)

            def caches(l):
                own = one_layer(l)
                sp.dma_start(kc, a["cache_k"][own].rearrange("o b w v d -> w (o b) (v d)")).then_inc(cache_in, 16)
                for r, name in enumerate(("state_ssm_re", "state_ssm_im")):
                    src = a[name][own].rearrange("o b (i h) p -> (o b i) (h p)", h=2)
                    sp.dma_start(h0[:, r, :], src).then_inc(h0_in, 16)
                for name, dst in (("cache_k", out[6]), ("cache_v", out[7])):
                    sp.dma_start(dst[own, :, 0:WIN - T].rearrange("o b w v d -> (o b) (w v d)"),
                                 a[name][own, :, T:WIN].rearrange("o b w v d -> (o b) (w v d)")
                                 ).then_inc(cache_copied, 16)

            def skew(l, s):
                if s == 0:
                    sp.wait_ge(zeros_set, 4)
                    sp.wait_ge(*work.taken(l, "K3"))
                for h in range(2):
                    dst = Toep[s * GC:(s + 1) * GC, h::2, s * GC:P]
                    sp.dma_start(dst, Ksb[h * GC:(h + 1) * GC, :, 0:P - s * GC]).then_inc(skew_in, 16)

            def cached_values(l):
                sp.wait_ge(*work.ready(l, "y3"))
                sp.dma_start(vc, a["cache_v"][one_layer(l)].rearrange("o b w v d -> w (o b) (v d)"))\
                    .then_inc(vcache_in, 16)

            def first_units(l):
                for unit in UNITS[:RAW]:
                    load(l, unit)

            def rest_of_layer(l, last):
                for unit in UNITS[RAW:]:
                    load(l, unit)
                    if unit == EARLY_AT and not last:
                        sp.wait_ge(*work.ready(l, "ss1"))
                        sp.wait_ge(gated, (l + 1) * MT)
                        early_units(l + 1)
                    if unit == "zs1":
                        cached_values(l)
                    if unit == CACHES_AT:
                        caches(l)
                    for s in range(T):
                        if SKEW_AT[s] == unit:
                            skew(l, s)

            sp.dma_start(crow[0:1, :], a["c_prompt"]).then_inc(cond_in, 16)
            sp.dma_start(crow[1:CT, :], a["c_sample"]).then_inc(cond_in, 16)
            for name, r0, r1 in (("norm_g", R_G, R_BADA), ("b_ada", R_BADA, R_BGLU), ("b_glu", R_BGLU, R_D)):
                sp.dma_start(rowsP[r0:r1, :], a[name].rearrange("l (r p) -> (l r) p", p=P)).then_inc(small_in, 16)
            sp.dma_start(rowsP[R_D:R_FIN, :], a["ssm_d"].rearrange("l (r g) c -> (l r) (g c)", r=MT))\
                .then_inc(small_in, 16)
            sp.dma_start(rowsP[R_FIN:R_END, :], a["final_g"].rearrange("(r p) -> r p", p=P)).then_inc(small_in, 16)
            for n, name in enumerate(("ssm_a_re", "ssm_a_im")):
                sp.dma_start(rowsS[n * W:(n + 1) * W, :], a[name].rearrange("l (i h) p -> (l i) (h p)", h=2))\
                    .then_inc(small_in, 16)
            sp.dma_start(ldt, a["ssm_log_dt"].rearrange("l (i h) -> (l i) h", h=2)).then_inc(small_in, 16)
            for r, name in enumerate(("ssm_b_re", "ssm_b_im")):
                sp.dma_start(Braw[r * W:(r + 1) * W, :], a[name].rearrange("l (i h) p c -> (l i) (h p c)", h=2))\
                    .then_inc(bc_in, 16)
            for r, name in enumerate(("ssm_c_re", "ssm_c_im")):
                for l in range(DEPTH):
                    for d in range(2):
                        sp.dma_start(Craw[:, 2 * l + r, :, d, :],
                                     a[name][l].rearrange("(t g) c p -> (g c) t p", t=4)).then_inc(bc_in, 16)
            sp.dma_start(small[:, :, S_SINKP:S_SINKP + 8], a["attn_sinks"].unsqueeze(0).to_broadcast([P, DEPTH, 8]))\
                .then_inc(sinks_in, 16)
            sp.dma_start(sel, a["constants"][0:NQ, C_SEL:C_END]).then_inc(sinks_in, 16)
            with nc.allow_non_contiguous_dma(reason="16 numbers"):
                sp.dma_start(sinkc, a["attn_sinks"].rearrange("l (v i) -> i (l v)", i=NQ)).then_inc(sinks_in, 16)
            sp.wait_ge(*work.ready(0, "cT"))
            early_units(0)
            first_units(0)
            with sp.Fori(0, DEPTH - 1) as l:
                rest_of_layer(l, False)
                first_units(l + 1)
            rest_of_layer(DEPTH - 1, True)
            sp.wait_ge(cache_copied, DEPTH * 32)

        @block.tensor
        def _(pe):
            def mm(out_, lhsT, rhs, start, stop, free=False):
                return nc.tensor.matmul(out_, lhsT, rhs, start=start, stop=stop, skip_group_check=free)

            pe.wait_ge(const_in, 16)
            pe.wait_ge(silu_r, 1)
            b = work.bank("cT")
            for k in range(KT):
                ins = nc.tensor.transpose(b[:, k * CT:(k + 1) * CT], cexp[:, k * P:(k + 1) * P], ident[0:CT, 0:CT])
            ins.then_inc(work.filled("cT"), 1)
            b = work.bank("rowsT")
            pe.wait_ge(small_in, 16 * 8)
            pe.wait_ge(ldt_wide, 1)
            nc.tensor.transpose(b[:, 0:R_END], rowsP, ident[0:R_END, 0:R_END])
            nc.tensor.transpose(b[:, P:P + 3 * W], rowsS, ident[0:3 * W, 0:3 * W]).then_inc(work.filled("rowsT"), 1)
            pe.wait_ge(x_in, 32)
            for k in range(KT):
                pe.wait_ge(*work.room(0, f"xT{k}"))
                b = work.bank(f"xT{k}")
                for n, rows in enumerate((P, P, NS)):
                    ins = nc.tensor.transpose(b[:, n * P:n * P + rows], xin[0:rows, n, k * P:(k + 1) * P],
                                              ident[0:rows, 0:rows])
                ins.then_inc(work.filled(f"xT{k}"), 1)
            b = ada.bank("sinks")
            pe.wait_ge(sinks_in, 48)
            mm(b[:, 0:DEPTH * KV], sel, sinkc, True, True).then_inc(ada.filled("sinks"), 1)
            pe.wait_ge(bc_in, 16 * 10)
            for n in range(2):
                b = proj.bank(f"BT{n}")
                for c in range(8):
                    src = Braw[:, n * 8 + c:2048:GC]
                    ins = nc.tensor.transpose(b[:, c * 64:(c + 1) * 64], src, ident[0:64, 0:64])
                ins.then_inc(proj.filled(f"BT{n}"), 1)
            for n in range(4):
                pe.wait_ge(*work.room(0, f"CT{n}"))
                b = work.bank(f"CT{n}")
                for t in range(4):
                    ins = nc.tensor.transpose(b[:, t * P:(t + 1) * P],
                                              Craw[:, n, t].rearrange("p d q -> p (d q)"), ident)
                ins.then_inc(work.filled(f"CT{n}"), 1)

            def sum_squares(l, job, layers):
                pe.wait_ge(*work.room(l, job))
                pe.wait_ge(sq_added, layers * KT)
                pe.wait_ge(mean_set, 3)
                mm(work.bank(job)[:, 0:TOK], mean[:, :], sqsum[:, :], True, True).then_inc(work.filled(job), 1)

            def modulation(l, kind, m):
                x, n = m // 4, m % 4
                c = (ADA_SS if kind == "ss" else ADA_GATE)[x]
                if n == 0:
                    pe.wait_ge(*ada.room(l, f"am{c}"))
                b = ada.bank(f"am{c}")
                unit = f"{kind}{m}"
                src = place(unit)
                pe.wait_ge(loaded_of(unit), loads_at(l, unit))
                for k in (2 * n, 2 * n + 1):
                    j = k % 4
                    ins = mm(b[j * AROW:(j + 1) * AROW, :], cT[:, k, :],
                             src[:, k % 2 * AC:(k % 2 + 1) * AC], k < 4, k >= 4, True)
                if n == 3:
                    ins.then_inc(ada.filled(f"am{c}"), 1)
                else:
                    ins.then_inc(used_of(unit), 1)

            def turn_modulation(l, kind, x):
                c = (ADA_SS if kind == "ss" else ADA_GATE)[x]
                pe.wait_ge(*ada.taken(l, f"am{c}"))
                for q in range(4):
                    ins = nc.tensor.transpose(ada.bank(f"at{c}")[:, q * P:(q + 1) * P], arow[:, q * P:(q + 1) * P],
                                              ident)
                    if q == 0:
                        ins.then_inc(used[slot_of(f"{kind}{4 * x + 3}")], 1)
                ins.then_inc(ada.filled(f"at{c}"), 1)

            def split_passes(out_, unit, k, cols, rhs_k, first, last):
                s = SPLIT.index(unit) % HL
                hi, lo = w_hi[:, s, cols], w_lo[:, s, cols]
                mm(out_, hi, h_hi[:, rhs_k, :], first, False)
                mm(out_, hi, h_lo[:, rhs_k, :], False, False)
                return mm(out_, lo, h_hi[:, rhs_k, :], False, last)

            def project(l, job):
                pe.wait_ge(used_of(job), uses_at(l, job))
                pe.wait_ge(*proj.room(l, job))
                for k in range(KT):
                    ins = split_passes(proj.bank(job)[:, 0:TOK], job, k, slice(k * P, (k + 1) * P), k,
                                       k == 0, k == KT - 1)
                ins.then_inc(proj.filled(job), 1)

            def project_two(l, jobs, tiles):
                first = tiles[0] == 0
                for job, k in [(job, k) for k in tiles for job in jobs] if first else \
                        [(job, k) for job in jobs for k in tiles]:
                    if k == 0:
                        pe.wait_ge(used_of(job), uses_at(l, job))
                        pe.wait_ge(*proj.room(l, job))
                    if first or job == jobs[0]:
                        pe.wait_ge(h_ready, l * KT + k + 1)
                    ins = split_passes(proj.bank(job)[:, 0:TOK], job, k, slice(k * P, (k + 1) * P), k,
                                       k == 0, k == KT - 1)
                    if k == KT - 1:
                        ins.then_inc(proj.filled(job), 1)

            def rope(l, n):
                job = f"rope{n}"
                pe.wait_ge(*work.room(l, job))
                pe.wait_ge(*proj.taken(l, f"q{n}" if n < 4 else "k"))
                mm(work.bank(job)[:, 0:TOK], rot, qraw[:, n % 2, :], True, True).then_inc(work.filled(job), 1)

            def turn_B(l, n):
                job, r, q = f"WB{n}", n % 2, n // 2
                pe.wait_ge(*work.room(l, job))
                pe.wait_ge(wb_ready, l * 8 + n + 1)
                b = work.bank(job)
                for i in range(4):
                    ins = nc.tensor.transpose(b[:, i * P:(i + 1) * P], WB[:, q, r, i, :], ident)
                ins.then_inc(work.filled(job), 1)

            def values(l):
                pe.wait_ge(*proj.taken(l, "v"))
                pe.wait_ge(*work.room(l, "vT"))
                b = work.bank("vT")
                for n, rows in enumerate((P, P, NS)):
                    ins = nc.tensor.transpose(b[0:rows, n * P:(n + 1) * P], qraw[:, 1, n * P:n * P + rows], ident)
                ins.then_inc(work.filled("vT"), 1)

            with pe.Fori(0, DEPTH) as l:
                sum_squares(l, "rms", l + 1)
                pe.wait_ge(*work.taken(0, "cT"))
                for half in range(2):
                    for m in range(8 * half, 8 * half + 8):
                        modulation(l, "ss", m)
                        if m % 4 == 3:
                            turn_modulation(l, "ss", m // 4)
                        if m in (11, 15):
                            for n in TURNED_AFTER[m]:
                                turn_B(l, n)
                    project_two(l, ("u0", "u1"), range(4 * half, 4 * half + 4))
                for m in range(2, 4):
                    project(l, f"u{m}")
                for m in range(4):
                    project(l, f"q{m}")
                    if m:
                        rope(l, m - 1)
                    for n in TURNED_AFTER[f"q{m}"]:
                        turn_B(l, n)
                    if m == 2:
                        pe.wait_ge(h0_in, l * 32 + 32)
                        pe.wait_ge(*work.room(l, "h0"))
                        for r in range(2):
                            ins = nc.tensor.transpose(work.bank("h0")[:, r * P:(r + 1) * P], h0[:, r, :], ident)
                        ins.then_inc(work.filled("h0"), 1)
                pe.wait_ge(u_back, (l + 1) * 16 * T)
                for n in range(8):
                    job, r, q = f"S{n}", n % 2, n // 2
                    pe.wait_ge(*work.room(l, job))
                    pe.wait_ge(*work.taken(l, f"WB{n}"))
                    for i in range(4):
                        g = 2 * (4 * q + i)
                        ins = mm(work.bank(job)[:, i * NPAIR:(i + 1) * NPAIR], WB[:, q, r, i, :],
                                 Upad[:, g * J:g * J + NPAIR], True, True)
                    ins.then_inc(work.filled(job), 1)

                pe.wait_ge(cache_in, l * 16 + 16)
                for n in range(2):
                    pe.wait_ge(*work.room(l, f"kcT{n}"))
                    for q in range(4):
                        ins = nc.tensor.transpose(work.bank(f"kcT{n}")[:, q * P:(q + 1) * P], kc[:, n * 4 + q, :], ident)
                    ins.then_inc(work.filled(f"kcT{n}"), 1)
                pe.wait_ge(g_ready, l + 1)
                for n in range(4):
                    job = f"K{n}"
                    pe.wait_ge(*work.room(l, job))
                    for q in range(4):
                        i = 4 * n + q
                        for r in range(2):
                            ins = mm(work.bank(job)[0:2 * GC, q * P:(q + 1) * P],
                                     Bblk[:, r, i].rearrange("p h c -> p (h c)"),
                                     Gm[:, r, i, 0:T].rearrange("p t c -> p (t c)"), r == 0, r == 1)
                    ins.then_inc(work.filled(job), 1)

                project(l, "k")
                rope(l, 3)
                project(l, "v")
                rope(l, 4)
                values(l)

                for m in range(2):
                    project(l, f"za{m}")
                    modulation(l, "gate", m)
                pe.wait_ge(*work.room(l, "ktok"))
                pe.wait_ge(*work.taken(l, "rope4"))
                b = work.bank("ktok")
                nc.tensor.transpose(b[:, 0:P], kT[:, P:2 * P], ident)
                nc.tensor.transpose(b[0:NS, P:2 * P], kT[:, SEQ:TOK], ident).then_inc(work.filled("ktok"), 1)

                for m in range(2, 4):
                    project(l, f"za{m}")
                    modulation(l, "gate", m)

                for kv in range(KV):
                    rows = slice(kv * HD, (kv + 1) * HD)
                    job = f"sc0{kv}"
                    pe.wait_ge(*work.room(l, job))
                    for i in range(NQ):
                        ins = mm(work.bank(job)[:, i * P:(i + 1) * P], qT[rows, i, 0:P], kT[rows, 0:P], True, True)
                    ins.then_inc(work.filled(job), 1)

                pe.wait_ge(H_ready, (l + 1) * 2)
                for n in range(4):
                    pe.wait_ge(*work.room(l, f"y{n}"))
                    for q in range(4):
                        i = 4 * n + q
                        for r in range(2):
                            at = 1280 + (r * NI + i) * 2 * J
                            mm(work.bank(f"y{n}")[:, q * NPAIR:(q + 1) * NPAIR],
                               Gm[:, r, i, 1:T + 1].rearrange("p t c -> p (t c)"), R1[:, at:at + NPAIR],
                               r == 0 and q == 0, False, True)
                pe.wait_ge(skew_in, (l + 1) * 2 * T * 16)
                for n in range(4):
                    for q in range(4):
                        i = 4 * n + q
                        o = work.bank(f"y{n}")[:, q * NPAIR:q * NPAIR + 2 * J]
                        for h in range(2):
                            for c in range(4):
                                rows = slice(c * 32, (c + 1) * 32)
                                ins = mm(o[rows, h * J:(h + 1) * J], Toep[:, 2 * i + h, rows], U[:, 2 * i + h, :],
                                         False, h == 1, True)
                    ins.then_inc(work.filled(f"y{n}"), 1)
                turn_modulation(l, "gate", 0)
                pe.wait_ge(*work.room(l, "state"))
                pe.wait_ge(fin_ready, l + 1)
                b = work.bank("state")
                for r in range(2):
                    nc.tensor.transpose(b[:, r * P:(r + 1) * P],
                                        fin[:, r, 1:1 + NB, :].rearrange("p b i -> p (b i)"), ident)
                for r in range(2):
                    ins = nc.tensor.transpose(b[0:NI, (2 + r) * P:(3 + r) * P], fin[:, r, 0, :], ident)
                ins.then_inc(work.filled("state"), 1)

                for kv in range(KV):
                    rows = slice(kv * HD, (kv + 1) * HD)
                    for n in range(2):
                        job = f"sc1{2 * kv + n}"
                        pe.wait_ge(*work.room(l, job))
                        for q in range(2):
                            ins = mm(work.bank(job)[:, q * 2 * P:(q + 1) * 2 * P], qT[rows, 2 * n + q, P:SEQ],
                                     kT[rows, 0:SEQ], True, True)
                        ins.then_inc(work.filled(job), 1)
                for kv in range(KV):
                    rows = slice(kv * HD, (kv + 1) * HD)
                    job = f"ss{kv}"
                    pe.wait_ge(*work.room(l, job))
                    pe.wait_ge(*work.taken(l, "kcT0"))
                    pe.wait_ge(*work.taken(l, "kcT1"))
                    for hb in range(2):
                        o = work.bank(job)[:, hb * (WIN + NS):(hb + 1) * (WIN + NS)]
                        mm(o[:, WIN:], qs[rows, hb * 4:hb * 4 + 4].rearrange("p b i t -> p (b i t)"),
                           kT[rows, SEQ:TOK], True, True, True)
                        for q in range(4):
                            ins = mm(o[q * 32:(q + 1) * 32, 0:WIN],
                                     qs[rows, hb * 4 + q].rearrange("p i t -> p (i t)"),
                                     kcT[rows, hb * 4 + q, :], True, True, True)
                    ins.then_inc(work.filled(job), 1)

                pe.wait_ge(*work.taken(l, "vT"))
                for m in range(4):
                    project(l, f"zs{m}")
                    modulation(l, "gate", 4 + m)

                pe.wait_ge(p_ready, l * 3 + 1)
                for n in range(6):
                    if n == 2:
                        turn_modulation(l, "gate", 1)
                        pe.wait_ge(p_ready, l * 3 + 2)
                    job, kv = f"PT{n}", n % 2
                    pe.wait_ge(*work.room(l, job))
                    for i in range(NQ):
                        src = P0[:, kv, i, :] if n < 2 else P1[:, kv, i, (n // 2 - 1) * P:(n // 2) * P]
                        ins = nc.tensor.transpose(work.bank(job)[:, i * P:(i + 1) * P], src, ident)
                    ins.then_inc(work.filled(job), 1)
                for m in range(4):
                    unit = f"glu{m // 2}"
                    pe.wait_ge(used[slot_of(unit)], uses_at(l, unit))
                    pe.wait_ge(*proj.room(l, f"glu{m}"))
                    for k in range(MT):
                        if m == 0:
                            pe.wait_ge(yglo, l * MT + k + 1)
                        c0 = k * 2 * P + (m % 2) * P
                        ins = split_passes(proj.bank(f"glu{m}")[:, 0:TOK], unit, k, slice(c0, c0 + P), MT + k,
                                           k == 0, k == MT - 1)
                    ins.then_inc(proj.filled(f"glu{m}"), 1)

                pe.wait_ge(p_ready, l * 3 + 3)
                pe.wait_ge(*work.room(l, "PTc"))
                pe.wait_ge(*work.room(l, "PTn"))
                for kv in range(KV):
                    for hb in range(2):
                        x = kv * 2 + hb
                        ins = nc.tensor.transpose(work.bank("PTc")[:, x * P:(x + 1) * P], Ps[:, kv, hb, 0:WIN], ident)
                ins.then_inc(work.filled("PTc"), 1)
                for kv in range(KV):
                    for hb in range(2):
                        x = kv * 2 + hb
                        ins = nc.tensor.transpose(work.bank("PTn")[0:NS, x * P:(x + 1) * P], Ps[:, kv, hb, WIN:], ident)
                ins.then_inc(work.filled("PTn"), 1)
                for job, parts in (("pv0", ((0, 0),)), ("pv1", ((1, 0), (2, 1)))):
                    pe.wait_ge(*work.room(l, job))
                    for n, _ in parts:
                        for kv in range(KV):
                            pe.wait_ge(*work.taken(l, f"PT{2 * n + kv}"))
                    for kv in range(KV):
                        for x, (n, tile) in enumerate(parts):
                            ins = mm(work.bank(job)[kv * HD:(kv + 1) * HD, :], vtok[:, tile, kv * HD:(kv + 1) * HD],
                                     PT[:, n, kv, :], x == 0, x == len(parts) - 1)
                    ins.then_inc(work.filled(job), 1)
                pe.wait_ge(*work.room(l, "pvs"))
                pe.wait_ge(*work.taken(l, "PTc"))
                pe.wait_ge(*work.taken(l, "PTn"))
                pe.wait_ge(vcache_in, l * 16 + 16)
                for kv in range(KV):
                    cols = slice(kv * HD, (kv + 1) * HD)
                    for hb in range(2):
                        o = work.bank("pvs")[cols, hb * P:(hb + 1) * P]
                        for q in range(4):
                            mm(o[:, q * 32:(q + 1) * 32], vc[:, hb * 4 + q, cols],
                               PTc[:, kv, hb, q * 32:(q + 1) * 32], hb == 0 and q == 0, False, True)
                        ins = mm(o, vtok[0:NS, 2, cols], PTn[0:NS, kv, hb, :], False, True, True)
                ins.then_inc(work.filled("pvs"), 1)

                def project_out(m, tiles, first, last):
                    unit = f"out{m}"
                    if first:
                        pe.wait_ge(used_of(unit), uses_at(l, unit))
                        pe.wait_ge(*proj.room(l, unit))
                    for k in tiles:
                        if m == 0:
                            pe.wait_ge(mix_ready, l * 7 + (k - MT + 1 if k >= MT else 7))
                        ins = split_passes(proj.bank(unit)[:, 0:TOK], unit, k, slice(k * P, (k + 1) * P), k,
                                           first and k == tiles[0], last and k == tiles[-1])
                    if last:
                        ins.then_inc(proj.filled(unit), 1)

                for m in range(2):
                    project_out(m, range(MT, KT), True, False)
                for m in range(2):
                    project_out(m, range(MT), False, True)
                for m in range(2, 8):
                    project_out(m, range(KT), True, True)

            def outputs(half):
                for tile in range(3):
                    job, rows = f"yT{3 * half + tile}", P if tile < 2 else NS
                    ring = output_ring(3 * half + tile)
                    pe.wait_ge(*ring.room(DEPTH, job))
                    for q in range(4):
                        pe.wait_ge(yn_ready, 4 * half + q + 1)
                        ins = nc.tensor.transpose(ring.bank(job)[0:rows, q * P:(q + 1) * P],
                                                  xn[:, half * 4 + q, tile * P:tile * P + rows], ident)
                    ins.then_inc(ring.filled(job), 1)

            outputs(0)
            pe.wait_ge(*work.room(DEPTH, "rmsF"))
            pe.wait_ge(sq_added, (DEPTH + 1) * KT)
            for rows, tile, t0 in ((slice(0, P), 0, 0), (slice(0, P), 1, P), (slice(0, NS), 2, SEQ), (slice(NS, P), 2, SEQ)):
                ins = mm(work.bank("rmsF")[rows, tile:tile + 1], sqsum[:, t0:t0 + rows.stop - rows.start],
                         mean[:, 0:1], True, True)
            ins.then_inc(work.filled("rmsF"), 1)
            outputs(1)

        @block.scalar
        def _(act):
            step = Steps(act, act_step)
            fn = nc.scalar.activation

            act.dma_start(const[:, :], a["constants"][:, 0:C_SEL]).then_inc(const_in, 16)
            act.dma_start(xin[:, 0:2, :], a["x_prompt"][0].rearrange("(n p) d -> p n d", p=P)).then_inc(x_in, 16)
            act.dma_start(xin[0:NS, 2, :], a["x_sample"].rearrange("b t d -> (b t) d")).then_inc(x_in, 16)

            act.wait_ge(cond_in, 32)
            fn(cexp, crow, ACT.Tanh, scale=0.5).then_inc(silu_c, 1)
            def first_rows(tiles):
                for k in tiles:
                    act.wait_ge(*work.ready(0, f"xT{k}"))
                    fn(xT[:, k, :], work.bank(f"xT{k}")[:, 0:TOK], ACT.Copy).then_inc(work.emptied(f"xT{k}"), 1)
                    act.wait_ge(*work.taken(0, f"xT{k}"))
                    if k >= 2:
                        act.wait_ge(sq_added, k - 1)
                    fn(sq[:, k % 2, :], xT[:, k, :], ACT.Square).then_inc(sq_done, 1)

            first_rows((0, 1))
            act.wait_ge(ssm_exp, 1)
            fn(zz[:, 3, :], rowsT[:, P + 2 * W:P + 3 * W], ACT.Exp).then_inc(ssm_val, 1)
            first_rows((2, 3))
            act.wait_ge(ssm_exp, 2)
            fn(zz[:, 6, :], zz[:, 4, :], ACT.Exp).then_inc(ssm_val, 1)
            first_rows((4, 5, 6))
            act.wait_ge(ssm_exp, 3)
            fn(zz[:, 7, :], zz[:, 7, :], ACT.Sin).then_inc(ssm_val, 1)
            fn(zz[:, 8, :], zz[:, 8, :], ACT.Sin).then_inc(ssm_val, 1)
            first_rows((7,))
            for n in range(2):
                act.wait_ge(*proj.ready(0, f"BT{n}"))
                src = proj.bank(f"BT{n}")[:, :].rearrange("p (c w) -> p w c", c=8)
                for r in range(2):
                    dst = Bsb[:, :, r, :, n * 8:(n + 1) * 8]
                    ins = fn(dst, src[:, r * W:(r + 1) * W, :].rearrange("p (l i) c -> p l i c", l=DEPTH), ACT.Copy)
                    if r == 1:
                        ins.then_inc(proj.emptied(f"BT{n}"), 1)
                    else:
                        step.add(ins)
            for n in range(4):
                l, r = n // 2, n % 2
                act.wait_ge(*work.ready(0, f"CT{n}"))
                for h in range(2):
                    rows = slice(h * NST, (h + 1) * NST)
                    src = work.bank(f"CT{n}")[rows, :].rearrange("p (i h c) -> p i h c", h=2, c=GC)[:, :, h, :]
                    ins = fn(Csb[rows, l, r], src, ACT.Copy, scale=(-1.0 if r else 1.0))
                    if h == 1:
                        ins.then_inc(work.emptied(f"CT{n}"), 1)
                    else:
                        step.add(ins)
            step.wait()

            def hi_part(l, n):
                unit = SPLIT[n]
                act.wait_ge(loaded_of(unit), loads_at(l, unit))
                if n >= HL:
                    old = SPLIT[n - HL]
                    if old.startswith("glu"):
                        act.wait_ge(*proj.ready(l, f"glu{2 * int(old[3:]) + 1}"))
                    else:
                        act.wait_ge(*proj.ready(l, old))
                fn(w_hi[:, n % HL, :], place(unit), ACT.Copy).then_inc(hi_done, 1)

            def root(l, job, n=TOK):
                act.wait_ge(*work.ready(l, job))
                fn(rstd[:, 1, 0:n], work.bank(job)[:, 0:n], ACT.Identity, bias=epsb[:, 0:1])\
                    .then_inc(work.emptied(job), 1)
                act.wait_ge(*work.taken(l, job))
                step.add(fn(rstd[:, 0, 0:n], rstd[:, 1, 0:n], ACT.Ln))
                step.wait()
                fn(rstd[:, 0, 0:n], rstd[:, 0, 0:n], ACT.Exp, scale=-0.5).then_inc(rstd_raw, 1)

            act.wait_ge(mean_set, 3)
            def modulation_rows(l, c):
                act.wait_ge(*ada.ready(l, f"am{c}"))
                order = ADA_SS + ADA_GATE
                if c != order[0]:
                    act.wait_ge(*ada.ready(l, f"at{order[order.index(c) - 1]}"))
                fn(arow, ada.bank(f"am{c}")[:, :], ACT.Copy).then_inc(ada.emptied(f"am{c}"), 1)

            def fetch_table():
                step.add(fn(warm[:, 0:1], epsb[:, 0:1], ACT.Ln))

            fetch_table()
            with act.Fori(0, DEPTH) as l:
                step.restart()
                root(l, "rms")
                modulation_rows(l, ADA_SS[0])
                hi_part(l, 0)
                hi_part(l, 1)
                modulation_rows(l, ADA_SS[1])
                def turned_B(n):
                    act.wait_ge(*work.ready(l, f"WB{n}"))
                    src = work.bank(f"WB{n}")[:, :].rearrange("p (i q) -> p i q", i=4)
                    fn(WB[:, n // 2, n % 2], src, ACT.Copy)\
                        .then_inc(work.emptied(f"WB{n}"), 1)

                for pair in range(0, KT, 2):
                    if pair == 4:
                        modulation_rows(l, ADA_SS[2])
                        for n in TURNED_AFTER[11]:
                            turned_B(n)
                        modulation_rows(l, ADA_SS[3])
                    act.wait_ge(mod_ready, l * 6 + (2 if pair < 4 else 4))
                    for k in (pair, pair + 1):
                        act.wait_ge(norm_done, l * KT + k + 1)
                        if k >= 2:
                            act.wait_ge(h_ready, l * KT + k - 1)
                        fn(hf[:, k % 2, 0:SEQ], xn[:, k, 0:SEQ], ACT.Identity,
                           scale=mod[:, KT + k, 0:1], bias=mod[:, k, 0:1]).then_inc(hp_done, 1)
                    for k in (pair, pair + 1):
                        act.wait_ge(hs_done, l * KT + k + 1)
                        act.wait_ge(hp_done, l * KT + k + 1)
                        fn(h_hi[:, k, :], hf[:, k % 2, :], ACT.Copy).then_inc(hhi_done, 1)
                for n in TURNED_AFTER[15]:
                    turned_B(n)

                for m in range(4):
                    act.wait_ge(*proj.ready(l, f"u{m}"))
                    fn(u_sb[:, m], proj.bank(f"u{m}")[:, 0:TOK].rearrange("p (j t) -> p t j", t=T), ACT.Copy)\
                        .then_inc(proj.emptied(f"u{m}"), 1)
                    hi_part(l, m + 2)
                    act.wait_ge(*proj.taken(l, f"u{m}"))
                    act.dma_start(u_dram[m * 8:(m + 1) * 8].rearrange("g c t j -> (g c) (t j)"),
                                  u_sb[:, m].rearrange("p t j -> p (t j)")).then_inc(u_out, 16)

                def raw_rows(n, job):
                    act.wait_ge(*proj.ready(l, job))
                    if n >= 2:
                        act.wait_ge(*work.taken(l, f"rope{n - 2}"))
                    fn(qraw[:, n % 2, :], proj.bank(job)[:, 0:TOK], ACT.Copy).then_inc(proj.emptied(job), 1)

                for m in range(4):
                    raw_rows(m, f"q{m}")
                    hi_part(l, 6 + m)
                    for n in TURNED_AFTER[f"q{m}"]:
                        turned_B(n)
                    if m == 0:
                        act.wait_ge(u_out, (l + 1) * 64)
                        for t in range(T):
                            act.dma_start(U[t * GC:(t + 1) * GC], u_dram[:, :, t, :].rearrange("g c j -> c g j"))\
                                .then_inc(u_back, 16)
                for n in range(8):
                    job, r, q = f"S{n}", n % 2, n // 2
                    act.wait_ge(*work.ready(l, job))
                    for h in range(2):
                        rows = slice(h * NST, (h + 1) * NST)
                        src = work.bank(job)[rows, 0:4 * NPAIR].rearrange(
                            "p (i x) -> p i x", i=4)[:, :, h * J:(h + 1) * J]
                        ins = fn(Ssb[rows, r, 4 * q:4 * q + 4, :], src, ACT.Copy)
                        if h == 1:
                            ins.then_inc(work.emptied(job), 1)
                        else:
                            step.add(ins)
                for n in range(2):
                    act.wait_ge(*work.ready(l, f"kcT{n}"))
                    fn(kcT[:, 4 * n:4 * n + 4, :], work.bank(f"kcT{n}")[:, :].rearrange("p (b w) -> p b w", b=4),
                       ACT.Copy).then_inc(work.emptied(f"kcT{n}"), 1)
                for n in range(4):
                    act.wait_ge(*work.ready(l, f"K{n}"))
                    fn(Ksb[0:2 * GC, 4 * n:4 * n + 4, :],
                       work.bank(f"K{n}")[0:2 * GC, :].rearrange("p (i q) -> p i q", i=4), ACT.Copy)\
                        .then_inc(work.emptied(f"K{n}"), 1)
                raw_rows(4, "k")
                hi_part(l, 10)
                raw_rows(5, "v")
                hi_part(l, 11)
                act.wait_ge(*work.ready(l, "vT"))
                step.add(fn(vtok[:, 0:2, :], work.bank("vT")[:, 0:2 * P].rearrange("p (n q) -> p n q", n=2), ACT.Copy))
                fn(vtok[0:NS, 2, :], work.bank("vT")[0:NS, 2 * P:3 * P], ACT.Copy).then_inc(work.emptied("vT"), 1)
                def gate(n, job):
                    act.wait_ge(*proj.ready(l, job))
                    if n >= 2:
                        before = f"za{n - 2}" if n - 2 < 4 else f"zs{n - 6}"
                        act.wait_ge(*proj.taken(l, before))
                    fn(ez[:, n % 2, :], proj.bank(job)[:, 0:TOK], ACT.Tanh, scale=0.5).then_inc(gate_tanh, 1)

                own = bass.ds(l, 1)
                for m in range(2):
                    gate(m, f"za{m}")
                    hi_part(l, 12 + m)
                act.wait_ge(*work.ready(l, "ktok"))
                step.add(fn(ktok[:, 0, :], work.bank("ktok")[:, 0:P], ACT.Copy))
                fn(ktok[0:NS, 1, :], work.bank("ktok")[0:NS, P:2 * P], ACT.Copy).then_inc(work.emptied("ktok"), 1)
                step.wait()
                act.wait_ge(*work.taken(l, "ktok"))
                for prompt, sample, src, new in ((out[2], out[6], ktok, 1), (out[3], out[7], vtok, 2)):
                    act.dma_start(prompt[own].rearrange("o b w v d -> (o b w) (v d)"), src[:, new - 1, :])\
                        .then_inc(kv_stored, 16)
                    act.dma_start(sample[own, :, WIN - T:WIN].rearrange("o b t v d -> (o b) t (v d)"),
                                  src[0:NS, new, :]).then_inc(kv_stored, 16)

                for m in range(2, 4):
                    gate(m, f"za{m}")
                    hi_part(l, 12 + m)
                modulation_rows(l, 4)
                def exponentials(g):
                    buf, n = ((P0, NQ), (P1, NQ), (Ps, 2))[g]
                    act.wait_ge(max_ready, l * 3 + g + 1)
                    for v in range(KV):
                        for i in range(n):
                            x = v * n + i
                            fn(buf[:, v, i, :], buf[:, v, i, :], ACT.Exp, scale=SCALE, bias=sm[:, g, 1, x:x + 1],
                               accum_out=sm[:, g, 2, x:x + 1])
                    fn(sm[:, g, 3, 0:KV * n], sm[:, g, 3, 0:KV * n], ACT.Exp).then_inc(p_exp, 1)

                exponentials(0)
                act.wait_ge(fin_ready, l + 1)
                for n in range(4):
                    act.wait_ge(*work.ready(l, f"y{n}"))
                    src = work.bank(f"y{n}")[:, 0:4 * NPAIR].rearrange("p (q x) -> p q x", q=4)[:, :, 0:2 * J]
                    fn(Ysb[:, 8 * n:8 * n + 8, :].rearrange("p (q h) j -> p q (h j)", h=2), src, ACT.Copy)\
                        .then_inc(work.emptied(f"y{n}"), 1)
                for n in range(4):
                    act.wait_ge(*work.taken(l, f"y{n}"))
                for t in range(T):
                    act.dma_start(y_dram[:, :, t, :].rearrange("g c j -> c g j"), Ysb[t * GC:(t + 1) * GC])\
                        .then_inc(y_out, 16)
                act.wait_ge(*work.ready(l, "state"))
                step.add(fn(stage[:, 0:2, :], work.bank("state")[:, 0:2 * P].rearrange("p (r q) -> p r q", r=2), ACT.Copy))
                fn(stage[0:NI, 2:4, :], work.bank("state")[0:NI, 2 * P:4 * P].rearrange("p (r q) -> p r q", r=2),
                   ACT.Copy).then_inc(work.emptied("state"), 1)
                step.wait()
                act.wait_ge(*work.taken(l, "state"))
                for r in range(2):
                    act.dma_start(out[8 + r][own].rearrange("o b (i h) p -> (o b i) (h p)", h=2), stage[:, r, :])\
                        .then_inc(state_stored, 16)
                    act.dma_start(out[4 + r][own].rearrange("o b (i h) p -> (o b i) (h p)", h=2), stage[0:NI, 2 + r, :])\
                        .then_inc(state_stored, 16)
                act.wait_ge(y_out, (l + 1) * 128)
                act.wait_ge(skew_in, (l + 1) * 2 * T * 16)
                for m in range(MT):
                    act.dma_start(ycp[:, m, :], y_dram[m * 8:(m + 1) * 8].rearrange("g c t j -> (g c) (t j)"))\
                        .then_inc(y_back, 16)

                def gelu_square(m):
                    act.wait_ge(y1_ready, l * MT + m + 1)
                    if m >= 2:
                        act.wait_ge(yg_ready, l * MT + m - 1)
                    fn(ge[:, m % 2, :], ycp[:, m, :], ACT.Square).then_inc(y_sq, 1)

                def gelu_tanh(m):
                    act.wait_ge(y_arg, l * MT + m + 1)
                    fn(ge[:, m % 2, :], ge[:, m % 2, :], ACT.Tanh, scale=GELU_B).then_inc(y_tanh, 1)

                def gelu_hi(m):
                    act.wait_ge(yg_ready, l * MT + m + 1)
                    fn(h_hi[:, MT + m, :], yg[:, m, :], ACT.Copy, scale=0.5).then_inc(yghi, 1)

                def turned_probabilities(n):
                    act.wait_ge(*work.ready(l, f"PT{n}"))
                    fn(PT[:, n // 2, n % 2, :], work.bank(f"PT{n}")[:, :], ACT.Copy)\
                        .then_inc(work.emptied(f"PT{n}"), 1)

                exponentials(1)
                gate(4, "zs0")
                hi_part(l, 16)
                gelu_square(0)
                gelu_square(1)
                gate(5, "zs1")
                hi_part(l, 17)
                exponentials(2)
                gelu_tanh(0)
                gelu_tanh(1)
                gate(6, "zs2")
                hi_part(l, 18)
                gelu_square(2)
                gelu_square(3)
                gate(7, "zs3")
                gelu_hi(0)
                gelu_hi(1)
                act.wait_ge(state_stored, (l + 1) * 64)
                modulation_rows(l, 5)
                for n in range(2):
                    turned_probabilities(n)
                gelu_tanh(2)
                gelu_tanh(3)
                gelu_hi(2)
                gelu_hi(3)
                hi_part(l, 19)
                for n in range(2, 6):
                    turned_probabilities(n)

                for pair in ((0, 1), (2, 3)):
                    for m in pair:
                        act.wait_ge(*proj.ready(l, f"glu{m}"))
                        if m < 2:
                            act.wait_ge(*proj.taken(l, f"zs{2 + m}"))
                        else:
                            act.wait_ge(gated, l * MT + m - 1)
                        fn(ez[:, m % 2, :], proj.bank(f"glu{m}")[:, 0:TOK], ACT.Tanh, scale=0.5,
                           bias=hbglu[:, m:m + 1]).then_inc(proj.emptied(f"glu{m}"), 1)
                    if pair[0] == 2:
                        act.wait_ge(*work.ready(l, "PTc"))
                        fn(PTc, work.bank("PTc")[:, :].rearrange("p (v b q) -> p v b q", v=KV, b=2), ACT.Copy)\
                            .then_inc(work.emptied("PTc"), 1)
                        act.wait_ge(*work.ready(l, "PTn"))
                        fn(PTn[0:NS], work.bank("PTn")[0:NS, :].rearrange("p (v b q) -> p v b q", v=KV, b=2), ACT.Copy)\
                            .then_inc(work.emptied("PTn"), 1)
                    if pair[0] == 0:
                        hi_part(l, 20)
                for m in range(MT):
                    act.wait_ge(gated, l * MT + m + 1)
                    fn(h_hi[:, MT + m, :], gs[:, m, :], ACT.Copy, scale=0.125).then_inc(mixhi, 1)
                hi_part(l, 21)
                for job, toks in (("pv0", slice(0, P)), ("pv1", slice(P, SEQ)), ("pvs", slice(SEQ, TOK))):
                    act.wait_ge(*work.taken(l, job))
                    fn(h_hi[:, 0:MT, toks], ga[:, :, toks], ACT.Copy, scale=0.5).then_inc(mixhi, 1)

                for m in range(8):
                    if m < 6:
                        hi_part(l, 22 + m)
                    if m == 7:
                        fetch_table()
                    act.wait_ge(x_ready, l * KT + m + 1)
                    if m >= 2:
                        act.wait_ge(sq_added, (l + 1) * KT + m - 1)
                    fn(sq[:, m % 2, :], xT[:, m, :], ACT.Square).then_inc(sq_done, 1)
                act.wait_ge(kv_stored, (l + 1) * 64)
                step.wait()

            step.restart()
            root(DEPTH, "rmsF", 3)
            act.wait_ge(rstd_done, 1)
            for half in range(2):
                cols = slice(half * 512, (half + 1) * 512)
                for tile in range(3):
                    n, rows = 3 * half + tile, P if tile < 2 else NS
                    if n % 2 == 0:
                        ring = output_ring(n)
                        act.wait_ge(*ring.ready(DEPTH, f"yT{n}"))
                        fn(ybuf[0:rows, tile, cols], ring.bank(f"yT{n}")[0:rows, :], ACT.Copy,
                           scale=rstd[0:rows, 0, tile:tile + 1]).then_inc(ring.emptied(f"yT{n}"), 1)
                for n in range(3 * half, 3 * half + 3):
                    act.wait_ge(*output_ring(n).taken(DEPTH, f"yT{n}"))
                act.dma_start(out[0][0].rearrange("(n p) d -> p n d", p=P)[:, :, cols], ybuf[:, 0:2, cols])\
                    .then_inc(y_stored, 16)
                act.dma_start(out[1].rearrange("b t d -> (b t) d")[:, cols], ybuf[0:NS, 2, cols]).then_inc(y_stored, 16)
            act.wait_ge(y_stored, 64)

        @block.vector
        def _(dve):
            step = Steps(dve, dve_step)
            v = nc.vector
            tt, ts, stt, cp = v.tensor_tensor, v.tensor_scalar, v.scalar_tensor_tensor, v.tensor_copy

            def own(ins):
                step.add(ins)
                step.wait()

            v.memset(mean[:, :], 1.0 / D).then_inc(mean_set, 1)
            v.memset(epsb[:, :], EPS).then_inc(mean_set, 1)
            v.memset(cT[:, :, CT:], 0.0).then_inc(mean_set, 1)
            step.add(v.memset(Apow[:, :, 0, :, 0:1], 1.0))
            step.add(v.memset(Apow[:, :, 1, :, 0:1], 0.0))
            dve.wait_ge(silu_c, 1)
            stt(cexp, cexp, 1.0, crow, ALU.add, ALU.mult).then_inc(silu_r, 1)
            dve.wait_ge(small_in, 16 * 8)
            cp(rowsS[2 * W:3 * W, :].rearrange("p (h q) -> p h q", h=2),
               ldt.unsqueeze(2).to_broadcast([W, 2, NST])).then_inc(ldt_wide, 1)
            dve.wait_ge(*work.ready(0, "cT"))
            ts(cT[:, :, 0:CT], work.bank("cT")[:, 0:KT * CT].rearrange("p (k c) -> p k c", c=CT), 0.5, None, ALU.mult)\
                .then_inc(work.emptied("cT"), 1)
            dve.wait_ge(*work.ready(0, "rowsT"))
            step.add(cp(rowsT[:, 0:R_END], work.bank("rowsT")[:, 0:R_END]))
            cp(rowsT[:, P:P + 3 * W], work.bank("rowsT")[:, P:P + 3 * W]).then_inc(work.emptied("rowsT"), 1)
            step.wait()
            dve.wait_ge(*work.taken(0, "rowsT"))
            for s0, n, r0 in ((S_G, KT, R_G), (S_BADA, 3 * KT, R_BADA), (S_BGLU, MT, R_BGLU), (S_D, MT, R_D)):
                step.add(cp(small[:, :, s0:s0 + n], rowsT[:, r0:r0 + DEPTH * n].rearrange("p (l r) -> p l r", l=DEPTH)))
            step.add(cp(fing[:, :], rowsT[:, R_FIN:R_END]))

            def add_square(n, done):
                dve.wait_ge(sq_done, done)
                if n:
                    dve.wait_ge(sq_added, done - 1)
                    tt(sqsum[:, :], sqsum[:, :], sq[:, n % 2, :], ALU.add).then_inc(sq_added, 1)
                else:
                    cp(sqsum[:, :], sq[:, 0, :]).then_inc(sq_added, 1)

            a_re, a_im = rowsT[:, P:P + W], rowsT[:, P + W:P + 2 * W]
            dt_, ard, th, mag, rs, rc = (zz[:, n, :] for n in (3, 4, 5, 6, 7, 8))
            k1, k2, t1, t2, den, nr = (zz[:, n, :] for n in (9, 10, 11, 12, 13, 14))
            dve.wait_ge(*work.taken(0, "rowsT"))
            step.wait()
            cp(zz[:, 0, :], a_re).then_inc(ssm_exp, 1)
            dve.wait_ge(ssm_val, 1)
            own(tt(th, a_im, dt_, ALU.mult))
            tt(ard, a_re, dt_, ALU.mult).then_inc(ssm_exp, 1)
            own(ts(k1, th, 1.0 / TWO_PI, ROUND, ALU.mult, ALU.add))
            own(ts(k1, k1, -ROUND, None, ALU.add))
            own(ts(k2, th, 1.0 / TWO_PI, 0.25, ALU.mult, ALU.add))
            own(ts(k2, k2, ROUND, None, ALU.add))
            own(ts(k2, k2, -ROUND, None, ALU.add))
            for r, k in ((rs, k1), (rc, k2)):
                own(stt(r, k, -PI_1, th, ALU.mult, ALU.add))
                own(stt(r, k, -PI_2, r, ALU.mult, ALU.add))
                own(stt(r, k, -PI_3, r, ALU.mult, ALU.add))
            own(ts(rs, rs, PI_SAFE, -PI_SAFE, ALU.min, ALU.max))
            own(ts(rc, rc, TWO_PI / 4, PI_SAFE, ALU.add, ALU.min))
            ts(rc, rc, -PI_SAFE, None, ALU.max).then_inc(ssm_exp, 1)
            own(tt(t1, a_re, a_re, ALU.mult))
            own(tt(t2, a_im, a_im, ALU.mult))
            own(tt(den, t1, t2, ALU.add))
            own(v.reciprocal(den, den))
            dve.wait_ge(*ada.ready(0, "sinks"))
            cp(small[:, :, S_SINKS:S_SINKS + KV],
               ada.bank("sinks")[:, 0:DEPTH * KV].rearrange("p (l s) -> p l s", l=DEPTH))\
                .then_inc(ada.emptied("sinks"), 1)
            dve.wait_ge(*ada.taken(0, "sinks"))
            dve.wait_ge(ssm_val, 4)

            def power(r, n0, n1):
                return Apow[:, :, r, :, n0:n1]

            def flat(x):
                return x.rearrange("p (l i) -> p l i", l=DEPTH).unsqueeze(3)

            ar, ai = power(0, 1, 2), power(1, 1, 2)
            own(tt(ar, flat(mag), flat(rc), ALU.mult))
            own(tt(ai, flat(mag), flat(rs), ALU.mult))
            own(ts(flat(nr), ar, -1.0, None, ALU.add))
            own(tt(t1, nr, a_re, ALU.mult))
            own(tt(flat(t2), ai, flat(a_im), ALU.mult))
            own(tt(t1, t1, t2, ALU.add))
            own(tt(coef[:, :, 0, :].unsqueeze(3), flat(t1), flat(den), ALU.mult))
            own(tt(flat(t1), ai, flat(a_re), ALU.mult))
            own(tt(t2, nr, a_im, ALU.mult))
            own(tt(t1, t1, t2, ALU.subtract))
            own(tt(coef[:, :, 1, :].unsqueeze(3), flat(t1), flat(den), ALU.mult))
            for n in (1, 2, 4):
                q = [zz[:, 3 + 4 * x:3 + 4 * x + n, :].rearrange("p n w -> p (n w)").rearrange(
                    "p (l i n) -> p l i n", l=DEPTH, i=NI) for x in range(2)]
                base = [power(r, n, n + 1).to_broadcast([P, DEPTH, NI, n]) for r in range(2)]
                low = [power(r, 1, n + 1) for r in range(2)]
                for r in range(2):
                    step.add(tt(q[0], low[0], base[r], ALU.mult))
                    own(tt(q[1], low[1], base[1 - r], ALU.mult))
                    own(tt(power(r, n + 1, 2 * n + 1), q[0], q[1], ALU.add if r else ALU.subtract))
            sv = small[:, :, :]
            A8 = [power(r, T, T + 1).rearrange("p l i o -> p l (i o)") for r in range(2)]
            step.add(cp(sv[:, :, S_A8R:S_A8R + NI], A8[0]))
            step.add(ts(sv[:, :, S_A8I:S_A8I + NI], A8[1], -1.0, None, ALU.mult))
            step.add(cp(sv[:, :, S_A8I + NI:S_A8I + 2 * NI], A8[1]))
            q = [x.rearrange("p (l i) -> p l i", l=DEPTH) for x in (t1, t2)]
            step.add(tt(q[0], A8[0], A8[0], ALU.mult))
            own(tt(q[1], A8[1], A8[1], ALU.mult))
            own(tt(sv[:, :, S_A16R:S_A16R + NI], q[0], q[1], ALU.subtract))
            own(tt(q[0], A8[0], A8[1], ALU.mult))
            step.add(ts(sv[:, :, S_A16I:S_A16I + NI], q[0], -2.0, None, ALU.mult))
            step.add(ts(sv[:, :, S_A16I + NI:S_A16I + 2 * NI], q[0], 2.0, None, ALU.mult))
            step.wait()
            cp(zz[:, 0, 0:1], zz[:, 0, 1:2]).then_inc(ssm_ready, 1)


            def newton(n, width=TOK):
                r, ms, t = rstd[:, 0, 0:width], rstd[:, 1, 0:width], sqsum[:, 0:width]
                dve.wait_ge(rstd_raw, n)
                own(tt(t, r, r, ALU.mult))
                own(tt(t, t, ms, ALU.mult))
                own(ts(t, t, -0.5, 1.5, ALU.mult, ALU.add))
                return tt(r, r, t, ALU.mult)

            def lo_part(l, n):
                unit = SPLIT[n]
                dve.wait_ge(hi_done, l * len(SPLIT) + n + 1)
                tt(w_lo[:, n % HL, :], place(unit), w_hi[:, n % HL, :].bitcast(F32), ALU.subtract)\
                    .then_inc(used_of(unit), 1)

            def samples(ap):
                return ap[..., SEQ:TOK].rearrange("p (b t) -> p b t", b=NB)

            def per_sample(m):
                return mod[:, m, 1:CT].unsqueeze(2).to_broadcast([P, NB, T])

            def modulation_of(l, x):
                c = (ADA_SS + ADA_GATE)[x]
                dst = mod[:, 4 * c:4 * c + 4, :]
                dve.wait_ge(*ada.ready(l, f"at{c}"))
                src = ada.bank(f"at{c}")[:, :].rearrange("p (q j c) -> p q c j", j=4, c=AROW)[:, :, 0:CT, :]
                v.tensor_reduce(dst, src, AX.X, ALU.add).then_inc(ada.emptied(f"at{c}"), 1)
                dve.wait_ge(*ada.taken(l, f"at{c}"))
                bias = cur[:, S_BADA + 4 * c:S_BADA + 4 * c + 4].unsqueeze(2).to_broadcast([P, 4, CT])
                if c in (2, 3):
                    own(tt(dst, dst, bias, ALU.add))
                    g = cur[:, S_G + 4 * (c - 2):S_G + 4 * (c - 1)].unsqueeze(2).to_broadcast([P, 4, CT])
                    stt(dst, dst, 1.0, g, ALU.add, ALU.mult).then_inc(mod_ready, 1)
                else:
                    tt(dst, dst, bias, ALU.add).then_inc(mod_ready, 1)

            dve.wait_ge(sinks_in, 48)
            with dve.Fori(0, DEPTH) as l:
                step.restart()
                own(cp(cur[:, :], small[:, bass.ds(l, 1), :].rearrange("p o s -> p (o s)")))
                step.add(ts(hbglu[:, :], cur[:, S_BGLU:S_BGLU + MT], 0.5, None, ALU.mult))
                step.wait()
                def normed(tiles):
                    for k in tiles:
                        tt(xn[:, k, :], xT[:, k, :], rstd[:, 0, :], ALU.mult).then_inc(norm_done, 1)

                own(newton(l + 1))
                modulation_of(l, 0)
                normed(range(4))
                lo_part(l, 0)
                modulation_of(l, 1)
                lo_part(l, 1)
                for pair in range(0, KT, 2):
                    if pair == 4:
                        normed(range(4, KT))
                        modulation_of(l, 2)
                        modulation_of(l, 3)
                    tiles = (pair, pair + 1)
                    dve.wait_ge(mod_ready, l * 6 + (2 if pair < 4 else 4))
                    for k in tiles:
                        dve.wait_ge(norm_done, l * KT + k + 1)
                        if k >= 2:
                            dve.wait_ge(h_ready, l * KT + k - 1)
                        step.add(tt(samples(hf[:, k % 2, :]), samples(xn[:, k, :]), per_sample(KT + k), ALU.mult))
                    step.wait()
                    for k in tiles:
                        tt(samples(hf[:, k % 2, :]), samples(hf[:, k % 2, :]), per_sample(k), ALU.add)\
                            .then_inc(hs_done, 1)
                    for k in tiles:
                        dve.wait_ge(hhi_done, l * KT + k + 1)
                        tt(h_lo[:, k, :], hf[:, k % 2, :], h_hi[:, k, :].bitcast(F32), ALU.subtract)\
                            .then_inc(h_ready, 1)
                for m in range(4):
                    lo_part(l, m + 2)

                def rope(n):
                    job = f"rope{n}"
                    if n:
                        dve.wait_ge(*work.taken(l, f"rope{n - 1}"))
                    dve.wait_ge(*proj.taken(l, f"q{n}" if n < 4 else "k"))
                    step.add(tt(rt[:, 0, :], qraw[:, n % 2, :], cos, ALU.mult))
                    dve.wait_ge(*work.ready(l, job))
                    own(tt(rt[:, 1, :], work.bank(job)[:, 0:TOK], sin, ALU.mult))
                    if n < 4:
                        step.add(tt(qT[:, n, :], rt[:, 0, 0:SEQ], rt[:, 1, 0:SEQ], ALU.add))
                        tt(qs[:, :, n, :], samples(rt[:, 0, :]), samples(rt[:, 1, :]), ALU.add)\
                            .then_inc(work.emptied(job), 1)
                    else:
                        tt(kT[:, :], rt[:, 0, :], rt[:, 1, :], ALU.add).then_inc(work.emptied(job), 1)

                lo_part(l, 6)
                for m in range(3):
                    if m < 2:
                        lo_part(l, 7 + m)
                    else:
                        dve.wait_ge(*work.ready(l, "h0"))
                        cp(Hst[:, :, :, JP:J], work.bank("h0")[:, 0:2 * P].rearrange(
                            "p (r b i) -> p r i b", r=2, b=NB)).then_inc(work.emptied("h0"), 1)
                    rope(m)
                lo_part(l, 9)
                step.add(v.memset(Hst[:, :, :, 0:1], 0.0))
                for h in range(2):
                    step.add(v.memset(Hblk[h * NST:(h + 1) * NST, :, :, 1 - h, :], 0.0))
                dve.wait_ge(*work.taken(l, "h0"))
                dve.wait_ge(*work.taken(l, "S7"))
                step.wait()

                def wide_of(s0, n, shape):
                    re = cur[:, s0:s0 + NI].unsqueeze(1).unsqueeze(3).to_broadcast(shape)
                    im = cur[:, s0 + NI:s0 + 3 * NI].rearrange("p (r i) -> p r i", r=2).unsqueeze(3)\
                        .to_broadcast(shape)
                    return re, im

                half = [P, 2, NI, JP // 2]
                a8, a8i = wide_of(S_A8R, JP // 2, half)
                even, odd = Ssb[:, :, :, 0:JP:2], Ssb[:, :, :, 1:JP:2]
                step.add(tt(wide, even, a8, ALU.mult))
                own(tt(prod, Ssb[:, ::-1, :, 0:JP:2], a8i, ALU.mult))
                own(tt(wide, wide, odd, ALU.add))
                own(tt(wide, wide, prod, ALU.add))

                def silu(n, job, dst):
                    dve.wait_ge(gate_tanh, l * 8 + n + 1)
                    stt(dst, ez[:, n % 2, :], 1.0, proj.bank(job)[:, 0:TOK], ALU.add, ALU.mult)\
                        .then_inc(proj.emptied(job), 1)

                one = [P, 2, NI]
                a16 = cur[:, S_A16R:S_A16R + NI].unsqueeze(1).to_broadcast(one)
                a16i = cur[:, S_A16I:S_A16I + 2 * NI].rearrange("p (r i) -> p r i", r=2)
                own(cp(Hst[:, :, :, 2], wide[:, :, :, 0]))
                lo_part(l, 10)
                rope(3)
                for k in range(1, JP // 2):
                    H = Hst[:, :, :, 2 * k]
                    last = k == JP // 2 - 1
                    step.add(tt(rec[:, 0], H, a16, ALU.mult))
                    step.add(tt(rec[:, 1], Hst[:, ::-1, :, 2 * k], a16i, ALU.mult))
                    step.wait()
                    own(tt(rec[:, 0], rec[:, 0], wide[:, :, :, k], ALU.add))
                    own(tt(fin[:, :, 0, :] if last else Hst[:, :, :, 2 * k + 2], rec[:, 0], rec[:, 1], ALU.add))
                    if k == 3:
                        lo_part(l, 11)
                        rope(4)
                    if k in GATES_AT:
                        n = GATES_AT.index(k)
                        silu(n, f"za{n}", ga[:, n, :])
                        lo_part(l, 12 + n)
                step.add(tt(Hst[:, :, :, 1:JP:2], Hst[:, :, :, 0:JP:2], a8, ALU.mult))
                own(tt(prod, Hst[:, ::-1, :, 0:JP:2], a8i, ALU.mult))
                own(tt(Hst[:, :, :, 1:JP:2], Hst[:, :, :, 1:JP:2], even, ALU.add))
                own(tt(Hst[:, :, :, 1:JP:2], Hst[:, :, :, 1:JP:2], prod, ALU.add))
                for h in range(2):
                    rows = slice(h * NST, (h + 1) * NST)
                    cp(Hblk[rows, :, :, h, :], Hst[rows]).then_inc(H_ready, 1)
                b8, b8i = wide_of(S_A8R, NB, [P, 2, NI, NB])
                part = [x[:, :, :, 0:NB] for x in (wide, prod)]
                step.add(tt(part[0], Hst[:, :, :, JP:J], b8, ALU.mult))
                own(tt(part[1], Hst[:, ::-1, :, JP:J], b8i, ALU.mult))
                own(tt(part[0], part[0], Ssb[:, :, :, JP:J], ALU.add))
                tt(fin[:, :, 1:1 + NB, :].rearrange("p r b i -> p r i b"), part[0], part[1], ALU.add)\
                    .then_inc(fin_ready, 1)
                for n in (2, 3):
                    silu(n, f"za{n}", ga[:, n, :])
                    lo_part(l, 12 + n)
                def masked(job, dst, mask, n):
                    dve.wait_ge(*work.ready(l, job))
                    src = work.bank(job)[:, 0:n * dst.shape[2]].rearrange("p (i k) -> p i k", i=n)
                    tt(dst, src, mask, ALU.add).then_inc(work.emptied(job), 1)

                def maximum(g):
                    buf, n = ((P0, NQ), (P1, NQ), (Ps, 2))[g]
                    job = ("sc01", "sc13", "ss1")[g]
                    dve.wait_ge(*work.taken(l, job))
                    x = KV * n
                    sink = (cur[:, S_SINKP:S_SINKP + 8] if g < 2
                            else cur[:, S_SINKS:S_SINKS + KV].unsqueeze(2).to_broadcast([P, KV, 2]))
                    s = [sm[:, g, q, 0:x] if g < 2 else sm[:, g, q, 0:x].rearrange("p (v b) -> p v b", v=KV)
                         for q in range(5)]
                    own(v.tensor_reduce(sm[:, g, 0, 0:x].rearrange("p (v i) -> p v i", v=KV), buf, AX.X, ALU.max))
                    own(stt(s[0], s[0], SCALE, sink, ALU.mult, ALU.max))
                    own(ts(s[1], s[0], -1.0, None, ALU.mult))
                    tt(s[3], sink, s[0], ALU.subtract).then_inc(max_ready, 1)

                def normalize(g):
                    buf, n = ((P0, NQ), (P1, NQ), (Ps, 2))[g]
                    x = KV * n
                    dve.wait_ge(p_exp, l * 3 + g + 1)
                    own(tt(sm[:, g, 2, 0:x], sm[:, g, 2, 0:x], sm[:, g, 3, 0:x], ALU.add))
                    own(v.reciprocal(sm[:, g, 4, 0:x], sm[:, g, 2, 0:x]))
                    r = sm[:, g, 4, 0:x].rearrange("p (v i) -> p v i", v=KV).unsqueeze(3)\
                        .to_broadcast([P, KV, n, buf.shape[3]])
                    tt(buf, buf, r, ALU.mult).then_inc(p_ready, 1)

                dve.wait_ge(fin_ready, l + 1)
                for kv in range(KV):
                    masked(f"sc0{kv}", P0[:, kv], const[:, C_MP + P:C_MP + 2 * P].unsqueeze(1).to_broadcast([P, NQ, P]), NQ)
                maximum(0)
                modulation_of(l, 4)

                for n in range(4):
                    masked(f"sc1{n}", P1[:, n // 2, 2 * (n % 2):2 * (n % 2) + 2],
                           const[:, C_MP:C_MP + 2 * P].unsqueeze(1).to_broadcast([P, 2, 2 * P]), 2)
                maximum(1)
                for kv in range(KV):
                    masked(f"ss{kv}", Ps[:, kv],
                           const[:, C_MS:C_MS + 2 * (WIN + NS)].rearrange("p (b k) -> p b k", b=2), 2)
                maximum(2)

                def gelu_argument(m):
                    e = ge[:, m % 2, :]
                    dve.wait_ge(y_sq, l * MT + m + 1)
                    own(ts(e, e, GELU_A, 1.0, ALU.mult, ALU.add))
                    tt(e, e, ycp[:, m, :], ALU.mult).then_inc(y_arg, 1)

                def gelu_product(m):
                    dve.wait_ge(y_tanh, l * MT + m + 1)
                    stt(yg[:, m, :], ge[:, m % 2, :], 1.0, ycp[:, m, :], ALU.add, ALU.mult).then_inc(yg_ready, 1)

                def gelu_lo(m):
                    dve.wait_ge(yghi, l * MT + m + 1)
                    stt(h_lo[:, MT + m, :], yg[:, m, :], 0.5, h_hi[:, MT + m, :].bitcast(F32), ALU.mult,
                        ALU.subtract).then_inc(yglo, 1)

                silu(4, "zs0", gs[:, 0, :])
                lo_part(l, 16)
                dve.wait_ge(y_back, (l + 1) * 64)
                dve.wait_ge(kv_stored, (l + 1) * 64)
                for m in range(MT):
                    stt(ycp[:, m, :], u_sb[:, m].rearrange("p t j -> p (t j)"), cur[:, S_D + m:S_D + m + 1],
                        ycp[:, m, :], ALU.mult, ALU.add).then_inc(y1_ready, 1)
                dve.wait_ge(y1_ready, (l + 1) * MT)
                gelu_argument(0)
                gelu_argument(1)
                silu(5, "zs1", gs[:, 1, :])
                lo_part(l, 17)
                normalize(0)
                gelu_product(0)
                gelu_product(1)
                silu(6, "zs2", gs[:, 2, :])
                lo_part(l, 18)
                normalize(1)
                gelu_argument(2)
                gelu_argument(3)
                silu(7, "zs3", gs[:, 3, :])
                gelu_lo(0)
                gelu_lo(1)
                gelu_product(2)
                gelu_product(3)
                gelu_lo(2)
                gelu_lo(3)
                lo_part(l, 19)
                normalize(2)

                for pair in ((0, 1), (2, 3)):
                    for m in pair:
                        e = ez[:, m % 2, :]
                        dve.wait_ge(*proj.taken(l, f"glu{m}"))
                        own(stt(e, e, 1.0, yg[:, m, :], ALU.add, ALU.mult))
                        dst = gs[:, m, :].rearrange("p (j t) -> p t j", t=T)
                        tt(dst, dst, e.rearrange("p (t j) -> p t j", t=T), ALU.mult).then_inc(gated, 1)
                    if pair[0] == 0:
                        lo_part(l, 20)
                for m in range(MT):
                    dve.wait_ge(mixhi, l * 7 + 1 + m)
                    stt(h_lo[:, MT + m, :], gs[:, m, :], 0.125, h_hi[:, MT + m, :].bitcast(F32), ALU.mult, ALU.subtract)\
                        .then_inc(mix_ready, 1)

                heads = (("pv0", slice(0, P)), ("pv1", slice(P, SEQ)), ("pvs", slice(SEQ, TOK)))
                for job, toks in heads:
                    dve.wait_ge(*work.ready(l, job))
                    if job != "pvs":
                        tt(ga[:, :, toks], work.bank(job)[:, :].rearrange("p (i q) -> p i q", i=NQ), ga[:, :, toks],
                           ALU.mult).then_inc(work.emptied(job), 1)
                    else:
                        g4 = ga[:, :, toks].rearrange("p i (b t) -> p i b t", b=NB)
                        tt(g4, work.bank(job)[:, 0:NS * NQ].rearrange("p (b i t) -> p i b t", b=NB, i=NQ), g4,
                           ALU.mult).then_inc(work.emptied(job), 1)
                lo_part(l, 21)
                for n, (job, toks) in enumerate(heads):
                    dve.wait_ge(*work.taken(l, job))
                    dve.wait_ge(mixhi, l * 7 + 4 + n + 1)
                    stt(h_lo[:, 0:MT, toks], ga[:, :, toks], 0.5, h_hi[:, 0:MT, toks].bitcast(F32), ALU.mult,
                        ALU.subtract).then_inc(mix_ready, 1)

                modulation_of(l, 5)
                dve.wait_ge(mod_ready, (l + 1) * 6)
                for m in range(8):
                    job = f"out{m}"
                    dve.wait_ge(*proj.ready(l, job))
                    b = proj.bank(job)
                    step.add(stt(xT[:, m, 0:SEQ], b[:, 0:SEQ], mod[:, 2 * KT + m, 0:1], xT[:, m, 0:SEQ],
                                 ALU.mult, ALU.add))
                    if m:
                        dve.wait_ge(x_ready, l * KT + m)
                    tt(rt[:, 0, 0:NS].rearrange("p (b t) -> p b t", b=NB), samples(b[:, 0:TOK]),
                       per_sample(2 * KT + m), ALU.mult).then_inc(proj.emptied(job), 1)
                    dve.wait_ge(*proj.taken(l, job))
                    tt(xT[:, m, SEQ:TOK], xT[:, m, SEQ:TOK], rt[:, 0, 0:NS], ALU.add).then_inc(x_ready, 1)
                    if m < 6:
                        lo_part(l, 22 + m)
                    if m:
                        add_square(m - 1, (l + 1) * KT + m)
                add_square(KT - 1, (l + 1) * KT + KT)

            step.restart()
            newton(DEPTH + 1, 3).then_inc(rstd_done, 1)
            dve.wait_ge(rstd_done, 1)
            for n in (1, 3, 5):
                half, tile, rows = n // 3, n % 3, P if n % 3 < 2 else NS
                ring = output_ring(n)
                dve.wait_ge(*ring.ready(DEPTH, f"yT{n}"))
                ts(ybuf[0:rows, tile, half * 512:(half + 1) * 512], ring.bank(f"yT{n}")[0:rows, :],
                   rstd[0:rows, 0, tile:tile + 1], None, ALU.mult).then_inc(ring.emptied(f"yT{n}"), 1)

        @block.gpsimd
        def _(pool):
            step = Steps(pool, pool_step)
            tt = nc.gpsimd.tensor_tensor

            def own(ins):
                step.add(ins)
                step.wait()

            nc.gpsimd.memset(Bblk[:, :, :, :, :], 0.0).then_inc(zeros_set, 1)
            nc.gpsimd.memset(Hpad, 0.0).then_inc(zeros_set, 1)
            nc.gpsimd.memset(Upad[:, G * J:], 0.0).then_inc(zeros_set, 1)
            nc.gpsimd.memset(Toep[:, :, :], 0.0).then_inc(zeros_set, 1)
            for k in range(KT):
                pool.wait_ge(sq_done, k + 1)
                if k:
                    pool.wait_ge(sq_added, k)
                    tt(sqsum[:, :], sqsum[:, :], sq[:, k % 2, :], ALU.add).then_inc(sq_added, 1)
                else:
                    nc.gpsimd.tensor_copy(sqsum[:, :], sq[:, 0, :]).then_inc(sq_added, 1)
            pool.wait_ge(zeros_set, 4)
            pool.wait_ge(ssm_ready, 1)
            pool.wait_ge(*proj.taken(0, "BT1"))
            pool.wait_ge(*work.taken(0, "CT3"))

            def prepare(l, before):
                one = bass.ds(l, 1)

                def flat(ap):
                    return ap.rearrange("p o i x -> p (o i) x")

                for r in range(2):
                    cr = [coef[:, one, q, :].rearrange("p o i -> p (o i)").unsqueeze(2).to_broadcast([P, NI, GC])
                          for q in (0, 1)]
                    b = [flat(Bsb[:, one, q]) for q in ((0, 1) if r == 0 else (1, 0))]
                    t = [pt[:, q, 0:NI * GC].rearrange("p (i c) -> p i c", i=NI) for q in range(2)]
                    step.add(tt(t[0], b[0], cr[0], ALU.mult))
                    own(tt(t[1], b[1], cr[1], ALU.mult))
                    own(tt(Bbar[:, r], t[0], t[1], ALU.add if r else ALU.subtract))

                def turned(n):
                    r, i0 = n % 2, 4 * (n // 2)
                    shape = [P, 4, T, GC]
                    t = [pt[:, q, 0:4 * T * GC].rearrange("p (i s c) -> p i s c", i=4, s=T) for q in range(2)]
                    for q in range(2):
                        A = Apow[:, one, q, i0:i0 + 4, T - 1::-1].rearrange("p o i s -> p (o i) s").unsqueeze(3)\
                            .to_broadcast(shape)
                        B = Bbar[:, q if r == 0 else 1 - q, i0:i0 + 4, :].unsqueeze(2).to_broadcast(shape)
                        step.add(tt(t[q], A, B, ALU.mult))
                    step.wait()
                    tt(WB[:, n // 2, r].rearrange("p i (s c) -> p i s c", s=T), t[0], t[1],
                       ALU.add if r else ALU.subtract).then_inc(wb_ready, 1)
                    pool.wait_ge(wb_ready, l * 8 + n + 1)

                def all_turned():
                    for n in range(8):
                        turned(n)

                if before is None:
                    pool.wait_ge(*work.taken(0, f"xT{KT - 1}"))
                    all_turned()
                else:
                    pool.wait_ge(*work.ready(before, "y3"))
                for h in range(2):
                    rows = slice(h * NST, (h + 1) * NST)
                    own(nc.gpsimd.tensor_copy(Bblk[rows, :, :, h, :], Bbar[rows]))
                for i0 in range(0, NI, 2):
                    shape = [P, 2, T + 1, GC]
                    t = [pt[:, q, 0:2 * (T + 1) * GC].rearrange("p (i s c) -> p i s c", i=2, s=T + 1)
                         for q in range(2)]
                    for r in range(2):
                        for q in range(2):
                            A = Apow[:, one, q, i0:i0 + 2, :].rearrange("p o i s -> p (o i) s").unsqueeze(3)\
                                .to_broadcast(shape)
                            C = Csb[:, one, q if r == 0 else 1 - q, i0:i0 + 2, :].rearrange("p o i c -> p (o i) c")\
                                .unsqueeze(2).to_broadcast(shape)
                            step.add(tt(t[q], A, C, ALU.mult))
                        step.wait()
                        ins = tt(Gm[:, r, i0:i0 + 2], t[0], t[1], ALU.subtract if r else ALU.add)
                        if (i0, r) == (NI - 2, 1):
                            ins.then_inc(g_ready, 1)
                            pool.wait_ge(g_ready, l + 1)
                        else:
                            own(ins)
                if before is not None:
                    pool.wait_ge(*work.ready(before, "pvs"))
                    all_turned()

            prepare(0, None)
            with pool.Fori(0, DEPTH - 1) as before:
                step.restart()
                prepare(before + 1, before)
            for k in range(KT):
                pool.wait_ge(x_ready, (DEPTH - 1) * KT + k + 1)
                tt(xn[:, k, :], xT[:, k, :], fing[:, k:k + 1].to_broadcast([P, TOK]), ALU.mult).then_inc(yn_ready, 1)


NAMES = ["x_prompt", "x_sample", "cache_k", "cache_v", "state_ssm_re", "state_ssm_im", "c_prompt", "c_sample",
         "norm_g", "w_ada", "b_ada", "w_in", "attn_sinks", "ssm_a_re", "ssm_a_im", "ssm_log_dt",
         "ssm_b_re", "ssm_b_im", "ssm_c_re", "ssm_c_im", "ssm_d", "w_glu", "b_glu", "w_out", "final_g"]
OUTS = [(1, SEQ, D), (NB, T, D), (DEPTH, 1, WIN, KV, HD), (DEPTH, 1, WIN, KV, HD), (DEPTH, 1, G, NST),
        (DEPTH, 1, G, NST), (DEPTH, NB, WIN, KV, HD), (DEPTH, NB, WIN, KV, HD), (DEPTH, NB, G, NST),
        (DEPTH, NB, G, NST)]


def kernel(**inputs):
    import concourse.bacc as bacc
    from concourse.bass_utils import run_bass_kernel_spmd

    nc = bacc.Bacc("TRN2", target_bir_lowering=False, num_devices=1, dynamic_dma_scratch_size=1024)
    arrays = {f"in_{n}": np.ascontiguousarray(inputs[n]) for n in NAMES}
    arrays["in_constants"] = constants()
    a = {n[3:]: nc.dram_tensor(n, x.shape, mybir.dt.from_np(x.dtype), kind="ExternalInput").ap()
         for n, x in arrays.items()}
    out = [nc.dram_tensor(f"out_{i}", s, F32, kind="ExternalOutput").ap() for i, s in enumerate(OUTS)]
    build(nc, a, out)
    r = run_bass_kernel_spmd(nc, [arrays], core_ids=[0])
    return tuple(r.results[0][f"out_{i}"] for i in range(len(OUTS)))
```
